# Optimizing a Trainium2 kernel written in Bass

```python
import math
import jax
import jax.numpy as jnp
from jax import lax
import numpy as np

D_MODEL = 1024
BATCH = 1
SEQ = 1024
DEPTH = 1
DEC_BATCH = 8
DEC_SEQ = 4
PAST_LEN = 256
PAGE_SIZE = 128

HEAD_DIM = 64
W_FOX = D_MODEL // 4
W_NSA = D_MODEL // 4
W_HG = D_MODEL // 2
H_FOX = W_FOX // HEAD_DIM
H_NSA = W_NSA // HEAD_DIM
DK_HG = 128
DV_HG = 128
H_HG = W_HG // DV_HG
N_NSA_BRANCH_KV = 6
P_IN = 3 * W_FOX + H_FOX + W_NSA + N_NSA_BRANCH_KV * HEAD_DIM + 3 * H_NSA + 2 * H_HG * DK_HG + 2 * W_HG
Q_BLOCK = 128
FOX_FGATE_BIAS = 4.0
CMP_LEN = 32
CMP_STRIDE = 16
CMP_HIDDEN = 128
SLC_LEN = 64
SLC_TOPN = 16
N_LOCAL_FORCED = 2
WINDOW = 512
N_BUCKETS = 32
MAX_DIST = 128
HG_CHUNK = 64
N_EXPERTS = 16
N_GROUPS = 4
E_PER_GROUP = N_EXPERTS // N_GROUPS
TOPK = 2
D_EXPERT = 256
ALPHA = (2 * DEPTH) ** 0.25
BETA = (8 * DEPTH) ** -0.25
EPS = 1e-5
NEG = -1e30
BIG = 1e30
TINY = 1e-30
F32 = jnp.float32

kernel_name = 'hybrid_fox_nsa_hgrn2_grouped_moe_step'

def layer_norm(x, g, b):
    xf = x.astype(F32)
    mu = jnp.mean(xf, axis=-1, keepdims=True)
    var = jnp.mean(jnp.square(xf - mu), axis=-1, keepdims=True)
    return ((xf - mu) * lax.rsqrt(var + EPS) * g.astype(F32) + b.astype(F32)).astype(x.dtype)

def rms_norm(x, g):
    xf = x.astype(F32)
    return xf * lax.rsqrt(jnp.mean(xf * xf, axis=-1, keepdims=True) + EPS) * g.astype(F32)

def masked_softmax(s, valid):
    s = jnp.where(valid, s, NEG)
    m = jnp.max(s, axis=-1, keepdims=True)
    e = jnp.where(valid, jnp.exp(s - m), 0.0)
    return e / jnp.maximum(jnp.sum(e, axis=-1, keepdims=True), TINY)

def t5_bucket(dist):
    n = jnp.maximum(dist, 0)
    max_exact = N_BUCKETS // 2
    nf = jnp.maximum(n, 1).astype(F32)
    large = max_exact + (jnp.log(nf / max_exact) / math.log(MAX_DIST / max_exact) * (N_BUCKETS - max_exact)).astype(jnp.int32)
    return jnp.where(n < max_exact, n, jnp.minimum(large, N_BUCKETS - 1))

def rel_bias(table, dist):
    return table[t5_bucket(dist)].astype(F32)

def gather_pages(pool, page_table):
    g = pool[page_table]
    return g.reshape((g.shape[0], g.shape[1] * g.shape[2]) + g.shape[3:])

def fox_attend(q, qc, qpos, k, v, kc, kpos):
    scale = q.shape[-1] ** -0.5
    s = jnp.einsum('bqhd,bkhd->bhqk', q, k, preferred_element_type=F32) * scale
    s = s + jnp.transpose(qc, (0, 2, 1))[..., None] - jnp.transpose(kc, (0, 2, 1))[:, :, None, :]
    s = jnp.where((kpos[None, :] <= qpos[:, None])[None, None], s, -jnp.inf)
    p = jax.nn.softmax(s, axis=-1)
    return jnp.einsum('bhqk,bkhd->bqhd', p.astype(v.dtype), v)

def fox_prompt(q, k, v, logf):
    B, T, H, D = q.shape
    c = jnp.cumsum(logf.astype(F32), axis=1)
    kpos = jnp.arange(T)

    def block(i):
        t0 = i * Q_BLOCK
        qb = lax.dynamic_slice_in_dim(q, t0, Q_BLOCK, axis=1)
        cb = lax.dynamic_slice_in_dim(c, t0, Q_BLOCK, axis=1)
        return fox_attend(qb, cb, t0 + jnp.arange(Q_BLOCK), k, v, c, kpos)

    o = lax.map(block, jnp.arange(T // Q_BLOCK))
    return jnp.transpose(o, (1, 0, 2, 3, 4)).reshape(B, T, H, D)

def nsa_compress(rows, w1, w2, pe):
    L = rows.shape[1]
    n_cmp = (L - CMP_LEN) // CMP_STRIDE + 1
    idx = jnp.arange(n_cmp)[:, None] * CMP_STRIDE + jnp.arange(CMP_LEN)[None, :]
    blocks = rows[:, idx] + pe
    h = jax.nn.gelu(jnp.einsum('bnld,ldh->bnh', blocks, w1))
    return jnp.einsum('bnh,hd->bnd', h, w2)

def nsa_cmp_slc(q, qpos, kcmp, vcmp, ks, vs, table):
    B, Tq, H, D = q.shape
    scale = D ** -0.5
    n_cmp = kcmp.shape[1]
    cstart = jnp.arange(n_cmp) * CMP_STRIDE
    dist_c = qpos[:, None] - (cstart + CMP_LEN - 1)[None, :]
    s = jnp.einsum('bqhd,bnd->bhqn', q, kcmp, preferred_element_type=F32) * scale
    s = s + jnp.transpose(rel_bias(table, dist_c), (2, 0, 1))[None]
    p_cmp = masked_softmax(s, (dist_c >= 0)[None, None])
    o_cmp = jnp.einsum('bhqn,bnd->bqhd', p_cmp.astype(vcmp.dtype), vcmp)
    L = ks.shape[1]
    pad = (-L) % SLC_LEN
    ks = jnp.pad(ks, ((0, 0), (0, pad), (0, 0)))
    vs = jnp.pad(vs, ((0, 0), (0, pad), (0, 0)))
    n_slc = (L + pad) // SLC_LEN
    sstart = jnp.arange(n_slc) * SLC_LEN
    cover = ((cstart[:, None] < sstart[None, :] + SLC_LEN) & (cstart[:, None] + CMP_LEN > sstart[None, :])).astype(F32)
    imp = jnp.einsum('bhqn,ns->bqs', p_cmp, cover)
    blk = jnp.arange(n_slc)
    qblk = qpos // SLC_LEN
    vblk = sstart[None, :] <= qpos[:, None]
    rel_blk = qblk[:, None] - blk[None, :]
    forced = (blk[None, :] == 0) | ((rel_blk >= 0) & (rel_blk < N_LOCAL_FORCED))
    score = jnp.where(vblk & forced, BIG, jnp.where(vblk, imp, NEG))
    k_top = min(SLC_TOPN, n_slc)
    top_val, top_idx = lax.top_k(score, k_top)
    sel_ok = top_val > 0.5 * NEG
    kb = ks.reshape(B, n_slc, SLC_LEN, D)
    vb = vs.reshape(B, n_slc, SLC_LEN, D)
    kg = jax.vmap(lambda a, i: a[i])(kb, top_idx).reshape(B, Tq, k_top * SLC_LEN, D)
    vg = jax.vmap(lambda a, i: a[i])(vb, top_idx).reshape(B, Tq, k_top * SLC_LEN, D)
    kpos = (top_idx[..., None] * SLC_LEN + jnp.arange(SLC_LEN)).reshape(B, Tq, k_top * SLC_LEN)
    dist_s = qpos[None, :, None] - kpos
    valid = jnp.repeat(sel_ok, SLC_LEN, axis=-1) & (dist_s >= 0)
    s = jnp.einsum('bqhd,bqkd->bhqk', q, kg, preferred_element_type=F32) * scale
    s = s + jnp.transpose(rel_bias(table, dist_s), (0, 3, 1, 2))
    p = masked_softmax(s, valid[:, None])
    o_slc = jnp.einsum('bhqk,bqkd->bqhd', p.astype(vg.dtype), vg)
    return o_cmp, o_slc

def nsa_window(q, qpos, k, v, kpos, table):
    scale = q.shape[-1] ** -0.5
    d = qpos[:, None] - kpos[None, :]
    valid = (d >= 0) & (d < WINDOW) & (kpos[None, :] >= 0)
    s = jnp.einsum('bqhd,bkd->bhqk', q, k, preferred_element_type=F32) * scale
    s = s + jnp.transpose(rel_bias(table, d), (2, 0, 1))[None]
    p = masked_softmax(s, valid[None, None])
    return jnp.einsum('bhqk,bkd->bqhd', p.astype(v.dtype), v)

def nsa_prompt(q, nkv, lw):
    B, T, H, D = q.shape
    kc = nsa_compress(nkv[:, :, 0], lw['cw1'][0], lw['cw2'][0], lw['cpe'][0])
    vc = nsa_compress(nkv[:, :, 1], lw['cw1'][1], lw['cw2'][1], lw['cpe'][1])
    ks, vs = nkv[:, :, 2], nkv[:, :, 3]
    kw = jnp.pad(nkv[:, :, 4], ((0, 0), (WINDOW, 0), (0, 0)))
    vw = jnp.pad(nkv[:, :, 5], ((0, 0), (WINDOW, 0), (0, 0)))
    table = lw['table']

    def block(i):
        t0 = i * Q_BLOCK
        qb = lax.dynamic_slice_in_dim(q, t0, Q_BLOCK, axis=1)
        qpos = t0 + jnp.arange(Q_BLOCK)
        o_c, o_s = nsa_cmp_slc(qb, qpos, kc, vc, ks, vs, table)
        kwb = lax.dynamic_slice_in_dim(kw, t0, WINDOW + Q_BLOCK, axis=1)
        vwb = lax.dynamic_slice_in_dim(vw, t0, WINDOW + Q_BLOCK, axis=1)
        o_w = nsa_window(qb, qpos, kwb, vwb, t0 - WINDOW + jnp.arange(WINDOW + Q_BLOCK), table)
        return jnp.stack([o_c, o_s, o_w], axis=3)

    o = lax.map(block, jnp.arange(T // Q_BLOCK))
    return jnp.transpose(o, (1, 0, 2, 3, 4, 5)).reshape(B, T, H, 3, D)

def nsa_gate_combine(o3, gates):
    return jnp.einsum('bthg,bthgd->bthd', gates.astype(o3.dtype), o3)

def hgrn2_chunked(q, k, v, g, S0):
    B, T, H, DK = q.shape
    DV = v.shape[-1]
    C = math.gcd(T, HG_CHUNK)
    n = T // C

    def to_chunks(a):
        return jnp.transpose(a.astype(F32).reshape(B, n, C, H, a.shape[-1]), (1, 0, 3, 2, 4))

    tri = jnp.tril(jnp.ones((C, C), dtype=bool))

    def step(S, xs):
        qq, kk, vv, gg = xs
        b = jnp.cumsum(gg, axis=2)
        diff = b[:, :, :, None, :] - b[:, :, None, :, :]
        dec = jnp.exp(jnp.where(tri[:, :, None], diff, -jnp.inf))
        A = jnp.einsum('bhtd,bhsd,bhtsd->bhts', qq, kk, dec)
        o = jnp.einsum('bhts,bhsv->bhtv', A, vv) + jnp.einsum('bhtd,bhdv->bhtv', qq * jnp.exp(b), S)
        bl = b[:, :, -1:, :]
        S_new = jnp.exp(bl[:, :, 0, :])[..., None] * S + jnp.einsum('bhsd,bhsv->bhdv', kk * jnp.exp(bl - b), vv)
        return S_new, o

    S, o = lax.scan(step, S0.astype(F32), (to_chunks(q), to_chunks(k), to_chunks(v), to_chunks(g)))
    o = jnp.transpose(o, (1, 0, 3, 2, 4)).reshape(B, T, H, DV)
    return o, S.astype(S0.dtype)

def project(h, w_in, b_in, lb):
    B, T, _ = h.shape
    p = jnp.einsum('btd,dp->btp', h, w_in) + b_in
    sizes = (W_FOX, W_FOX, W_FOX, H_FOX, W_NSA, N_NSA_BRANCH_KV * HEAD_DIM, 3 * H_NSA,
             H_HG * DK_HG, H_HG * DK_HG, W_HG, W_HG)
    offs = []
    acc = 0
    for s_ in sizes[:-1]:
        acc += s_
        offs.append(acc)
    fq, fk, fv, ff, nq, nkv, ngt, hq, hf, hi, hgt = jnp.split(p, offs, axis=-1)
    lb = lb.astype(F32).reshape(H_HG, DK_HG)
    hf = hf.astype(F32).reshape(B, T, H_HG, DK_HG)
    return dict(
        fq=fq.reshape(B, T, H_FOX, HEAD_DIM),
        fk=fk.reshape(B, T, H_FOX, HEAD_DIM),
        fv=fv.reshape(B, T, H_FOX, HEAD_DIM),
        flogf=jax.nn.log_sigmoid(ff.astype(F32)),
        nq=nq.reshape(B, T, H_NSA, HEAD_DIM),
        nkv=nkv.reshape(B, T, N_NSA_BRANCH_KV, HEAD_DIM),
        ngate=jax.nn.sigmoid(ngt.astype(F32)).reshape(B, T, H_NSA, 3),
        hq=hq.reshape(B, T, H_HG, DK_HG),
        hlogf=jnp.logaddexp(jnp.log(lb), jnp.log1p(-lb) + jax.nn.log_sigmoid(hf)),
        hk=(1.0 - lb) * jax.nn.sigmoid(-hf),
        hv=hi.reshape(B, T, H_HG, DV_HG),
        hgate=hgt.reshape(B, T, H_HG, DV_HG),
    )

def merge(o_fox, o_nsa, o_hg, hgate, hg_norm_g, w_out, dtype):
    B, T = o_fox.shape[:2]
    o_hg = rms_norm(o_hg, hg_norm_g) * jax.nn.silu(hgate.astype(F32))
    o = jnp.concatenate([o_fox.reshape(B, T, W_FOX).astype(dtype), o_nsa.reshape(B, T, W_NSA).astype(dtype),
                         o_hg.reshape(B, T, W_HG).astype(dtype)], axis=-1)
    return jnp.einsum('btc,cd->btd', o, w_out)

def mixer_prompt(h, lw):
    B, T, _ = h.shape
    pr = project(h, lw['w_in'], lw['b_in'], lw['lb'])
    o_fox = fox_prompt(pr['fq'], pr['fk'], pr['fv'], pr['flogf'])
    o_nsa = nsa_gate_combine(nsa_prompt(pr['nq'], pr['nkv'], lw), pr['ngate'])
    S0 = jnp.zeros((B, H_HG, DK_HG, DV_HG), F32)
    o_hg, S = hgrn2_chunked(pr['hq'], pr['hk'], pr['hv'], pr['hlogf'], S0)
    y = merge(o_fox, o_nsa, o_hg, pr['hgate'], lw['hg_norm_g'], lw['w_out'], h.dtype)
    wlen = min(WINDOW, T)
    fkv = jnp.stack([pr['fk'], pr['fv']], axis=2)
    return y, (fkv, pr['flogf'], pr['nkv'][:, :, 0:4], pr['nkv'][:, T - wlen:, 4:6], S)

def mixer_sample(h, lw, fox_kv_l, fox_logf_l, nsa_kv_l, win_l, S_l, page_table):
    DB, T, _ = h.shape
    pr = project(h, lw['w_in'], lw['b_in'], lw['lb'])
    past = page_table.shape[1] * fox_kv_l.shape[1]
    qpos = past + jnp.arange(T)
    fkv_new = jnp.stack([pr['fk'], pr['fv']], axis=2)
    fkv = jnp.concatenate([gather_pages(fox_kv_l, page_table).astype(fkv_new.dtype), fkv_new], axis=1)
    c = jnp.cumsum(jnp.concatenate([gather_pages(fox_logf_l, page_table).astype(F32), pr['flogf']], axis=1), axis=1)
    o_fox = fox_attend(pr['fq'], c[:, past:], qpos, fkv[:, :, 0], fkv[:, :, 1], c, jnp.arange(past + T))
    nsa_new = pr['nkv'][:, :, 0:4]
    rows = jnp.concatenate([gather_pages(nsa_kv_l, page_table).astype(nsa_new.dtype), nsa_new], axis=1)
    kc = nsa_compress(rows[:, :, 0], lw['cw1'][0], lw['cw2'][0], lw['cpe'][0])
    vc = nsa_compress(rows[:, :, 1], lw['cw1'][1], lw['cw2'][1], lw['cpe'][1])
    o_c, o_s = nsa_cmp_slc(pr['nq'], qpos, kc, vc, rows[:, :, 2], rows[:, :, 3], lw['table'])
    wbuf = win_l.shape[1]
    wrows = jnp.concatenate([win_l.astype(nsa_new.dtype), pr['nkv'][:, :, 4:6]], axis=1)
    o_w = nsa_window(pr['nq'], qpos, wrows[:, :, 0], wrows[:, :, 1], past - wbuf + jnp.arange(wbuf + T), lw['table'])
    o_nsa = nsa_gate_combine(jnp.stack([o_c, o_s, o_w], axis=3), pr['ngate'])
    o_hg, S = hgrn2_chunked(pr['hq'], pr['hk'], pr['hv'], pr['hlogf'], S_l)
    y = merge(o_fox, o_nsa, o_hg, pr['hgate'], lw['hg_norm_g'], lw['w_out'], h.dtype)
    return y, (fkv_new, pr['flogf'], nsa_new, wrows[:, T:], S)

def route(x, router_w, router_bias):
    n = x.shape[0]
    s = jax.nn.sigmoid(jnp.einsum('nd,de->ne', x, router_w).astype(F32))
    sb = s + router_bias.astype(F32)
    gscore = jnp.sum(lax.top_k(sb.reshape(n, N_GROUPS, E_PER_GROUP), TOPK)[0], axis=-1)
    gsel = jnp.argmax(gscore, axis=-1)
    emask = jnp.repeat(jax.nn.one_hot(gsel, N_GROUPS, dtype=F32), E_PER_GROUP, axis=-1) > 0
    _, idx = lax.top_k(jnp.where(emask, sb, NEG), TOPK)
    sel = jnp.sum(jax.nn.one_hot(idx, N_EXPERTS, dtype=F32), axis=-2)
    w = s * sel
    return w / jnp.sum(w, axis=-1, keepdims=True)

def moe_block(x, router_w, router_bias, w1, w3, w2):
    B, T, D = x.shape
    xf = x.reshape(B * T, D)
    comb = route(xf, router_w, router_bias)
    hgt = jnp.einsum('nd,edf->nef', xf, w1)
    hup = jnp.einsum('nd,edf->nef', xf, w3)
    hh = jax.nn.silu(hgt) * hup * comb[..., None].astype(x.dtype)
    return jnp.einsum('nef,efd->nd', hh, w2).reshape(B, T, D)

def setup_inputs(seed: int = 0) -> dict:
    key = jax.random.key(seed)
    ks = jax.random.split(key, 32)
    nrm = jax.random.normal
    n_pages = PAST_LEN // PAGE_SIZE
    n_used = DEC_BATCH * n_pages
    n_phys = n_used + max(1, n_used // 4)
    wbuf = min(WINDOW, PAST_LEN)
    x_prompt = nrm(ks[0], (BATCH, SEQ, D_MODEL), F32)
    x_sample = nrm(ks[1], (DEC_BATCH, DEC_SEQ, D_MODEL), F32)
    cache_fox_kv = nrm(ks[2], (DEPTH, n_phys, PAGE_SIZE, 2, H_FOX, HEAD_DIM), F32)
    cache_fox_logf = jax.nn.log_sigmoid(FOX_FGATE_BIAS + nrm(ks[3], (DEPTH, n_phys, PAGE_SIZE, H_FOX), F32))
    cache_nsa_kv = nrm(ks[4], (DEPTH, n_phys, PAGE_SIZE, 4, HEAD_DIM), F32)
    state_nsa_win = nrm(ks[5], (DEPTH, DEC_BATCH, wbuf, 2, HEAD_DIM), F32)
    state_hgrn = 0.5 * nrm(ks[6], (DEPTH, DEC_BATCH, H_HG, DK_HG, DV_HG), F32)
    page_table = jax.random.permutation(ks[7], n_phys)[:n_used].reshape(DEC_BATCH, n_pages).astype(jnp.int32)
    ln_in_g = 1.0 + 0.02 * nrm(ks[8], (D_MODEL,), F32)
    ln_in_b = 0.02 * nrm(ks[9], (D_MODEL,), F32)
    w_in = nrm(ks[10], (DEPTH, D_MODEL, P_IN), F32) * D_MODEL ** -0.5
    b_in = 0.02 * nrm(ks[11], (DEPTH, P_IN), F32)
    b_in = b_in.at[:, 3 * W_FOX:3 * W_FOX + H_FOX].add(FOX_FGATE_BIAS)
    hg_lb_logits = 0.5 * nrm(ks[12], (DEPTH, H_HG * DK_HG), F32)
    hg_norm_g = 1.0 + 0.02 * nrm(ks[13], (DEPTH, DV_HG), F32)
    nsa_cmp_w1 = nrm(ks[14], (DEPTH, 2, CMP_LEN, HEAD_DIM, CMP_HIDDEN), F32) * (CMP_LEN * HEAD_DIM) ** -0.5
    nsa_cmp_w2 = nrm(ks[15], (DEPTH, 2, CMP_HIDDEN, HEAD_DIM), F32) * CMP_HIDDEN ** -0.5
    nsa_cmp_pe = 0.1 * nrm(ks[16], (DEPTH, 2, CMP_LEN, HEAD_DIM), F32)
    rel_bias_table = 0.5 * nrm(ks[17], (N_BUCKETS, H_NSA), F32)
    w_out = nrm(ks[18], (DEPTH, D_MODEL, D_MODEL), F32) * D_MODEL ** -0.5 * BETA
    ln1_g = 1.0 + 0.02 * nrm(ks[19], (DEPTH, D_MODEL), F32)
    ln1_b = 0.02 * nrm(ks[20], (DEPTH, D_MODEL), F32)
    router_w = nrm(ks[21], (D_MODEL, N_EXPERTS), F32) * D_MODEL ** -0.5
    router_bias = 0.01 * nrm(ks[22], (N_EXPERTS,), F32)
    exp_w1 = nrm(ks[23], (DEPTH, N_EXPERTS, D_MODEL, D_EXPERT), F32) * D_MODEL ** -0.5
    exp_w3 = nrm(ks[24], (DEPTH, N_EXPERTS, D_MODEL, D_EXPERT), F32) * D_MODEL ** -0.5
    exp_w2 = nrm(ks[25], (DEPTH, N_EXPERTS, D_EXPERT, D_MODEL), F32) * D_EXPERT ** -0.5 * BETA
    ln2_g = 1.0 + 0.02 * nrm(ks[26], (DEPTH, D_MODEL), F32)
    ln2_b = 0.02 * nrm(ks[27], (DEPTH, D_MODEL), F32)
    return {'x_prompt': x_prompt, 'x_sample': x_sample, 'cache_fox_kv': cache_fox_kv, 'cache_fox_logf': cache_fox_logf,
            'cache_nsa_kv': cache_nsa_kv, 'state_nsa_win': state_nsa_win, 'state_hgrn': state_hgrn, 'page_table': page_table,
            'ln_in_g': ln_in_g, 'ln_in_b': ln_in_b, 'w_in': w_in, 'b_in': b_in, 'hg_lb_logits': hg_lb_logits,
            'hg_norm_g': hg_norm_g, 'nsa_cmp_w1': nsa_cmp_w1, 'nsa_cmp_w2': nsa_cmp_w2, 'nsa_cmp_pe': nsa_cmp_pe,
            'rel_bias_table': rel_bias_table, 'w_out': w_out, 'ln1_g': ln1_g, 'ln1_b': ln1_b, 'router_w': router_w,
            'router_bias': router_bias, 'exp_w1': exp_w1, 'exp_w3': exp_w3, 'exp_w2': exp_w2, 'ln2_g': ln2_g, 'ln2_b': ln2_b}

def reference(x_prompt, x_sample, cache_fox_kv, cache_fox_logf, cache_nsa_kv, state_nsa_win, state_hgrn, page_table,
              ln_in_g, ln_in_b, w_in, b_in, hg_lb_logits, hg_norm_g, nsa_cmp_w1, nsa_cmp_w2, nsa_cmp_pe, rel_bias_table,
              w_out, ln1_g, ln1_b, router_w, router_bias, exp_w1, exp_w3, exp_w2, ln2_g, ln2_b):
    lb_cum = jnp.cumsum(jax.nn.softmax(hg_lb_logits.astype(F32), axis=0), axis=0)
    lower_bounds = lb_cum - lb_cum[:1]
    xp = layer_norm(x_prompt, ln_in_g, ln_in_b)
    xs = layer_norm(x_sample, ln_in_g, ln_in_b)
    p_fkv, p_flogf, p_nkv, p_win, p_hg = [], [], [], [], []
    s_fkv, s_flogf, s_nkv, s_win, s_hg = [], [], [], [], []
    for l in range(DEPTH):
        lw = dict(w_in=w_in[l], b_in=b_in[l], lb=lower_bounds[l], hg_norm_g=hg_norm_g[l], cw1=nsa_cmp_w1[l],
                  cw2=nsa_cmp_w2[l], cpe=nsa_cmp_pe[l], table=rel_bias_table, w_out=w_out[l])
        mp, st = mixer_prompt(xp, lw)
        xp = layer_norm(ALPHA * xp + mp, ln1_g[l], ln1_b[l])
        xp = layer_norm(ALPHA * xp + moe_block(xp, router_w, router_bias, exp_w1[l], exp_w3[l], exp_w2[l]), ln2_g[l], ln2_b[l])
        p_fkv.append(st[0]); p_flogf.append(st[1]); p_nkv.append(st[2]); p_win.append(st[3]); p_hg.append(st[4])
        ms, st = mixer_sample(xs, lw, cache_fox_kv[l], cache_fox_logf[l], cache_nsa_kv[l], state_nsa_win[l],
                              state_hgrn[l], page_table)
        xs = layer_norm(ALPHA * xs + ms, ln1_g[l], ln1_b[l])
        xs = layer_norm(ALPHA * xs + moe_block(xs, router_w, router_bias, exp_w1[l], exp_w3[l], exp_w2[l]), ln2_g[l], ln2_b[l])
        s_fkv.append(st[0]); s_flogf.append(st[1]); s_nkv.append(st[2]); s_win.append(st[3]); s_hg.append(st[4])
    return (xp, xs,
            jnp.stack(p_fkv), jnp.stack(p_flogf), jnp.stack(p_nkv), jnp.stack(p_win), jnp.stack(p_hg),
            jnp.stack(s_fkv), jnp.stack(s_flogf), jnp.stack(s_nkv), jnp.stack(s_win), jnp.stack(s_hg))


_drawn_inputs = setup_inputs


def setup_inputs(seed=0):
    import zlib

    import numpy as np

    out = dict(_drawn_inputs(seed))
    spreads = {}
    factors = {'cache_fox_logf': 8.0,
     'hg_norm_g': 3.569,
     'nsa_cmp_pe': 3.501,
     'ln2_g': 7.73,
     'ln2_b': 8.669,
     'rel_bias_table': 2.982}
    for name, (base, spread) in spreads.items():
        noise = np.random.default_rng([zlib.crc32(name.encode()), seed]).standard_normal(out[name].shape)
        drawn = base * np.exp(spread * noise) if base else spread * noise
        out[name] = jnp.asarray(drawn.astype(out[name].dtype))
    for name, factor in factors.items():
        out[name] = (out[name] * factor).astype(out[name].dtype)
    return out
```

```python
import math
from contextlib import ExitStack

import numpy as np
import concourse.bass as bass
from concourse import mybir

F32 = mybir.dt.float32
I32 = mybir.dt.int32
ALU = mybir.AluOpType
ACT = mybir.ActivationFunctionType
AXX = mybir.AxisListType.X

P = 128
D = 1024
NC = D // P
SEQ = 1024
DB, DS = 8, 4
NS = DB * DS
NTOK = SEQ + NS
NT = 9
PAST, PAGE = 256, 128
NP = PAST // PAGE
H, HD = 4, 64
WIN, NCMP, NCMPS = 512, 63, 15
NE, FE = 16, 256
ALPHA = 2 ** 0.25
EPS = 1e-5
MASKED = -1e30
FLOOR = -1e29
TINY = 1e-30
LEVELS = (64, 32, 16, 8, 4, 2, 1)
CHUNKS = ((0, 512), (512, 512), (1024, 32))
FQ, FK, FV, FF, NQ, NKV, NG, HQ, HF, HI, HG = 0, 256, 512, 768, 772, 1028, 1412, 1424, 1936, 2448, 2960
P_IN = 3472
SLCW, WINW = 1151, 767
STRIPW = SLCW + WINW
SK = PAST + NS
SKC = SK + NCMPS


def rows(t):
    return P if t < 8 else NS


def bucket(n):
    return n if n < 16 else min(31, 16 + int(np.float32(math.log(n / 16)) / math.log(8) * 16 + 1e-6))


CONST = {}


def shape_constants():
    parts, at = [], 0

    def put(name, a):
        nonlocal at
        full = np.zeros((P, a.shape[1]), np.float32)
        full[:a.shape[0]] = a
        CONST[name] = (at, a.shape[1])
        parts.append(full)
        at += a.shape[1]

    i = np.arange(P)
    put("ident", np.eye(P))
    put("ones", np.ones((P, P)))
    put("negtri", -(i[:, None] <= i[None, :]).astype(np.float32))
    put("negones", -np.ones((P, P)))
    put("diagmask", np.where(i[None, :] > i[:, None], MASKED, 0))
    r_b, r_h, r_q = i // 16, i // 4 % 4, i % 4
    j = np.arange(NS)
    q_of, bk = i // 32, i % 32
    oh = np.zeros((P, SKC))
    for c in range(SKC):
        for q in range(DS):
            if c < PAST:
                d = PAST + q - c
            elif c < SK:
                d = q - (c - PAST) % DS
            else:
                d = PAST + q - 16 * (c - SK) - 31
            if d >= 0:
                oh[32 * q + bucket(d), c] = 1
    put("s_onehot", oh)
    put("s_expand", (q_of[:, None] == r_q[None, :]))
    m = np.zeros((P, SKC))
    m[:, PAST:SK] = np.where((r_b[:, None] == (j // DS)[None, :]) & (r_q[:, None] >= (j % DS)[None, :]), 0, MASKED)
    put("s_mask", m)
    put("s_negtri", -((j[:, None] // DS == j[None, :] // DS) & (j[:, None] <= j[None, :])).astype(np.float32))
    put("s_sel", (j[:, None] == (r_b * DS + r_q)[None, :]))
    put("s_head", (r_h[:, None] == np.arange(H)[None, :]))
    put("s_batch", (j[:, None] // DS == np.arange(DB)[None, :]))
    put("iota16", np.tile(np.arange(16) - 99.0, (P, 1)))
    fl = np.ascontiguousarray(np.concatenate(parts, 1), np.float32)
    lv = np.zeros((P, 8, P), np.int32)
    for n, m_ in enumerate(LEVELS):
        s, t = i[:, None], i[None, :]
        lv[:, n] = (s // (2 * m_) == t // (2 * m_)) & (s % (2 * m_) < m_) & (t % (2 * m_) >= m_)
    lv[:, 7] = np.eye(P)
    oh = np.zeros((33, STRIPW), np.float32)
    for w in range(SLCW):
        d = 1023 - w
        oh[bucket(d) if d >= 0 else 32, w] = 1
    for w in range(WINW):
        d = 639 - w
        oh[bucket(d) if 0 <= d < WIN else 32, SLCW + w] = 1
    return fl, lv.reshape(P, 8 * P), oh, np.full((1, H), MASKED, np.float32)


shape_constants()
CW = sum(w for _, w in CONST.values())


class Events:

    def __init__(self, nc, ctx, known):
        self.nc, self.ctx, self.known = nc, ctx, known
        self.sems, self.count, self.at = {}, {}, {}

    def sem(self, name):
        if name not in self.sems:
            self.sems[name] = self.ctx.enter_context(self.nc.semaphore(name))
            self.count[name] = 0
        return self.sems[name]

    def add(self, key, n, events):
        s = self.sem(key)
        self.count[key] += n
        for x in events:
            self.at[x] = (key, self.count[key])
        return s, n


class Engine:

    def __init__(self, ev, e, name):
        self.ev, self.e, self.name, self.jobs = ev, e, name, {}

    def stage(self, name):
        self.key = f"{name}_by_{self.name}"

    def at(self, event):
        key, n = self.ev.known[event] if self.ev.known else (event if isinstance(event, str) else str(event[0]), 1)
        return self.ev.sem(key), n

    def own(self):
        return self.ev.sem(self.last), self.ev.count[self.last]

    def done(self, *events):
        self.last = self.key
        return self.ev.add(self.key, 1, events)

    def moved(self, key, event=None):
        return self.ev.add(key, 16, [event or key])

    def free(self, ring):
        n = self.jobs.get(ring, -1) + 1
        return self.at(("drained", ring, n - 4) if n >= 4 else "consts_in")

    def bank(self, ring):
        n = self.jobs[ring] = self.jobs.get(ring, -1) + 1
        return self.banks[ring][n % 4]

    def filled(self, ring, *events):
        return self.done(("filled", ring, self.jobs[ring]), *events)

    def full(self, ring):
        return self.at(("filled", ring, self.jobs.get(ring, -1) + 1))

    def job(self, ring):
        return self.bank(ring)

    def drained(self, ring, *events):
        return self.done(("drained", ring, self.jobs[ring]), *events)


def build(nc, t_in, t_out, known):
    ctx = ExitStack()
    with ctx:
        return program(nc, ctx, t_in, t_out, known)


def program(nc, ctx, I, O_, known):
    ev = Events(nc, ctx, known)
    arena = ctx.enter_context(nc.sbuf_tensor("arena", [P, 53200], F32))
    banks = {r: [ctx.enter_context(nc.psum_tensor(f"{r}{n}", [P, 512], F32))[:, :] for n in range(4)] for r in ("vec", "act")}
    x_spill = nc.dram_tensor("x_spill", (P, NT * D), F32, kind="Internal").ap()
    strip_rows = nc.dram_tensor("strip_rows", (H, P, STRIPW), F32, kind="Internal").ap()

    class Zone:

        def __init__(self, at):
            self.at = at

        def take(self, n, *shape, dt=F32):
            a = arena[:, self.at:self.at + n]
            self.at += n
            assert self.at <= 53200, self.at
            if dt is not F32:
                a = a.bitcast(dt)
            if len(shape) == 1:
                a = a.rearrange("p (a b) -> p a b", a=shape[0])
            if len(shape) == 2:
                a = a.rearrange("p (a b c) -> p a b c", a=shape[0], b=shape[1])
            return a

    def skew(base, offset, *dims):
        return bass.AP(base.tensor, base.offset + offset, [list(base.ap[0])] + [list(d) for d in dims])

    z = Zone(0)
    consts = z.take(CW)
    C = {n: consts[:, a:a + w] for n, (a, w) in CONST.items()}
    ident, ones = C["ident"], C["ones"]
    ln_g, ln_b = z.take(D), z.take(D)
    eps_col = z.take(1)
    stats, mv, rstd = z.take(NT * 12, NT), z.take(NT * 2, NT), z.take(NT)
    LF, GT, tmp9 = z.take(NT * 4, NT), z.take(NT * 12, NT), z.take(NT * 16, NT)
    QTs = z.take(H * NS, H)
    fkv8, nkvg8 = z.take(512), z.take(400)
    oTh = z.take(4 * NTOK, 4)
    body = z.at
    top = 53200 - (8 * 512 + 32 * P + 2 * P + P + 2 + 240 + 240 + 64 + 64 + 2 * P)
    z = Zone(top)
    OT = z.take(8 * 512, 8)
    w1c, w2 = z.take(32 * P, 32), z.take(2 * P, 2)
    pe_sb, pc = z.take(P), z.take(2)
    gx, gu, KC, VC = z.take(240), z.take(240), z.take(64), z.take(64)
    w2d = z.take(2 * P)

    X1 = Zone(body).take(NT * D, NT)
    tail = 53200 - 2 * 4096 - NC * NTOK
    z = Zone(tail)
    xT = z.take(NC * NTOK, NC)
    W = [z.take(4096, NC) for _ in range(2)]

    z = Zone(body)
    V, b_v, lvmask, reset, bcol = z.take(NT * 512, NT), z.take(512), z.take(1024, 8, dt=I32), z.take(NTOK), z.take(20)
    hz, hk, hb, hq, hy, hs, qe, ke = (z.take(NTOK) for _ in range(8))
    lev = [z.take(NTOK) for _ in range(2)]
    AT, ATs, Sall, KeT = z.take(SEQ, 8), z.take(NS), z.take(9 * P, 9), z.take(9 * P, 9)
    S0, VM, ebl = z.take(DB * P, DB), z.take(DB * P, DB), z.take(16)
    oraw = hz
    assert z.at <= tail, (z.at, tail)

    z = Zone(body)
    QT = z.take(H * SEQ, H)
    fkv, nkvg = z.take(8 * 512, 8), z.take(8 * 400, 8)
    bcolq, b_fkv, b_nkvg = z.take(H), z.take(512), z.take(400)
    assert z.at <= tail
    tab33, tabB = z.take(H), z.take(H * P, H)
    small = z.take(4 * 16, 4)
    KT, kcvc = z.take(4 * SEQ, 4), z.take(NTOK)
    strip_s, strip_w, negc, foxdiag = z.take(1024), z.take(640), z.take(1024), z.take(SEQ, 8)
    zs = Zone(z.at)
    S = [z.take(1024) for _ in range(4)]
    PT = [z.take(1024, 8) for _ in range(2)]
    assert z.at <= top, (z.at, top)
    onehot, strip_tmp = zs.take(STRIPW), zs.take(STRIPW)

    z = Zone(body)
    oTa = z.take(4 * NTOK, 4)
    Fc, Nc, Wc = z.take(DB * NP * 512, DB, NP), z.take(DB * NP * 256, DB, NP), z.take(DB * NP * P, DB, NP)
    LFc, LFr, LFn = z.take(DB * NP * H, DB, NP), z.take(NP * P, NP), z.take(P)
    FKT, KVT, T1 = z.take(2 * DB * PAST, 2, DB), z.take(DB * PAST, DB), z.take(DB * PAST, DB)
    KTn = z.take(4 * NS, 4)
    QS, QSall, QN, QNall = z.take(2 * DB * P, 2, DB), z.take(2 * P, 2), z.take(DB * P, DB), z.take(P)
    tabX, TX, s_bias, f_bias = z.take(H), z.take(P), z.take(SKC), z.take(SK)
    zl = Zone(CW)
    Ss = [zl.take(SK) for _ in range(4)]
    PTs = [z.take(3 * P, 3) for _ in range(4)]
    KCs, VCs = z.take(120), z.take(DB * 64, DB)
    sg, sm, ss, gsel = z.take(12), z.take(8), z.take(8), z.take(4)
    pt_sb = z.take(16, dt=I32)
    assert z.at <= top, (z.at, top)

    z = Zone(body + 4 * NTOK)
    X, x1T = z.take(NT * D, NT), z.take(NC * NTOK, NC)
    Wo = Zone(z.at).take(NC * D, NC)
    Wg, Wu, Wd = [], [], []
    for _ in range(2):
        Wg.append(z.take(NC * FE, NC)), Wu.append(z.take(NC * FE, NC)), Wd.append(z.take(2 * D, 2))
    hh = [z.take(2 * NTOK, 2) for _ in range(2)]
    eb = [z.take(512) for _ in range(2)]
    zr = Zone(z.at - 1024 - 4 * NTOK)
    z2 = Zone(z.at)
    comb, ccol = z2.take(NT * NE, NT), [z2.take(NT) for _ in range(2)]
    rs, rb, rm, r1, r2 = (zr.take(NT * NE, NT) for _ in range(5))
    rbias, rg, rgm, rt1, rt2, rw = zr.take(NE), zr.take(NT * 4, NT), zr.take(NT * 4, NT), zr.take(NT), zr.take(NT), zr.take(NC * NE, NC)

    w_blocks = [[(0, HI, 512)]]
    for h in range(H):
        w_blocks.append([(0, HQ + h * P, P), (P, HF + h * P, P), (2 * P, HG + h * P, P)])
    w_blocks.append([x for h in range(H) for x in ((h * P, FQ + h * HD, HD), (h * P + HD, NQ + h * HD, HD))])
    w_blocks.append([(0, FK, 512)])
    w_blocks.append([(0, NKV, 396), (396, FF, 4)])
    w_view = I["w_in"][0].rearrange("(c p) n -> p c n", p=P)

    UNITS = [(h, kind, i) for h in range(H) for i in range(8) for kind in ("fox", "slc", "win", "cmp")]

    def unit_keys(kind, i):
        if kind == "cmp":
            return 0, min(8 * i + 7, NCMP), 1
        first = max(0, i - 4) if kind == "win" else 0
        return first * P, (i + 1 - first) * P, i + 1 - first

    def transpose_rings(u, nb):
        return [("act", "vec")[(u + j) % 2] for j in range((nb + 3) // 4)]

    GU_JOBS = [(f, n) for f in range(2) for n in range(3)]
    gate_bank, up_bank, y_bank = banks["vec"][0:2], banks["vec"][2:4], banks["act"]
    msem = {n: ctx.enter_context(nc.semaphore(f"moe_{n}")) for n in
            ("w0_loaded", "w1_loaded", "gu_filled", "gu_free", "exp_done", "vec_steps",
             "y_filled", "y_free")}

    block = ctx.enter_context(nc.Block())

    def bcast(src, n):
        return bass.AP(src.tensor, src.offset, [[0, P], [1, n]])

    def expert_weights(e, k, b):
        ds = bass.ds(k, 1)
        e.dma_start(Wg[b], I["exp_w1"][0, ds].rearrange("e (c p) f -> p (e c) f", p=P)).then_inc(msem[f"w{b}_loaded"], 16)
        e.dma_start(Wu[b], I["exp_w3"][0, ds].rearrange("e (c p) f -> p (e c) f", p=P)).then_inc(msem[f"w{b}_loaded"], 16)
        e.dma_start(Wd[b], I["exp_w2"][0, ds].rearrange("e (c p) f -> p (e c) f", p=P)).then_inc(msem[f"w{b}_loaded"], 16)

    @block.sync
    def _(e):
        E = Engine(ev, e, "sync")
        xp, xs = I["x_prompt"][0], I["x_sample"].rearrange("b t d -> (b t) d")
        for t in range(NT):
            e.dma_start(X1[:rows(t), t, :], xp[t * P:(t + 1) * P] if t < 8 else xs).then_inc(*E.moved(f"x{t}_in"))
        e.dma_start(ln_g, bcast(I["ln_in_g"], D)).then_inc(*E.moved("ln_in"))
        e.dma_start(ln_b, bcast(I["ln_in_b"], D)).then_inc(*E.moved("ln_in"))
        e.dma_start(consts, I["consts"]).then_inc(*E.moved("consts_in"))

        def load_w(k):
            if k >= 2:
                e.wait_ge(*E.at(("w_in used", k - 2)))
            for a, c, n in w_blocks[k]:
                e.dma_start(W[k % 2][:, :, a:a + n], w_view[:, :, c:c + n]).then_inc(*E.moved(f"w{k % 2}_in", ("w_in", k)))

        load_w(0)
        load_w(1)
        e.wait_ge(*E.at("x transposed pe"))
        e.wait_ge(*E.at("x_spill"))
        e.dma_start(b_v, bcast(I["b_in"][0, HI:HI + 512], 512)).then_inc(*E.moved("hgrn_in"))
        e.dma_start(lvmask, I["level_masks"].rearrange("p (a b) -> p a b", a=8)).then_inc(*E.moved("hgrn_in"))
        b = I["b_in"][0]
        e.dma_start(bcol[:, 0:8], b[HQ:HQ + 1024].rearrange("(h p) -> p h", p=P), allow_slow_non_contiguous=True).then_inc(*E.moved("hgrn_in"))
        e.dma_start(bcol[:, 8:12], b[HG:HG + 512].rearrange("(h p) -> p h", p=P), allow_slow_non_contiguous=True).then_inc(*E.moved("hgrn_in"))
        e.dma_start(bcol[:, 12:13], I["hg_norm_g"][0].rearrange("(p a) -> p a", a=1), allow_slow_non_contiguous=True).then_inc(*E.moved("hgrn_in"))
        for h in range(H):
            if h:
                e.wait_ge(*E.at(("hgrn done", h - 1)))
            e.dma_start(S0, I["state_hgrn"][0, :, h].rearrange("b d v -> d b v")).then_inc(*E.moved("s0_in", ("s0", h)))
            load_w(2 + h)
        load_w(6)
        e.wait_ge(*E.at(("hgrn done", H - 1)))
        e.dma_start(bcolq[0:64, :], b[FQ:FQ + 256].rearrange("(h p) -> p h", p=HD), allow_slow_non_contiguous=True).then_inc(*E.moved("attn_in"))
        e.dma_start(bcolq[64:128, :], b[NQ:NQ + 256].rearrange("(h p) -> p h", p=HD), allow_slow_non_contiguous=True).then_inc(*E.moved("attn_in"))
        e.dma_start(b_fkv, bcast(b[FK:FK + 512], 512)).then_inc(*E.moved("attn_in"))
        e.dma_start(b_nkvg[:, 0:396], bcast(b[NKV:NKV + 396], 396)).then_inc(*E.moved("attn_in"))
        e.dma_start(b_nkvg[:, 396:400], bcast(b[FF:FF + 4], 4)).then_inc(*E.moved("attn_in"))
        load_w(7)
        e.wait_ge(*E.at(("w_in used", 7)))
        e.dma_start(tab33[0:32, :], I["rel_bias_table"]).then_inc(*E.moved("tab_in"))
        e.dma_start(tab33[32:33, :], I["masked_row"]).then_inc(*E.moved("tab_in"))
        e.dma_start(onehot[0:33, :], I["bucket_rows"]).then_inc(*E.moved("tab_in"))
        e.dma_start(w1c[0:64], I["nsa_cmp_w1"][0, 0].rearrange("l d x -> d l x")).then_inc(*E.moved("cmp_in"))
        e.dma_start(w1c[64:128], I["nsa_cmp_w1"][0, 1].rearrange("l d x -> d l x")).then_inc(*E.moved("cmp_in"))
        e.dma_start(w2[:, :, 0:64], I["nsa_cmp_w2"][0].rearrange("k x d -> x k d")).then_inc(*E.moved("cmp_in"))
        e.dma_start(pe_sb[0:32, :].rearrange("l (k d) -> l k d", k=2), I["nsa_cmp_pe"][0].rearrange("k l d -> l k d")).then_inc(*E.moved("cmp_in"))
        for h in range(H):
            e.wait_ge(*E.at(("strip rows", h)))
            e.dma_start(strip_rows[h], strip_tmp).then_inc(*E.moved("strip_out", ("strip stored", h)))
            e.wait_ge(*E.at(("strip stored", h)))
        for h in range(H):
            if h:
                e.wait_ge(*E.at(("strips used", h - 1)))
            at = strip_rows.offset + h * P * STRIPW
            e.dma_start(strip_s, bass.AP(strip_rows.tensor, at + 127, [[STRIPW - 1, P], [1, 1024]])).then_inc(*E.moved("strip_in", ("strips", h)))
            e.dma_start(strip_w, bass.AP(strip_rows.tensor, at + SLCW + 127, [[STRIPW - 1, P], [1, 640]])).then_inc(*E.moved("strip_in", ("strips", h)))
        e.wait_ge(*E.at("prompt attention done"))
        e.wait_ge(*E.at("kv_out"))
        e.dma_start(pt_sb[0:1, :], I["page_table"].rearrange("b j -> (b j)").rearrange("(a n) -> a n", a=1)).then_inc(*E.moved("table_in"))
        e.wait_ge(*E.at("table_in"))
        for q in range(DS):
            e.dma_start(tabX[32 * q:32 * q + 32, :], I["rel_bias_table"]).then_inc(*E.moved("tabx_in"))
        kvp = I["cache_fox_kv"][0].rearrange("n p k h d -> n p (k h d)")
        nkp = I["cache_nsa_kv"][0].rearrange("n p k d -> n p (k d)")
        lfp = I["cache_fox_logf"][0]
        for n in range(DB * NP):
            page = e.value_load(pt_sb[0:1, n:n + 1], min_val=0, max_val=kvp.shape[0] - 1)
            bb, jj = n // NP, n % NP
            e.dma_start(Fc[:, bb, jj, :], kvp[bass.ds(page, 1)].rearrange("a p x -> p (a x)")).then_inc(*E.moved("cache_in"))
            e.dma_start(Nc[:, bb, jj, :], nkp[bass.ds(page, 1)].rearrange("a p x -> p (a x)")).then_inc(*E.moved("cache_in"))
            e.dma_start(LFc[:, bb, jj, :], lfp[bass.ds(page, 1)].rearrange("a p x -> p (a x)")).then_inc(*E.moved("cache_in"))
        for bb in range(DB):
            e.dma_start(Wc[:, bb], I["state_nsa_win"][0, bb].rearrange("(j p) k d -> p j (k d)", p=P)).then_inc(*E.moved("cache_in"))
        e.wait_ge(*E.at("sample attention done"))
        for t in range(NT):
            e.dma_start(X[:rows(t), t, :], x_spill[:rows(t), t * D:(t + 1) * D]).then_inc(*E.moved("xres_in"))
        e.dma_start(Wo, I["w_out"][0].rearrange("(c p) n -> p c n", p=P)).then_inc(*E.moved("wo_in"))
        e.dma_start(ln_g, bcast(I["ln1_g"][0], D)).then_inc(*E.moved("ln1_in"))
        e.dma_start(ln_b, bcast(I["ln1_b"][0], D)).then_inc(*E.moved("ln1_in"))
        e.wait_ge(*E.at("projected out"))
        e.dma_start(rw, I["router_w"].rearrange("(c p) n -> p c n", p=P)).then_inc(*E.moved("router_in"))
        e.dma_start(rbias, bcast(I["router_bias"], NE)).then_inc(*E.moved("router_in"))
        expert_weights(e, 0, 0)
        expert_weights(e, 1, 1)
        e.wait_ge(*E.at("x1 normalised"))
        e.dma_start(ln_g, bcast(I["ln2_g"][0], D)).then_inc(*E.moved("ln2_in"))
        e.dma_start(ln_b, bcast(I["ln2_b"][0], D)).then_inc(*E.moved("ln2_in"))
        with e.Fori(1, NE // 2) as i:
            for bf in range(2):
                e.wait_ge(msem["y_filled"], 36 * i + 18 * (bf - 1))
                expert_weights(e, 2 * i + bf, bf)
        yp, ys = O_["y_prompt"][0], O_["y_sample"].rearrange("b t d -> (b t) d")
        for t in range(NT):
            e.wait_ge(*E.at(("y normalised", t)))
            e.dma_start(yp[t * P:(t + 1) * P] if t < 8 else ys, X[:rows(t), t, :]).then_inc(*E.moved("y_out"))
        e.wait_ge(*E.at("y_out"))

    @block.tensor
    def _(e):
        E = Engine(ev, e, "tensor")
        E.banks = banks
        mm = e.matmul
        E.stage("p1")
        e.wait_ge(*E.at("consts_in"))
        for t in range(NT):
            e.wait_ge(*E.at(("x normal", t)))
            r = rows(t)
            for half in range(2):
                ring = "act" if half else "vec"
                e.wait_ge(*E.free(ring))
                bk = E.bank(ring)
                for c in range(4):
                    last = e.transpose(bk[:, c * P:c * P + r], X1[:r, t, (4 * half + c) * P:(4 * half + c + 1) * P], ident[:r, :r])
                last.then_inc(*E.filled(ring, "x transposed pe"))

        def channel_major(k, m, col, ring):
            for a, n in CHUNKS:
                e.wait_ge(*E.free(ring))
                bk = E.bank(ring)
                for c in range(NC):
                    last = mm(bk[:, 0:n], W[k % 2][:, c, col:col + P], xT[:, c, a:a + n], start=c == 0, stop=c == NC - 1)
                last.then_inc(*E.filled(ring, ("w_in used", k)))

        def token_major(k, width, ring):
            for t in range(NT):
                r = rows(t)
                e.wait_ge(*E.free(ring))
                bk = E.bank(ring)
                for c in range(NC):
                    last = mm(bk[:r, 0:width], xT[:, c, t * P:t * P + r], W[k % 2][:, c, 0:width], start=c == 0, stop=c == NC - 1)
                last.then_inc(*E.filled(ring, ("w_in used", k)))

        e.wait_ge(*E.at("xT by vec"))
        e.wait_ge(*E.at("xT by act"))
        e.wait_ge(*E.at(("w_in", 0)))
        token_major(0, 512, "vec")

        def hgrn_project(h):
            e.wait_ge(*E.at(("w_in", 1 + h)))
            for m in range(3):
                channel_major(1 + h, m, m * P, "act")

        hgrn_project(0)
        for h in range(H):
            E.stage("hgrn")
            for l in range(8):
                for x in [("level q", h, l), ("level k", h, l)] if l < 7 else [("k", h), ("projected", h, 0)]:
                    e.wait_ge(*E.at(x))
                for g in range(2):
                    e.wait_ge(*E.free("vec"))
                    bk = E.bank("vec")
                    for c in range(4):
                        ch = slice((4 * g + c) * P, (4 * g + c + 1) * P)
                        a, b = (hk, hq) if l == 7 else (lev[l % 2], lev[l % 2])
                        last = mm(bk[:, c * P:(c + 1) * P], a[:, ch], b[:, ch], start=True, stop=True)
                    last.then_inc(*E.filled("vec", ("level used", h, l)))
                if l >= 5:
                    e.wait_ge(*E.free("vec"))
                    bk = E.bank("vec")
                    mm(bk[:NS, 0:NS], a[:, SEQ:], b[:, SEQ:], start=True, stop=True).then_inc(*E.filled("vec", ("level used", h, l)))
            e.wait_ge(*E.at(("ke", h)))
            for g in range(2):
                e.wait_ge(*E.free("act"))
                bk = E.bank("act")
                for c in range(4):
                    last = e.transpose(bk[:, c * P:(c + 1) * P], ke[:, (4 * g + c) * P:(4 * g + c + 1) * P], ident)
                last.then_inc(*E.filled("act"))
            e.wait_ge(*E.free("act"))
            bk = E.bank("act")
            e.transpose(bk[:NS, 0:P], ke[:, SEQ:], ident).then_inc(*E.filled("act"))
            e.wait_ge(*E.at(("KeT", h)))
            e.wait_ge(*E.at("V ready"))
            hv = slice(h * P, (h + 1) * P)
            for g in range(2):
                e.wait_ge(*E.free("vec"))
                bk = E.bank("vec")
                for c in range(4):
                    last = mm(bk[:, c * P:(c + 1) * P], KeT[:, 4 * g + c, :], V[:, 4 * g + c, hv], start=True, stop=True)
                last.then_inc(*E.filled("vec"))
            e.wait_ge(*E.at(("VM", h)))
            for g in range(2):
                e.wait_ge(*E.free("vec"))
                bk = E.bank("vec")
                mm(bk, KeT[:NS, 8, :], VM[:NS, 4 * g:4 * g + 4, :], start=True, stop=True).then_inc(*E.filled("vec"))
            e.wait_ge(*E.at(("AT", h)))
            e.wait_ge(*E.at(("states", h)))
            e.wait_ge(*E.at(("qe", h)))
            e.wait_ge(*E.at(("s0", h)))
            for g in range(2):
                e.wait_ge(*E.free("act"))
                bk = E.bank("act")
                for c in range(4):
                    n = 4 * g + c
                    mm(bk[:, c * P:(c + 1) * P], V[:, n, hv], AT[:, n, :], start=True, stop=False)
                    last = mm(bk[:, c * P:(c + 1) * P], Sall[:, n, :], qe[:, n * P:(n + 1) * P], start=False, stop=True)
                last.then_inc(*E.filled("act"))
            e.wait_ge(*E.free("act"))
            bk = E.bank("act")
            mm(bk[:, 0:NS], V[:NS, 8, hv], ATs[:NS, :], start=True, stop=False)
            for b in range(DB):
                last = mm(bk[:, 4 * b:4 * b + 4], S0[:, b, :], qe[:, SEQ + 4 * b:SEQ + 4 * b + 4], start=False, stop=b == DB - 1)
            last.then_inc(*E.filled("act", ("hgrn outputs", h)))
            e.wait_ge(*E.at(("squares", h)))
            for a, n in CHUNKS:
                e.wait_ge(*E.free("act"))
                bk = E.bank("act")
                mm(bk[:, 0:n], ones, lev[0][:, a:a + n], start=True, stop=True).then_inc(*E.filled("act", ("sums", h)))
            if h < H - 1:
                hgrn_project(h + 1)
        E.stage("p2b")
        e.wait_ge(*E.at(("hgrn done", H - 1)))
        e.wait_ge(*E.at(("w_in", 5)))
        for h in range(H):
            channel_major(5, h, h * P, "act")
        e.wait_ge(*E.at(("w_in", 6)))
        token_major(6, 512, "vec")
        e.wait_ge(*E.at(("w_in", 7)))
        token_major(7, 400, "vec")

        E.stage("p3")
        e.wait_ge(*E.at("tab_in"))
        e.wait_ge(*E.at("tabB"))
        for h in range(H):
            for a in range(0, STRIPW, 512):
                n = min(512, STRIPW - a)
                e.wait_ge(*E.free("act"))
                bk = E.bank("act")
                mm(bk[:, 0:n], tabB[:33, h, :], onehot[:33, a:a + n], start=True, stop=True).then_inc(*E.filled("act"))
        e.wait_ge(*E.at("fkv ready"))
        e.wait_ge(*E.at("nkvg ready"))
        e.wait_ge(*E.at("cmp_in"))
        for t in range(8):
            e.wait_ge(*E.free("act"))
            bk = E.bank("act")
            for h in range(H):
                last = e.transpose(bk[0:64, h * P:(h + 1) * P], fkv[:, t, h * HD:(h + 1) * HD], ident)
            last.then_inc(*E.filled("act"))
            e.wait_ge(*E.free("vec"))
            bk = E.bank("vec")
            for j, a in enumerate((0, 64, 192)):
                last = e.transpose(bk[:, j * P:(j + 1) * P], nkvg[:, t, a:a + P], ident)
            last.then_inc(*E.filled("vec"))
        e.wait_ge(*E.free("vec"))
        bk = E.bank("vec")
        e.transpose(bk[:, 0:32], pe_sb[0:32, :], ident[0:32, 0:32]).then_inc(*E.filled("vec"))
        e.wait_ge(*E.at("kcvc ready"))
        for kv in range(2):
            s = slice(64 * kv, 64 * kv + 64)
            e.wait_ge(*E.free("vec"))
            bk = E.bank("vec")
            for l in range(32):
                last = mm(bk[:, 0:65], w1c[s, l, :], skew(kcvc[s, :], l, [16, 65]), start=l == 0, stop=l == 31)
            last.then_inc(*E.filled("vec"))
        e.wait_ge(*E.at("cmp hidden"))
        e.wait_ge(*E.free("vec"))
        bk = E.bank("vec")
        mm(bk[:, 0:NCMP], w2d[:, 0:P], gx[:, 0:NCMP], start=True, stop=True).then_inc(*E.filled("vec"))
        e.wait_ge(*E.free("vec"))
        bk = E.bank("vec")
        mm(bk[:NCMP, 0:64], gx[:, NCMP:2 * NCMP], w2[:, 1, 0:64], start=True, stop=True).then_inc(*E.filled("vec"))

        def decay_rows(h):
            for g in range(2):
                e.wait_ge(*E.free("vec"))
                bk = E.bank("vec")
                for c in range(4):
                    lf = LF[:, 4 * g + c, h:h + 1].to_broadcast([P, P])
                    last = mm(bk[:, c * P:(c + 1) * P], lf, C["negtri"], start=True, stop=True)
                last.then_inc(*E.filled("vec"))

        def scores(u):
            h, kind, i = UNITS[u]
            first, L, nb = unit_keys(kind, i)
            s = slice(0, 64) if kind == "fox" else slice(64, 128)
            q = QT[s, h, i * P:(i + 1) * P]
            for a in range(0, L, 512):
                n = min(512, L - a)
                k = {"fox": KT[0:64, h], "slc": KT[64:128, 0], "win": KT[64:128, 1], "cmp": KC[64:128]}[kind]
                e.wait_ge(*E.free("vec"))
                bk = E.bank("vec")
                mm(bk[:, 0:n], q, k[:, first + a:first + a + n], start=True, stop=True).then_inc(*E.filled("vec"))

        def transposes(u):
            h, kind, i = UNITS[u]
            _, L, nb = unit_keys(kind, i)
            e.wait_ge(*E.at(("probs", u)))
            for j, ring in enumerate(transpose_rings(u, nb)):
                e.wait_ge(*E.free(ring))
                bk = E.bank(ring)
                for c in range(min(4, nb - 4 * j)):
                    n = min(P, L)
                    last = e.transpose(bk[:n, c * P:(c + 1) * P], S[u % 4][:, (4 * j + c) * P:(4 * j + c) * P + n], ident)
                last.then_inc(*E.filled(ring))

        def values(u):
            h, kind, i = UNITS[u]
            first, L, nb = unit_keys(kind, i)
            for x in [("pt", u, j) for j in range((nb + 3) // 4)]:
                e.wait_ge(*E.at(x))
            e.wait_ge(*E.free("vec"))
            bk = E.bank("vec")
            for c in range(nb):
                b = first // P + c
                v = {"fox": fkv[:, b, 256 + h * HD:256 + (h + 1) * HD], "slc": nkvg[:, b, 192:256],
                     "win": nkvg[:, b, 320:384], "cmp": VC[:min(L, P)]}[kind]
                last = mm(bk[:, 0:64], PT[u % 2][:min(P, L), c, :], v, start=c == 0, stop=c == nb - 1)
            last.then_inc(*E.filled("vec", ("unit", u)))

        E.stage("attn")
        e.wait_ge(*E.at("KC ready"))
        e.wait_ge(*E.at("QT ready"))
        e.wait_ge(*E.at("KT by act"))
        e.wait_ge(*E.at("KT by vec"))
        n = len(UNITS)
        for u in range(n + 3):
            if u < n:
                if u % 32 == 0:
                    decay_rows(UNITS[u][0])
                scores(u)
            if 2 <= u < n + 2:
                transposes(u - 2)
            if u >= 3:
                values(u - 3)

        E.stage("p4")
        e.wait_ge(*E.at("prompt attention done"))
        e.wait_ge(*E.at("kv_out"))
        for t in range(8):
            e.wait_ge(*E.free("act"))
            bk = E.bank("act")
            for c in range(4):
                last = e.transpose(bk[:, c * P:(c + 1) * P], OT[:, t, c * P:(c + 1) * P], ident)
            last.then_inc(*E.filled("act"))
        e.wait_ge(*E.at("cache_in"))
        for b in range(DB):
            e.wait_ge(*E.free("act"))
            bk = E.bank("act")
            for c in range(2):
                for j in range(NP):
                    last = e.transpose(bk[:, (2 * c + j) * P:(2 * c + j + 1) * P], Fc[:, b, j, c * P:(c + 1) * P], ident)
            last.then_inc(*E.filled("act"))
            e.wait_ge(*E.free("vec"))
            bk = E.bank("vec")
            for c in range(2):
                for j in range(NP):
                    last = e.transpose(bk[:, (2 * c + j) * P:(2 * c + j + 1) * P], Nc[:, b, j, 64 * c:64 * c + P], ident)
            last.then_inc(*E.filled("vec"))
            e.wait_ge(*E.free("vec"))
            bk = E.bank("vec")
            for j in range(NP):
                last = e.transpose(bk[:, j * P:(j + 1) * P], Wc[:, b, j, :], ident)
            last.then_inc(*E.filled("vec"))
        e.wait_ge(*E.free("vec"))
        bk = E.bank("vec")
        for j, src in enumerate((fkv8[:NS, 0:P], fkv8[:NS, P:2 * P], nkvg8[:NS, 64:192], nkvg8[:NS, 256:384])):
            last = e.transpose(bk[:, j * NS:(j + 1) * NS], src, ident[:NS, :NS])
        last.then_inc(*E.filled("vec"))
        e.wait_ge(*E.at("sample operands"))
        e.wait_ge(*E.at("tabx_in"))
        e.wait_ge(*E.free("vec"))
        bk = E.bank("vec")
        mm(bk[:, 0:P], LFr[:, 0, :], C["negtri"], start=True, stop=True)
        mm(bk[:, P:2 * P], LFr[:, 0, :], C["negones"], start=True, stop=False)
        mm(bk[:, P:2 * P], LFr[:, 1, :], C["negtri"], start=False, stop=True)
        mm(bk[:, 2 * P:SK], LFr[:, 0, :], C["negones"][:, 0:NS], start=True, stop=False)
        mm(bk[:, 2 * P:SK], LFr[:, 1, :], C["negones"][:, 0:NS], start=False, stop=False)
        mm(bk[:, 2 * P:SK], LFn, C["s_negtri"], start=False, stop=True).then_inc(*E.filled("vec"))
        e.wait_ge(*E.free("vec"))
        bk = E.bank("vec")
        mm(bk[:, 0:SKC], TX, C["s_onehot"], start=True, stop=True).then_inc(*E.filled("vec"))
        e.wait_ge(*E.free("vec"))
        bk = E.bank("vec")
        mm(bk[:, 0:12], C["s_sel"][:NS, :], GT[:NS, 8, :], start=True, stop=True).then_inc(*E.filled("vec"))
        e.wait_ge(*E.at("sample keys"))
        for kv in range(2):
            s = slice(64 * kv, 64 * kv + 64)
            e.wait_ge(*E.free("vec"))
            bk = E.bank("vec")
            for l in range(32):
                last = mm(bk[:, 0:DB * NCMPS], w1c[s, l, :], skew(KVT[s, 0, :], l, [PAST, DB], [16, NCMPS]), start=l == 0, stop=l == 31)
            last.then_inc(*E.filled("vec"))
        e.wait_ge(*E.at("sample cmp hidden"))
        e.wait_ge(*E.free("vec"))
        bk = E.bank("vec")
        mm(bk[:, 0:120], w2d[:, 0:P], gx[:, 0:120], start=True, stop=True).then_inc(*E.filled("vec"))
        e.wait_ge(*E.free("vec"))
        bk = E.bank("vec")
        for b in range(DB):
            last = mm(bk[:NCMPS, b * 64:(b + 1) * 64], gx[:, 120 + 15 * b:120 + 15 * b + 15], w2[:, 1, 0:64], start=True, stop=True)
        last.then_inc(*E.filled("vec"))
        e.wait_ge(*E.at("sample keys by act"))
        e.wait_ge(*E.at("sample cmp ready"))
        e.wait_ge(*E.free("vec"))
        bk = E.bank("vec")
        for b in range(DB):
            for c in range(2):
                mm(bk[:, 0:PAST], QS[:, c, b, :], FKT[:, c, b, :], start=b + c == 0, stop=b * 2 + c == 15)
        for c in range(2):
            last = mm(bk[:, PAST:SK], QSall[:, c, :], KTn[:, c, :], start=c == 0, stop=c == 1)
        last.then_inc(*E.filled("vec"))
        for s, slot in ((slice(64, 128), 2), (slice(0, 64), 3)):
            e.wait_ge(*E.free("vec"))
            bk = E.bank("vec")
            for b in range(DB):
                mm(bk[:, 0:PAST], QN[s, b, :], T1[s, b, :], start=b == 0, stop=b == DB - 1)
            mm(bk[:, PAST:SK], QNall[s, :], KTn[s, slot, :], start=True, stop=True).then_inc(*E.filled("vec"))
        e.wait_ge(*E.free("vec"))
        bk = E.bank("vec")
        for b in range(DB):
            last = mm(bk[:, 0:NCMPS], QN[64:128, b, :], KCs[64:128, 15 * b:15 * b + 15], start=b == 0, stop=b == DB - 1)
        last.then_inc(*E.filled("vec"))
        for k in range(4):
            e.wait_ge(*E.at(("sample probs", k)))
            e.wait_ge(*E.free("vec"))
            bk = E.bank("vec")
            if k < 3:
                e.transpose(bk[:, 0:P], Ss[k][:, 0:P], ident)
                e.transpose(bk[:, P:2 * P], Ss[k][:, P:2 * P], ident)
                last = e.transpose(bk[:NS, 2 * P:3 * P], Ss[k][:, 2 * P:SK], ident)
            else:
                last = e.transpose(bk[:NCMPS, 0:P], Ss[k][:, 0:NCMPS], ident)
            last.then_inc(*E.filled("vec"))
        e.wait_ge(*E.at("sample PT"))
        e.wait_ge(*E.free("vec"))
        bk = E.bank("vec")
        for c in range(2):
            o = slice(c * P, (c + 1) * P)
            mm(bk[:, o], fkv8[:NS, 256 + c * P:256 + (c + 1) * P], PTs[0][:NS, 2, :], start=True, stop=False)
            for b in range(DB):
                for j in range(NP):
                    last = mm(bk[:, c * P + 16 * b:c * P + 16 * b + 16], Fc[:, b, j, 256 + c * P:256 + (c + 1) * P],
                              PTs[0][:, j, 16 * b:16 * b + 16], start=False, stop=b * NP + j == 15)
        last.then_inc(*E.filled("vec"))
        e.wait_ge(*E.free("vec"))
        bk = E.bank("vec")
        mm(bk[:64, 0:P], nkvg8[:NS, 192:256], PTs[1][:NS, 2, :], start=True, stop=False)
        mm(bk[:64, 0:P], nkvg8[:NS, 320:384], PTs[2][:NS, 2, :], start=False, stop=False)
        for b in range(DB):
            o = slice(16 * b, 16 * b + 16)
            for j in range(NP):
                mm(bk[:64, o], Nc[:, b, j, 192:256], PTs[1][:, j, o], start=False, stop=False)
                mm(bk[:64, o], Wc[:, b, j, 64:128], PTs[2][:, j, o], start=False, stop=False)
            last = mm(bk[:64, o], VCs[:NCMPS, b, :], PTs[3][:NCMPS, 0, o], start=False, stop=b == DB - 1)
        last.then_inc(*E.filled("vec"))

        E.stage("p5")
        e.wait_ge(*E.at("oTa by act"))
        e.wait_ge(*E.at("sample attention done"))
        e.wait_ge(*E.at(("hgrn done", H - 1)))
        e.wait_ge(*E.at("wo_in"))
        for t in range(NT):
            r = rows(t)
            for half in range(2):
                e.wait_ge(*E.free("vec"))
                bk = E.bank("vec")
                for c in range(NC):
                    src = oTa[:, c, :] if c < 4 else oTh[:, c - 4, :]
                    last = mm(bk[:r], src[:, t * P:t * P + r], Wo[:, c, half * 512:(half + 1) * 512], start=c == 0, stop=c == NC - 1)
                last.then_inc(*E.filled("vec", "projected out"))
        for t in range(NT):
            e.wait_ge(*E.at(("x1", t)))
            r = rows(t)
            for half in range(2):
                ring = "act" if half else "vec"
                e.wait_ge(*E.free(ring))
                bk = E.bank(ring)
                for c in range(4):
                    last = e.transpose(bk[:, c * P:c * P + r], X[:r, t, (4 * half + c) * P:(4 * half + c + 1) * P], ident[:r, :r])
                last.then_inc(*E.filled(ring, ("x1 read", t)))
        e.wait_ge(*E.at("x1T by act"))
        e.wait_ge(*E.at("x1T by vec"))
        e.wait_ge(*E.at("router_in"))
        e.wait_ge(*E.free("vec"))
        bk = E.bank("vec")
        for t in range(NT):
            r = rows(t)
            for c in range(NC):
                last = mm(bk[:r, t * NE:(t + 1) * NE], x1T[:, c, t * P:t * P + r], rw[:, c, :], start=c == 0, stop=c == NC - 1)
        last.then_inc(*E.filled("vec"))
        e.wait_ge(*E.at("router done"))

        def gate_up(k, b):
            e.wait_ge(msem[f"w{b}_loaded"], 48 * ((k - b) // 2 + 1) if isinstance(k, int) else k[1])
            for s, (f, n) in enumerate(GU_JOBS):
                a, w = CHUNKS[n]
                slot = 6 * k + s if isinstance(k, int) else k[0] * 6 + s
                e.wait_ge(msem["gu_free"], slot + 1)
                for wt, bank in ((Wg, gate_bank), (Wu, up_bank)):
                    for c in range(NC):
                        last = mm(bank[s % 2][:, 0:w], wt[b][:, c, f * P:(f + 1) * P], x1T[:, c, a:a + w], start=c == 0, stop=c == NC - 1)
                last.then_inc(msem["gu_filled"], 1)

        def down(k, b):
            kk = k if isinstance(k, int) else k[0]
            e.wait_ge(msem["gu_free"], 6 * kk + 8)
            for t in range(NT):
                r = rows(t)
                for half in range(2):
                    j = 2 * t + half
                    e.wait_ge(msem["y_free"], 18 * kk + j + 1)
                    bank = y_bank[j % 3]
                    for f in range(2):
                        last = mm(bank[:r], hh[b][:, f, t * P:t * P + r], Wd[b][:, f, half * 512:(half + 1) * 512], start=f == 0, stop=f == 1)
                    last.then_inc(msem["y_filled"], 1)

        gate_up(0, 0)
        with e.Fori(0, NE // 2 - 1) as i:
            gate_up((2 * i + 1, 48 * i + 48), 1)
            down((2 * i, None), 0)
            gate_up((2 * i + 2, 48 * i + 96), 0)
            down((2 * i + 1, None), 1)
        gate_up(NE - 1, 1)
        down(NE - 2, 0)
        down(NE - 1, 1)

    @block.scalar
    def _(e):
        E = Engine(ev, e, "scalar")
        E.banks = banks
        act = e.activation

        def rsqrt_of_variance(tag):
            E.stage(tag)
            e.wait_ge(*E.at(("variances", tag)))
            act(rstd, rstd, ACT.Ln).then_inc(*E.done())
            e.wait_ge(*E.own())
            act(rstd, rstd, ACT.Exp, scale=-0.5).then_inc(*E.done(("rstd", tag)))

        def transposed(dst, tag):
            for t in range(NT):
                r = rows(t)
                e.wait_ge(*E.full("act"))
                bk = E.job("act")
                e.copy(dst[:, 4:8, t * P:t * P + r], bk.rearrange("p (c n) -> p c n", c=4)[:, :, 0:r]).then_inc(*E.drained("act", tag))

        rsqrt_of_variance("ln0")
        transposed(xT, "xT by act")
        e.wait_ge(*E.at("hgrn_in"))
        for h in range(H):
            E.stage("hgrn")
            if h:
                e.wait_ge(*E.at(("hgrn done", h - 1)))
            for m, dst in enumerate((hq, hz, hy)):
                for a, n in CHUNKS:
                    e.wait_ge(*E.full("act"))
                    bk = E.job("act")
                    act(dst[:, a:a + n], bk[:, 0:n], ACT.Identity, bias=bcol[:, 4 * m + h:4 * m + h + 1]).then_inc(*E.drained("act", ("projected", h, m)))
            e.wait_ge(*E.own())
            act(ke, hz, ACT.Abs).then_inc(*E.done())
            e.wait_ge(*E.own())
            act(ke, ke, ACT.Exp, scale=-1.0).then_inc(*E.done())
            e.wait_ge(*E.own())
            act(ke, ke, ACT.Ln, bias=1.0).then_inc(*E.done(("softplus", h)))
            act(hs, hy, ACT.Exp, scale=-1.0).then_inc(*E.done(("gate exp", h)))
            e.wait_ge(*E.at(("g-z", h)))
            act(hk, hk, ACT.Exp).then_inc(*E.done(("k", h)))
            e.wait_ge(*E.at(("b", h)))
            act(qe, hb, ACT.Exp).then_inc(*E.done(("exp b", h)))
            e.wait_ge(*E.at(("bl-b", h)))
            act(ke, ke, ACT.Exp).then_inc(*E.done(("decay to end", h)))
            for l in range(7):
                n = NTOK if l >= 5 else SEQ
                e.wait_ge(*E.at(("diff", h, l)))
                act(lev[l % 2][:, 0:n], lev[l % 2][:, 0:n], ACT.Exp).then_inc(*E.done(("decay", h, l)))
            for g in range(2):
                e.wait_ge(*E.full("act"))
                bk = E.job("act")
                e.copy(KeT[:, 4 * g:4 * g + 4, :], bk.rearrange("p (c n) -> p c n", c=4)).then_inc(*E.drained("act"))
            e.wait_ge(*E.full("act"))
            bk = E.job("act")
            e.copy(KeT[:NS, 8, :], bk[:NS, 0:P]).then_inc(*E.drained("act", ("KeT", h)))
            for a, n in CHUNKS:
                e.wait_ge(*E.full("act"))
                bk = E.job("act")
                e.copy(oraw[:, a:a + n], bk[:, 0:n]).then_inc(*E.drained("act"))
            e.wait_ge(*E.own())
            act(lev[0], oraw, ACT.Square).then_inc(*E.done(("squares", h)))
            e.wait_ge(*E.at(("eps", 0)))
            for a, n in CHUNKS:
                e.wait_ge(*E.full("act"))
                bk = E.job("act")
                act(lev[1][:, a:a + n], bk[:, 0:n], ACT.Ln, scale=1.0 / P, bias=eps_col[:, 0:1]).then_inc(*E.drained("act"))
            e.wait_ge(*E.own())
            act(lev[1], lev[1], ACT.Exp, scale=-0.5).then_inc(*E.done(("rrms", h)))
        E.stage("p2b")
        e.wait_ge(*E.at("bcolq ready"))
        for h in range(H):
            for a, n in CHUNKS:
                e.wait_ge(*E.full("act"))
                bk = E.job("act")
                dst = QT[:, h, a:a + n] if a < SEQ else QTs[:, h, :]
                act(dst, bk[:, 0:n], ACT.Identity, bias=bcolq[:, h:h + 1], scale=HD ** -0.5).then_inc(*E.drained("act", "QT ready"))
        e.wait_ge(*E.at("gate logits"))
        act(LF, tmp9[:, :, 0:4], ACT.Abs).then_inc(*E.done())
        act(GT, tmp9[:, :, 4:16], ACT.Exp, scale=-1.0).then_inc(*E.done("gate exps"))
        e.wait_ge(*E.own())
        act(LF, LF, ACT.Exp, scale=-1.0).then_inc(*E.done())
        e.wait_ge(*E.own())
        act(LF, LF, ACT.Ln, bias=1.0).then_inc(*E.done("fox softplus"))
        E.stage("p3")
        for h in range(H):
            if h:
                e.wait_ge(*E.at(("strip stored", h - 1)))
            for a in range(0, STRIPW, 512):
                n = min(512, STRIPW - a)
                e.wait_ge(*E.full("act"))
                bk = E.job("act")
                e.copy(strip_tmp[:, a:a + n], bk[:, 0:n]).then_inc(*E.drained("act", ("strip rows", h)))
        for t in range(8):
            e.wait_ge(*E.full("act"))
            bk = E.job("act")
            e.copy(KT[0:64, :, t * P:(t + 1) * P], bk[0:64].rearrange("p (c n) -> p c n", c=4)).then_inc(*E.drained("act", "KT by act"))

        def gelu_exp(n, tag):
            e.wait_ge(*E.at((tag, "inner")))
            act(gu[:, 0:n], gu[:, 0:n], ACT.Exp, scale=-1.5957691216057308).then_inc(*E.done((tag, "exp")))

        gelu_exp(126, "cmp hidden")
        E.stage("attn")
        n = len(UNITS)
        for it in range(n + 3):
            u = it - 2
            if 0 <= u < n:
                h, kind, i = UNITS[u]
                _, L, nb = unit_keys(kind, i)
                for j, ring in enumerate(transpose_rings(u, nb)):
                    if ring == "act":
                        k, w = min(4, nb - 4 * j), min(P, L)
                        e.wait_ge(*E.full("act"))
                        bk = E.job("act")
                        if u >= 2:
                            e.wait_ge(*E.at(("unit", u - 2)))
                        e.copy(PT[u % 2][:w, 4 * j:4 * j + k, :], bk[:w, 0:k * P].rearrange("p (c n) -> p c n", c=k)).then_inc(*E.drained("act", ("pt", u, j)))
            u = it
            if u < n:
                h, kind, i = UNITS[u]
                _, L, _ = unit_keys(kind, i)
                e.wait_ge(*E.at(("scores", u)))
                s = S[u % 4][:, 0:L]
                act(s, s, ACT.Exp, bias=small[:, u % 4, 0:1], accum_out=small[:, u % 4, 1:2]).then_inc(*E.done(("probs", u)))
        E.stage("p4")
        for t in range(8):
            e.wait_ge(*E.full("act"))
            bk = E.job("act")
            e.copy(oTa[:, :, t * P:(t + 1) * P], bk.rearrange("p (c n) -> p c n", c=4)).then_inc(*E.drained("act", "oTa by act"))
        for b in range(DB):
            e.wait_ge(*E.full("act"))
            bk = E.job("act")
            e.copy(FKT[:, :, b, :], bk.rearrange("p (c n) -> p c n", c=2)).then_inc(*E.drained("act", "sample keys by act"))
        gelu_exp(240, "sample cmp hidden")
        for k in range(4):
            e.wait_ge(*E.at(("sample scores", k)))
            s = Ss[k][:, 0:(SK if k < 3 else NCMPS)]
            act(s, s, ACT.Exp, bias=sm[:, k:k + 1], accum_out=ss[:, k:k + 1]).then_inc(*E.done(("sample exp", k)))
        rsqrt_of_variance("ln1")
        transposed(x1T, "x1T by act")
        e.wait_ge(*E.at("router logits"))
        act(rs, rs, ACT.Exp, scale=-1.0).then_inc(*E.done("router exp"))

        def gate_exp(k):
            for s, (f, n) in enumerate(GU_JOBS):
                w = CHUNKS[n][1]
                e.wait_ge(msem["gu_filled"], 6 * k + s + 1)
                e.wait_ge(msem["gu_free"], 6 * k + s + 1)
                act(eb[s % 2][:, 0:w], gate_bank[s % 2][:, 0:w], ACT.Exp, scale=-1.0).then_inc(msem["exp_done"], 1)

        with e.Fori(0, NE) as k:
            gate_exp(k)
        rsqrt_of_variance("ln2")

    @block.vector
    def _(e):
        E = Engine(ev, e, "vector")
        E.banks = banks
        tt, ts, stt, cp = e.tensor_tensor, e.tensor_scalar, e.scalar_tensor_tensor, e.tensor_copy

        def layer_norm(Xt, tag, loaded, name):
            e.memset(mv, 1.0).then_inc(*E.done())
            for t in range(NT):
                r = rows(t)
                loaded(t)
                for half in range(2):
                    e.bn_stats(stats[:r, t, 6 * half:6 * half + 6], Xt[:r, t, 512 * half:512 * half + 512]).then_inc(*E.done())
            e.wait_ge(*E.own())
            for t in range(NT):
                r = rows(t)
                e.bn_aggr(mv[:r, t, :], stats[:r, t, :]).then_inc(*E.done())
            e.wait_ge(*E.own())
            ts(rstd, mv[:, :, 1], EPS, None, ALU.add).then_inc(*E.done(("variances", tag)))
            e.wait_ge(*E.at(f"{tag}_in" if tag != "ln0" else "ln_in"))
            for t in range(NT):
                r = rows(t)
                stt(Xt[:r, t, :], Xt[:r, t, :], mv[:r, t, 0:1], ln_g[:r], ALU.subtract, ALU.mult).then_inc(*E.done())
            e.wait_ge(*E.own())
            e.wait_ge(*E.at(("rstd", tag)))
            for t in range(NT):
                r = rows(t)
                stt(Xt[:r, t, :], Xt[:r, t, :], rstd[:r, t:t + 1], ln_b[:r], ALU.mult, ALU.add).then_inc(*E.done((name, t)))

        def transposed(dst, tag):
            for t in range(NT):
                r = rows(t)
                e.wait_ge(*E.full("vec"))
                bk = E.job("vec")
                cp(dst[:, 0:4, t * P:t * P + r], bk.rearrange("p (c n) -> p c n", c=4)[:, :, 0:r]).then_inc(*E.drained("vec", tag))

        E.stage("ln0")
        e.memset(eps_col, EPS).then_inc(*E.done(("eps", 0)))
        layer_norm(X1, "ln0", lambda t: e.wait_ge(*E.at(f"x{t}_in")), "x normal")
        transposed(xT, "xT by vec")
        E.stage("p2")
        e.wait_ge(*E.at("x_spill"))
        e.wait_ge(*E.at("hgrn_in"))
        e.wait_ge(*E.at("x transposed pe"))
        e.memset(reset, 1.0).then_inc(*E.done())
        e.wait_ge(*E.own())
        e.memset(skew(reset, 0, [P, 8]), 0.0).then_inc(*E.done())
        e.memset(skew(reset, SEQ, [DS, DB]), 0.0).then_inc(*E.done())
        for t in range(NT):
            r = rows(t)
            e.wait_ge(*E.full("vec"))
            bk = E.job("vec")
            tt(V[:r, t, :], bk[:r], b_v[:r], ALU.add).then_inc(*E.drained("vec", "V ready"))

        e.wait_ge(*E.own())
        E.stage("hgrn")
        for h in range(H):
            e.wait_ge(*E.own())
            e.wait_ge(*E.at(("softplus", h)))
            e.wait_ge(*E.at(("projected", h, 1)))
            stt(lev[0], hz, 0.0, ke, ALU.min, ALU.subtract).then_inc(*E.done())
            e.wait_ge(*E.own())
            tt(hk, lev[0], hz, ALU.subtract).then_inc(*E.done(("g-z", h)))
            e.tensor_tensor_scan(hb, reset, lev[0], 0.0, ALU.mult, ALU.add).then_inc(*E.done(("b", h)))
            e.memset(AT, 0.0).then_inc(*E.done())
            e.memset(ATs, 0.0).then_inc(*E.done())
            e.memset(Sall[:, 0, :], 0.0).then_inc(*E.done())
            e.wait_ge(*E.own())
            for n, c, a in ((P, 8, 0), (DS, DB, SEQ)):
                ends = skew(hb, a + n - 1, [n, c], [0, n])
                o = (a, a + n * c)
                v = [x[:, o[0]:o[1]].rearrange("p (c n) -> p c n", n=n) for x in (ke, hb)]
                tt(v[0], ends, v[1], ALU.subtract).then_inc(*E.done(("bl-b", h)))
            e.wait_ge(*E.at(("exp b", h)))
            cp(ebl[:, 0:8], skew(qe, P - 1, [P, 8])).then_inc(*E.done())
            cp(ebl[:, 8:16], skew(qe, SEQ + DS - 1, [DS, DB])).then_inc(*E.done(("ebl", h)))

            def views(x, l):
                n = NTOK if l >= 5 else SEQ
                return x[:, 0:n].rearrange("p (n two m) -> p n two m", two=2, m=LEVELS[l])

            def refs(l):
                m, n = LEVELS[l], (NTOK if l >= 5 else SEQ)
                return skew(hb, m - 1, [2 * m, n // (2 * m)], [0, m])

            for l in range(10):
                if l < 7:
                    if l >= 2:
                        e.wait_ge(*E.at(("level used", h, l - 2)))
                    lv, b = views(lev[l % 2], l), views(hb, l)
                    tt(lv[:, :, 0, :], refs(l), b[:, :, 0, :], ALU.subtract).then_inc(*E.done())
                    tt(lv[:, :, 1, :], b[:, :, 1, :], refs(l), ALU.subtract).then_inc(*E.done(("diff", h, l)))
                if 1 <= l < 8:
                    e.wait_ge(*E.at(("decay", h, l - 1)))
                    lv, q = views(lev[(l - 1) % 2], l - 1), views(hq, l - 1)
                    tt(lv[:, :, 1, :], lv[:, :, 1, :], q[:, :, 1, :], ALU.mult).then_inc(*E.done(("level q", h, l - 1)))
                if l >= 2:
                    k = l - 2
                    e.wait_ge(*E.own())
                    for g in range(2):
                        e.wait_ge(*E.full("vec"))
                        bk = E.job("vec")
                        mask = lvmask[:, k:k + 1, :].to_broadcast([P, 4, P])
                        e.copy_predicated(AT[:, 4 * g:4 * g + 4, :], mask, bk.rearrange("p (c n) -> p c n", c=4)).then_inc(*E.drained("vec", ("AT", h)))
                    if k >= 5:
                        e.wait_ge(*E.full("vec"))
                        bk = E.job("vec")
                        e.copy_predicated(ATs[:NS, :], lvmask[:NS, k, 0:NS], bk[:NS, 0:NS]).then_inc(*E.drained("vec", ("AT", h)))
            if h:
                e.wait_ge(*E.at(("states stored", h - 1)))
            vb = V[:NS, 8, h * P:(h + 1) * P].unsqueeze(1).to_broadcast([NS, DB, P])
            tt(VM[:NS], vb, C["s_batch"][:NS].unsqueeze(2).to_broadcast([NS, DB, P]), ALU.mult).then_inc(*E.done(("VM", h)))
            for g in range(2):
                e.wait_ge(*E.full("vec"))
                bk = E.job("vec")
                for c in range(4):
                    n = 4 * g + c
                    e.wait_ge(*E.own())
                    i = stt(Sall[:, n + 1, :], Sall[:, n, :], ebl[:, n:n + 1], bk[:, c * P:(c + 1) * P], ALU.mult, ALU.add)
                    i.then_inc(*(E.done() if c < 3 else E.drained("vec", ("states", h))))
            e.wait_ge(*E.at(("s0", h)))
            for g in range(2):
                e.wait_ge(*E.full("vec"))
                bk = E.job("vec")
                if g == 0:
                    e.wait_ge(*E.at(("filled", "vec", E.jobs["vec"] + 1)))
                for c in range(4):
                    b = 4 * g + c
                    i = stt(VM[:, b, :], S0[:, b, :], ebl[:, 8 + b:9 + b], bk[:, c * P:(c + 1) * P], ALU.mult, ALU.add)
                    i.then_inc(*(E.done() if c < 3 else E.drained("vec", ("new states", h))))
            e.wait_ge(*E.at(("gate exp", h)))
            ts(hs, hs, 1.0, None, ALU.add).then_inc(*E.done())
            e.wait_ge(*E.own())
            e.reciprocal(hs, hs).then_inc(*E.done())
            e.wait_ge(*E.own())
            tt(hy, hy, hs, ALU.mult).then_inc(*E.done())
            e.wait_ge(*E.at(("rrms", h)))
            e.wait_ge(*E.at(("hgrn outputs", h)))
            stt(oraw, oraw, bcol[:, 12:13], lev[1], ALU.mult, ALU.mult).then_inc(*E.done())
            e.wait_ge(*E.own())
            tt(oTh[:, h, :], oraw, hy, ALU.mult).then_inc(*E.done(("hgrn done", h)))

        E.stage("p2b")
        e.wait_ge(*E.at("attn_in"))
        e.wait_ge(*E.at(("states stored", H - 1)))
        e.wait_ge(*E.at(("hgrn done", H - 1)))
        ts(bcolq, bcolq, HD ** -0.5, None, ALU.mult).then_inc(*E.done("bcolq ready"))
        for t in range(NT):
            r = rows(t)
            e.wait_ge(*E.full("vec"))
            bk = E.job("vec")
            dst = fkv[:, t, :] if t < 8 else fkv8[:NS]
            tt(dst, bk[:r], b_fkv[:r], ALU.add).then_inc(*E.drained("vec", ("fkv", t), "fkv ready"))
        e.memset(tmp9, 0.0).then_inc(*E.done())
        for t in range(NT):
            r = rows(t)
            e.wait_ge(*E.full("vec"))
            bk = E.job("vec")
            dst = nkvg[:, t, :] if t < 8 else nkvg8[:NS]
            tt(dst, bk[:r, 0:400], b_nkvg[:r], ALU.add).then_inc(*E.drained("vec", ("nkvg", t), "nkvg ready"))
        e.wait_ge(*E.own())
        for src, dst in ((nkvg, tmp9[:, 0:8, :]), (nkvg8[:NS].rearrange("p (a n) -> p a n", a=1), tmp9[:NS, 8:9, :])):
            cp(dst[:, :, 0:4], src[:, :, 396:400]).then_inc(*E.done())
            cp(dst[:, :, 4:16], src[:, :, 384:396]).then_inc(*E.done("gate logits"))
        e.wait_ge(*E.own())
        e.wait_ge(*E.at("fox softplus"))
        e.wait_ge(*E.at("gate exps"))
        stt(LF, tmp9[:, :, 0:4], 0.0, LF, ALU.min, ALU.subtract).then_inc(*E.done("LF ready"))
        ts(GT, GT, 1.0, None, ALU.add).then_inc(*E.done())
        e.wait_ge(*E.own())
        e.reciprocal(GT, GT).then_inc(*E.done())

        E.stage("p3")
        e.wait_ge(*E.at("tab_in"))
        cp(tabB[:33], tab33[:33].unsqueeze(2).to_broadcast([33, H, P])).then_inc(*E.done("tabB"))
        for t in range(8):
            e.wait_ge(*E.full("vec"))
            bk = E.job("vec")
            cp(kcvc[:, t * P:(t + 1) * P], bk[:, 0:P]).then_inc(*E.done())
            cp(KT[64:128, 0:2, t * P:(t + 1) * P], bk[64:128, P:3 * P].rearrange("p (c n) -> p c n", c=2)).then_inc(*E.drained("vec", "KT by vec"))
        e.wait_ge(*E.full("vec"))
        bk = E.job("vec")
        cp(kcvc[:, SEQ:], bk[:, 0:32]).then_inc(*E.drained("vec", "kcvc ready"))

        def gelu(n, tag):
            x, u = gx[:, 0:n], gu[:, 0:n]
            e.wait_ge(*E.own())
            tt(u, x, x, ALU.mult).then_inc(*E.done())
            e.wait_ge(*E.own())
            ts(u, u, 0.044715, 1.0, ALU.mult, ALU.add).then_inc(*E.done())
            e.wait_ge(*E.own())
            tt(u, u, x, ALU.mult).then_inc(*E.done((tag, "inner")))
            e.wait_ge(*E.at((tag, "exp")))
            ts(u, u, 1.0, None, ALU.add).then_inc(*E.done())
            e.wait_ge(*E.own())
            e.reciprocal(u, u).then_inc(*E.done())
            e.wait_ge(*E.own())
            tt(x, x, u, ALU.mult).then_inc(*E.done(tag))

        for kv in range(2):
            e.wait_ge(*E.full("vec"))
            bk = E.job("vec")
            cp(pc[:, kv:kv + 1], bk[:, 64:65]).then_inc(*E.done())
            e.wait_ge(*E.own())
            ts(gx[:, NCMP * kv:NCMP * (kv + 1)], bk[:, 0:NCMP], pc[:, kv:kv + 1], None, ALU.add).then_inc(*E.drained("vec"))
        for k in range(2):
            cp(w2d[:, 64 * k:64 * k + 64], w2[:, 0, 0:64]).then_inc(*E.done())
        gelu(2 * NCMP, "cmp hidden")
        e.wait_ge(*E.full("vec"))
        bk = E.job("vec")
        cp(KC[64:128, 0:NCMP], bk[64:128, 0:NCMP]).then_inc(*E.drained("vec"))
        e.wait_ge(*E.full("vec"))
        bk = E.job("vec")
        cp(VC[:NCMP, :], bk[:NCMP, 0:64]).then_inc(*E.drained("vec", "KC ready"))

        E.stage("attn")

        def decay_rows(h):
            e.wait_ge(*E.own())
            for g in range(2):
                e.wait_ge(*E.full("vec"))
                bk = E.job("vec")
                for c in range(4):
                    n = 4 * g + c
                    e.wait_ge(*E.own())
                    carry = negc[:, n * P - 1:n * P] if n else 0.0
                    i = ts(negc[:, n * P:(n + 1) * P], bk[:, c * P:(c + 1) * P], carry, None, ALU.add)
                    i.then_inc(*(E.done() if c < 3 else E.drained("vec", ("negc", h))))

        def scores(u):
            h, kind, i = UNITS[u]
            first, L, nb = unit_keys(kind, i)
            sm_, s = small[:, u % 4], S[u % 4]
            if u >= 4:
                e.wait_ge(*E.at(("unit", u - 4)))
            e.wait_ge(*E.at(("foxdiag", h) if kind == "fox" else ("strips", h)))
            m = -1
            for a in range(0, L, 512):
                n = min(512, L - a)
                if kind == "fox":
                    off = min(n, i * P - a)
                    pieces = [(0, off, negc[:, a:a + off])] if off > 0 else []
                    if a + n == L:
                        pieces.append((n - P, P, foxdiag[:, i, :]))
                elif kind == "cmp":
                    pieces = [(0, n, skew(strip_s, 896 - P * i + 31, [16, n]))]
                else:
                    st, off = (strip_s, 896 - P * i) if kind == "slc" else (strip_w, WIN - P * i)
                    pieces = [(0, n, st[:, off + first + a:off + first + a + n])]
                e.wait_ge(*E.full("vec"))
                bk = E.job("vec")
                for j, (o, w, bias) in enumerate(pieces):
                    if m >= 0:
                        e.wait_ge(*E.own())
                    prior = sm_[:, 4 + m:5 + m] if m >= 0 else FLOOR
                    m += 1
                    ins = e.tensor_tensor_reduce(out=s[:, a + o:a + o + w], in0=bk[:, o:o + w], in1=bias, scale=1.0, scalar=prior,
                                                 op0=ALU.add, op1=ALU.max, accum_out=sm_[:, 4 + m:5 + m])
                    ins.then_inc(*(E.drained("vec") if j == len(pieces) - 1 else E.done()))
            e.wait_ge(*E.own())
            used = [("strips used", h)] if u % 32 == 31 else []
            ts(sm_[:, 0:1], sm_[:, 4 + m:5 + m], -1.0, None, ALU.mult).then_inc(*E.done(("scores", u), *used))

        def finish(u):
            h, kind, i = UNITS[u]
            sm_ = small[:, u % 4]
            e.wait_ge(*E.full("vec"))
            bk = E.job("vec")
            ts(sm_[:, 2:3], sm_[:, 1:2], TINY, None, ALU.max).then_inc(*E.done())
            e.wait_ge(*E.own())
            e.reciprocal(sm_[:, 2:3], sm_[:, 2:3]).then_inc(*E.done())
            e.wait_ge(*E.own())
            if kind == "fox":
                ins = ts(OT[:, i, h * HD:(h + 1) * HD], bk[:, 0:64], sm_[:, 2:3], None, ALU.mult)
            else:
                g = {"cmp": 0, "slc": 1, "win": 2}[kind]
                o = OT[:, i, 256 + h * HD:256 + (h + 1) * HD]
                gate = GT[:, i, 3 * h + g:3 * h + g + 1]
                if kind == "slc":
                    ins = ts(o, bk[:, 0:64], sm_[:, 2:3], gate, ALU.mult, ALU.mult)
                else:
                    tt(sm_[:, 3:4], sm_[:, 2:3], gate, ALU.mult).then_inc(*E.done())
                    e.wait_ge(*E.own())
                    ins = stt(o, bk[:, 0:64], sm_[:, 3:4], o, ALU.mult, ALU.add)
            ins.then_inc(*E.drained("vec", "prompt attention done"))

        n = len(UNITS)
        for it in range(n + 3):
            if it < n:
                if it % 32 == 0:
                    decay_rows(UNITS[it][0])
                scores(it)
            u = it - 2
            if 0 <= u < n:
                h, kind, i = UNITS[u]
                _, L, nb = unit_keys(kind, i)
                for j, ring in enumerate(transpose_rings(u, nb)):
                    if ring == "vec":
                        k, w = min(4, nb - 4 * j), min(P, L)
                        e.wait_ge(*E.full("vec"))
                        bk = E.job("vec")
                        if u >= 2:
                            e.wait_ge(*E.at(("unit", u - 2)))
                        cp(PT[u % 2][:w, 4 * j:4 * j + k, :], bk[:w, 0:k * P].rearrange("p (c n) -> p c n", c=k)).then_inc(*E.drained("vec", ("pt", u, j)))
            if it >= 3:
                finish(it - 3)

        E.stage("p4")
        for b in range(DB):
            e.wait_ge(*E.full("vec"))
            bk = E.job("vec")
            cp(KVT[:, b, :], bk[:, 0:PAST]).then_inc(*E.done())
            cp(T1[64:128, b, :], bk[64:128, PAST:512]).then_inc(*E.drained("vec"))
            e.wait_ge(*E.full("vec"))
            bk = E.job("vec")
            cp(T1[0:64, b, :], bk[0:64, 0:PAST]).then_inc(*E.drained("vec"))
        e.wait_ge(*E.full("vec"))
        bk = E.job("vec")
        cp(KTn, bk[:, 0:P].rearrange("p (c n) -> p c n", c=4)).then_inc(*E.drained("vec", "sample keys"))
        e.wait_ge(*E.at("sample zeros"))
        e.wait_ge(*E.at("tabx_in"))
        for h in range(H):
            s = slice(64 * (h % 2), 64 * (h % 2) + 64)
            q = QTs[:, h, :].rearrange("p (b q) -> p b q", q=DS)
            cp(skew(QSall[s, h // 2, :], 4 * h, [16, DB], [1, DS]), q[0:64]).then_inc(*E.done())
            for s in (slice(0, 64), slice(64, 128)):
                cp(skew(QNall[s, :], 4 * h, [16, DB], [1, DS]), q[64:128]).then_inc(*E.done())
        e.wait_ge(*E.own())
        for c in range(2):
            cp(skew(QS[:, c, 0, :], 0, [P + 16, DB], [1, 16]), QSall[:, c, :].rearrange("p (b r) -> p b r", b=DB)).then_inc(*E.done())
        cp(skew(QN[:, 0, :], 0, [P + 16, DB], [1, 16]), QNall.rearrange("p (b r) -> p b r", b=DB)).then_inc(*E.done())
        bhq = "p (b h q) -> p b h q"
        for j in range(NP):
            cp(LFr[:, j, :].rearrange(bhq, b=DB, h=H), skew(LFc[:, 0, j, :], 0, [NP * H, DB], [1, H], [0, DS])).then_inc(*E.done())
        cp(LFn[:NS].rearrange(bhq, b=DB, h=H), skew(LF[:NS, 8, :], 0, [0, DB], [1, H], [0, DS])).then_inc(*E.done())
        tt(TX.rearrange(bhq, b=DB, h=H), skew(tabX, 0, [0, DB], [1, H], [0, DS]),
                C["s_expand"].rearrange(bhq, b=DB, h=H), ALU.mult).then_inc(*E.done("sample operands"))
        e.wait_ge(*E.full("vec"))
        bk = E.job("vec")
        tt(f_bias, bk[:, 0:SK], C["s_mask"][:, 0:SK], ALU.add).then_inc(*E.drained("vec"))
        e.wait_ge(*E.full("vec"))
        bk = E.job("vec")
        tt(s_bias, bk[:, 0:SKC], C["s_mask"], ALU.add).then_inc(*E.drained("vec"))
        e.wait_ge(*E.full("vec"))
        bk = E.job("vec")
        tt(sg.rearrange("p (g h) -> p g h", g=3), bk[:, 0:12].rearrange("p (h g) -> p g h", g=3),
                            C["s_head"].unsqueeze(1).to_broadcast([P, 3, H]), ALU.mult).then_inc(*E.drained("vec"))
        e.wait_ge(*E.own())
        e.tensor_reduce(gsel[:, 0:3], sg.rearrange("p (g h) -> p g h", g=3), AXX, ALU.add).then_inc(*E.done())
        for kv in range(2):
            e.wait_ge(*E.full("vec"))
            bk = E.job("vec")
            ts(gx[:, 120 * kv:120 * (kv + 1)], bk[:, 0:120], pc[:, kv:kv + 1], None, ALU.add).then_inc(*E.drained("vec"))
        gelu(240, "sample cmp hidden")
        e.wait_ge(*E.full("vec"))
        bk = E.job("vec")
        cp(KCs[64:128, :], bk[64:128, 0:120]).then_inc(*E.drained("vec"))
        e.wait_ge(*E.full("vec"))
        bk = E.job("vec")
        cp(VCs[:NCMPS], bk[:NCMPS].rearrange("p (b d) -> p b d", b=DB)).then_inc(*E.drained("vec", "sample cmp ready"))
        for k in range(4):
            w = SK if k < 3 else NCMPS
            bias = f_bias if k == 0 else s_bias[:, 0:SK] if k < 3 else s_bias[:, SK:SKC]
            e.wait_ge(*E.full("vec"))
            bk = E.job("vec")
            e.tensor_tensor_reduce(out=Ss[k][:, 0:w], in0=bk[:, 0:w], in1=bias, scale=1.0, scalar=FLOOR,
                                                    op0=ALU.add, op1=ALU.max, accum_out=sm[:, 4 + k:5 + k]).then_inc(*E.drained("vec"))
            e.wait_ge(*E.own())
            ts(sm[:, k:k + 1], sm[:, 4 + k:5 + k], -1.0, None, ALU.mult).then_inc(*E.done(("sample scores", k)))
        for k in range(4):
            w = SK if k < 3 else NCMPS
            e.wait_ge(*E.at(("sample exp", k)))
            ts(ss[:, 4 + k:5 + k], ss[:, k:k + 1], TINY, None, ALU.max).then_inc(*E.done())
            e.wait_ge(*E.own())
            e.reciprocal(ss[:, 4 + k:5 + k], ss[:, 4 + k:5 + k]).then_inc(*E.done())
            e.wait_ge(*E.own())
            gate = None if k == 0 else gsel[:, (1, 2, 0)[k - 1]:(1, 2, 0)[k - 1] + 1]
            if k:
                ins = ts(Ss[k][:, 0:w], Ss[k][:, 0:w], ss[:, 4 + k:5 + k], gate, ALU.mult, ALU.mult)
            else:
                ins = ts(Ss[k][:, 0:w], Ss[k][:, 0:w], ss[:, 4 + k:5 + k], None, ALU.mult)
            ins.then_inc(*E.done(("sample probs", k)))
        for k in range(4):
            e.wait_ge(*E.full("vec"))
            bk = E.job("vec")
            if k < 3:
                cp(PTs[k][:, 0:2, :], bk[:, 0:2 * P].rearrange("p (c n) -> p c n", c=2)).then_inc(*E.done())
                cp(PTs[k][:NS, 2, :], bk[:NS, 2 * P:3 * P]).then_inc(*E.drained("vec"))
            else:
                cp(PTs[k][:NCMPS, 0, :], bk[:NCMPS, 0:P]).then_inc(*E.drained("vec", "sample PT"))
        for part in range(2):
            e.wait_ge(*E.full("vec"))
            bk = E.job("vec")
            for h in range(H):
                s = slice(64 * (h % 2), 64 * (h % 2) + 64)
                src = skew(bk[s, :], P * (h // 2) + 4 * h, [16, DB], [1, DS]) if part == 0 else skew(bk[0:64, :], 4 * h, [16, DB], [1, DS])
                dst = oTa[s, 2 * part + h // 2, SEQ:].rearrange("p (b q) -> p b q", q=DS)
                ins = cp(dst, src)
                ins.then_inc(*(E.done() if h < 3 else E.drained("vec", "sample attention done")))

        E.stage("p5")
        e.wait_ge(*E.at("xres_in"))
        for t in range(NT):
            r = rows(t)
            for half in range(2):
                x = X[:r, t, half * 512:(half + 1) * 512]
                e.wait_ge(*E.full("vec"))
                bk = E.job("vec")
                stt(x, x, ALPHA, bk[:r], ALU.mult, ALU.add).then_inc(*E.drained("vec"))
        e.wait_ge(*E.own())
        layer_norm(X, "ln1", lambda t: None, "x1")
        e.wait_ge(*E.own())
        transposed(x1T, "x1T by vec")
        E.ev.at["x1 normalised"] = (E.key, E.ev.count[E.key])
        for t in range(NT):
            r = rows(t)
            e.wait_ge(*E.at(("x1 read", t)))
            ts(X[:r, t, :], X[:r, t, :], ALPHA, None, ALU.mult).then_inc(*E.done())
        e.memset(rs, 0.0).then_inc(*E.done())
        e.wait_ge(*E.full("vec"))
        bk = E.job("vec")
        e.wait_ge(*E.own())
        cp(rs[:, 0:8, :], bk[:, 0:8 * NE].rearrange("p (t n) -> p t n", n=NE)).then_inc(*E.done())
        cp(rs[:NS, 8, :], bk[:NS, 8 * NE:9 * NE]).then_inc(*E.drained("vec", "router logits"))
        e.wait_ge(*E.at("router exp"))
        b3 = [P, NT, NE]

        def step(ins, *ev_):
            ins.then_inc(*E.done(*ev_))
            e.wait_ge(*E.own())

        step(ts(rs, rs, 1.0, None, ALU.add))
        step(e.reciprocal(rs, rs))
        step(tt(rb, rs, rbias.unsqueeze(1).to_broadcast(b3), ALU.add))
        g4 = rb.rearrange("p t (g j) -> p t g j", g=4)
        first = True
        for a in range(4):
            for b in range(a + 1, 4):
                dst = rg if first else rgm
                step(tt(dst, g4[:, :, :, a], g4[:, :, :, b], ALU.add))
                if not first:
                    step(tt(rg, rg, rgm, ALU.max))
                first = False

        def first_best(scores_, n, best, out):
            step(e.tensor_reduce(best, scores_, AXX, ALU.max))
            step(tt(out, scores_, best.unsqueeze(2).to_broadcast([P, NT, n]), ALU.is_equal))
            step(tt(out, out, C["iota16"][:, 0:n].unsqueeze(1).to_broadcast([P, NT, n]), ALU.mult))
            step(e.tensor_reduce(best, out, AXX, ALU.min))
            step(tt(out, out, best.unsqueeze(2).to_broadcast([P, NT, n]), ALU.is_equal))

        first_best(rg, 4, rt1, rgm)
        step(cp(rm.rearrange("p t (g j) -> p (t g) j", g=4), rgm.rearrange("p t g -> p (t g)").unsqueeze(2).to_broadcast([P, NT * 4, 4])))
        step(tt(rb, rb, rm, ALU.mult))
        step(ts(rm, rm, -1.0, -MASKED, ALU.add, ALU.mult))
        step(tt(rb, rb, rm, ALU.add))
        first_best(rb, NE, rt1, r1)
        step(stt(rb, r1, 2 * MASKED, rb, ALU.mult, ALU.add))
        first_best(rb, NE, rt1, r2)
        step(tt(r1, r1, r2, ALU.add))
        step(tt(r1, r1, rs, ALU.mult))
        step(e.tensor_reduce(rt1, r1, AXX, ALU.add))
        step(e.reciprocal(rt1, rt1))
        step(tt(comb, r1, rt1.unsqueeze(2).to_broadcast(b3), ALU.mult), "router done")

        e.sem_inc(msem["gu_free"], 2)
        e.sem_inc(msem["y_free"], 3)

        def gate_up(k, base):
            for s, (f, n) in enumerate(GU_JOBS):
                a, w = CHUNKS[n]
                x, g, u = eb[s % 2][:, 0:w], gate_bank[s % 2][:, 0:w], up_bank[s % 2][:, 0:w]
                e.wait_ge(msem["exp_done"], 6 * k + s + 1)
                ts(x, x, 1.0, None, ALU.add).then_inc(msem["vec_steps"], 1)
                e.wait_ge(msem["vec_steps"], base + 3 * s + 1)
                e.reciprocal(x, x).then_inc(msem["vec_steps"], 1)
                e.wait_ge(msem["vec_steps"], base + 3 * s + 2)
                tt(x, x, g, ALU.mult).then_inc(msem["vec_steps"], 1)
                e.wait_ge(msem["vec_steps"], base + 3 * s + 3)
                tt(hh_of(k)[:, f, a:a + w], x, u, ALU.mult).then_inc(msem["gu_free"], 1)

        def hh_of(k):
            return hh[parity[0]]

        parity = [0]

        def down(k, base):
            b = parity[0]
            cp(ccol[b], comb[:, :, bass.ds(k, 1)].rearrange("p t a -> p (t a)")).then_inc(msem["vec_steps"], 1)
            e.wait_ge(msem["vec_steps"], base + 1)
            e.wait_ge(msem["y_free"], 18 * k + 3)
            for t in range(NT):
                r = rows(t)
                for half in range(2):
                    j = 2 * t + half
                    x = X[:r, t, half * 512:(half + 1) * 512]
                    e.wait_ge(msem["y_filled"], 18 * k + j + 1)
                    stt(x, y_bank[j % 3][:r], ccol[b][:r, t:t + 1], x, ALU.mult, ALU.add).then_inc(msem["y_free"], 1)

        def turn(f, k, b, base):
            parity[0] = b
            f(k, base)

        turn(gate_up, 0, 0, 0)
        with e.Fori(0, NE // 2 - 1) as i:
            turn(gate_up, 2 * i + 1, 1, 38 * i + 18)
            turn(down, 2 * i, 0, 38 * i + 36)
            turn(gate_up, 2 * i + 2, 0, 38 * i + 37)
            turn(down, 2 * i + 1, 1, 38 * i + 55)
        last = 38 * (NE // 2 - 1)
        turn(gate_up, NE - 1, 1, last + 18)
        turn(down, NE - 2, 0, last + 36)
        turn(down, NE - 1, 1, last + 37)
        e.wait_ge(msem["y_free"], 18 * NE + 3)
        E.stage("p7")
        layer_norm(X, "ln2", lambda t: None, "y normalised")

    @block.gpsimd
    def _(e):
        E = Engine(ev, e, "gpsimd")
        tt = e.tensor_tensor
        for t in range(NT):
            e.wait_ge(*E.at(("x normal", t)))
            e.dma_start(x_spill[:rows(t), t * D:(t + 1) * D], X1[:rows(t), t, :]).then_inc(*E.moved("x_spill"))
        E.stage("hgrn")
        for h in range(H):
            e.wait_ge(*E.at(("ebl", h)))
            e.wait_ge(*E.at(("projected", h, 0)))
            tt(qe, qe, hq, ALU.mult).then_inc(*E.done(("qe", h)))
            e.wait_ge(*E.at(("decay to end", h)))
            e.wait_ge(*E.at(("k", h)))
            tt(ke, ke, hk, ALU.mult).then_inc(*E.done(("ke", h)))
            for l in range(7):
                n = NTOK if l >= 5 else SEQ
                e.wait_ge(*E.at(("decay", h, l)))
                lv, k = (x[:, 0:n].rearrange("p (n two m) -> p n two m", two=2, m=LEVELS[l])[:, :, 0, :] for x in (lev[l % 2], hk))
                tt(lv, lv, k, ALU.mult).then_inc(*E.done(("level k", h, l)))
            e.wait_ge(*E.at(("states", h)))
            e.dma_start(O_["new_hgrn_p"][0, 0, h], Sall[:, 8, :]).then_inc(*E.moved("hgrn_out", ("states stored", h)))
            e.wait_ge(*E.at(("new states", h)))
            e.dma_start(O_["new_hgrn_s"][0, :, h].rearrange("b d v -> d b v"), VM).then_inc(*E.moved("hgrn_out", ("states stored", h)))
        E.stage("p2b")
        for b in range(DB):
            e.dma_start(O_["new_nsa_win_s"][0, b, 0:PAST - DS].rearrange("t k d -> t (k d)"), I["state_nsa_win"][0, b, DS:].rearrange("t k d -> t (k d)")).then_inc(*E.moved("kv_out"))
        e.wait_ge(*E.at("fkv ready"))
        e.wait_ge(*E.at("nkvg ready"))
        e.wait_ge(*E.at("LF ready"))
        e.dma_start(O_["new_fox_kv_p"][0, 0].rearrange("(t p) k h d -> p t (k h d)", p=P), fkv).then_inc(*E.moved("kv_out"))
        e.dma_start(O_["new_nsa_kv_p"][0, 0].rearrange("(t p) k d -> p t (k d)", p=P), nkvg[:, :, 0:256]).then_inc(*E.moved("kv_out"))
        e.dma_start(O_["new_nsa_win_p"][0, 0].rearrange("(t p) k d -> p t (k d)", p=P), nkvg[:, 4:8, 256:384]).then_inc(*E.moved("kv_out"))
        e.dma_start(O_["new_fox_logf_p"][0, 0].rearrange("(t p) h -> p t h", p=P), LF[:, 0:8, :]).then_inc(*E.moved("kv_out"))
        e.dma_start(O_["new_fox_kv_s"][0].rearrange("b t k h d -> (b t) (k h d)"), fkv8[:NS]).then_inc(*E.moved("kv_out"))
        e.dma_start(O_["new_nsa_kv_s"][0].rearrange("b t k d -> (b t) (k d)"), nkvg8[:NS, 0:256]).then_inc(*E.moved("kv_out"))
        e.dma_start(O_["new_fox_logf_s"][0].rearrange("b t h -> (b t) h"), LF[:NS, 8, :]).then_inc(*E.moved("kv_out"))
        for b in range(DB):
            e.dma_start(O_["new_nsa_win_s"][0, b, PAST - DS:].rearrange("t k d -> t (k d)"), nkvg8[DS * b:DS * b + DS, 256:384]).then_inc(*E.moved("kv_out"))
        E.stage("attn")
        for h in range(H):
            e.wait_ge(*E.at(("negc", h)))
            tt(foxdiag, negc.rearrange("p (t k) -> p t k", t=8), C["diagmask"].unsqueeze(1).to_broadcast([P, 8, P]), ALU.add).then_inc(*E.done(("foxdiag", h)))
        E.stage("p4")
        e.wait_ge(*E.at("prompt attention done"))
        e.wait_ge(*E.at("kv_out"))
        e.wait_ge(*E.at(("states stored", H - 1)))
        for x in (QS, QSall, QN, LFn):
            e.memset(x, 0.0).then_inc(*E.done("sample zeros"))

    return dict(ev.at)


OUTPUTS = [("y_prompt", (1, SEQ, D)), ("y_sample", (DB, DS, D)), ("new_fox_kv_p", (1, 1, SEQ, 2, H, HD)),
           ("new_fox_logf_p", (1, 1, SEQ, H)), ("new_nsa_kv_p", (1, 1, SEQ, 4, HD)), ("new_nsa_win_p", (1, 1, WIN, 2, HD)),
           ("new_hgrn_p", (1, 1, H, P, P)), ("new_fox_kv_s", (1, DB, DS, 2, H, HD)), ("new_fox_logf_s", (1, DB, DS, H)),
           ("new_nsa_kv_s", (1, DB, DS, 4, HD)), ("new_nsa_win_s", (1, DB, PAST, 2, HD)), ("new_hgrn_s", (1, DB, H, P, P))]


def kernel(**inputs):
    import concourse.bacc as bacc
    from concourse.bass_utils import run_bass_kernel_spmd

    arrays = {n: np.ascontiguousarray(a) for n, a in inputs.items() if n != "hg_lb_logits"}
    for n, a in zip(("consts", "level_masks", "bucket_rows", "masked_row"), shape_constants()):
        arrays[n] = a
    known = None
    for _ in range(2):
        nc = bacc.Bacc("TRN2", target_bir_lowering=False, num_devices=1)
        t_in = {n: nc.dram_tensor(f"in_{n}", a.shape, mybir.dt.from_np(a.dtype), kind="ExternalInput").ap() for n, a in arrays.items()}
        t_out = {n: nc.dram_tensor(f"out_{n}", s, F32, kind="ExternalOutput").ap() for n, s in OUTPUTS}
        known = build(nc, t_in, t_out, known)
    r = run_bass_kernel_spmd(nc, [{f"in_{n}": a for n, a in arrays.items()}], core_ids=[0])
    return tuple(r.results[0][f"out_{n}"] for n, _ in OUTPUTS)
```

```python
import math
from contextlib import ExitStack

import numpy as np
import concourse.bass as bass
from concourse import mybir

F32 = mybir.dt.float32
I32 = mybir.dt.int32
ALU = mybir.AluOpType
ACT = mybir.ActivationFunctionType
AXX = mybir.AxisListType.X

P = 128
D = 1024
NC = D // P
SEQ = 1024
DB, DS = 8, 4
NS = DB * DS
NTOK = SEQ + NS
NT = 9
PAST, PAGE = 256, 128
NP = PAST // PAGE
H, HD = 4, 64
WIN, NCMP, NCMPS = 512, 63, 15
NE, FE = 16, 256
TILES = NE + (2 * NTOK - NE) // P
SLOTS = TILES * P
ALPHA = 2 ** 0.25
EPS = 1e-5
MASKED = -1e30
FLOOR = -1e29
TINY = 1e-30
LEVELS = (64, 32, 16, 8, 4, 2, 1)
GROUPS = (range(0, 3), range(3, 6), range(6, 9))
CHUNKS = ((0, 512), (512, 512), (1024, 32))
FQ, FK, FV, FF, NQ, NKV, NG, HQ, HF, HI, HG = 0, 256, 512, 768, 772, 1028, 1412, 1424, 1936, 2448, 2960
P_IN = 3472
SLCW, WINW = 1151, 767
STRIPW = SLCW + WINW
SK = PAST + NS
SKC = SK + NCMPS


def rows(t):
    return P if t < 8 else NS


def bucket(n):
    return n if n < 16 else min(31, 16 + int(np.float32(math.log(n / 16)) / math.log(8) * 16 + 1e-6))


CONST = {}


def shape_constants():
    parts, at = [], 0

    def put(name, a):
        nonlocal at
        full = np.zeros((P, a.shape[1]), np.float32)
        full[:a.shape[0]] = a
        CONST[name] = (at, a.shape[1])
        parts.append(full)
        at += a.shape[1]

    i = np.arange(P)
    put("ident", np.eye(P))
    put("ones", np.ones((P, P)))
    put("negtri", -(i[:, None] <= i[None, :]).astype(np.float32))
    put("negones", -np.ones((P, P)))
    put("diagmask", np.where(i[None, :] > i[:, None], MASKED, 0))
    r_b, r_h, r_q = i // 16, i // 4 % 4, i % 4
    j = np.arange(NS)
    q_of, bk = i // 32, i % 32
    oh = np.zeros((P, SKC))
    for c in range(SKC):
        for q in range(DS):
            if c < PAST:
                d = PAST + q - c
            elif c < SK:
                d = q - (c - PAST) % DS
            else:
                d = PAST + q - 16 * (c - SK) - 31
            if d >= 0:
                oh[32 * q + bucket(d), c] = 1
    put("s_onehot", oh)
    put("s_expand", (q_of[:, None] == r_q[None, :]))
    m = np.zeros((P, SKC))
    m[:, PAST:SK] = np.where((r_b[:, None] == (j // DS)[None, :]) & (r_q[:, None] >= (j % DS)[None, :]), 0, MASKED)
    put("s_mask", m)
    put("s_negtri", -((j[:, None] // DS == j[None, :] // DS) & (j[:, None] <= j[None, :])).astype(np.float32))
    put("s_sel", (j[:, None] == (r_b * DS + r_q)[None, :]))
    put("s_head", (r_h[:, None] == np.arange(H)[None, :]))
    put("s_batch", (j[:, None] // DS == np.arange(DB)[None, :]))
    put("before", (i[:, None] < i[None, :]))
    put("steps", np.tile(np.arange(NT) * float(P), (P, 1)))
    put("tiles", np.tile(np.arange(TILES) * 1.0, (P, 1)))
    put("token", (np.arange(NT)[None, :] * P + i[:, None] < NTOK))
    put("iota16", np.tile(np.arange(16) - 99.0, (P, 1)))
    fl = np.ascontiguousarray(np.concatenate(parts, 1), np.float32)
    lv = np.zeros((P, 8, P), np.int32)
    for n, m_ in enumerate(LEVELS):
        s, t = i[:, None], i[None, :]
        lv[:, n] = (s // (2 * m_) == t // (2 * m_)) & (s % (2 * m_) < m_) & (t % (2 * m_) >= m_)
    lv[:, 7] = np.eye(P)
    oh = np.zeros((33, STRIPW), np.float32)
    for w in range(SLCW):
        d = 1023 - w
        oh[bucket(d) if d >= 0 else 32, w] = 1
    for w in range(WINW):
        d = 639 - w
        oh[bucket(d) if 0 <= d < WIN else 32, SLCW + w] = 1
    return fl, lv.reshape(P, 8 * P), oh, np.full((1, H), MASKED, np.float32)


shape_constants()
CW = sum(w for _, w in CONST.values())


class Events:

    def __init__(self, nc, ctx, known):
        self.nc, self.ctx, self.known = nc, ctx, known
        self.sems, self.count, self.at = {}, {}, {}

    def sem(self, name):
        if name not in self.sems:
            self.sems[name] = self.ctx.enter_context(self.nc.semaphore(name))
            self.count[name] = 0
        return self.sems[name]

    def add(self, key, n, events):
        s = self.sem(key)
        self.count[key] += n
        for x in events:
            self.at[x] = (key, self.count[key])
        return s, n


class Engine:

    def __init__(self, ev, e, name):
        self.ev, self.e, self.name, self.jobs = ev, e, name, {}

    def stage(self, name):
        self.key = f"{name}_by_{self.name}"

    def at(self, event):
        key, n = self.ev.known[event] if self.ev.known else ("counting", 1)
        return self.ev.sem(key), n

    def own(self):
        return self.ev.sem(self.last), self.ev.count[self.last]

    def done(self, *events):
        self.last = self.key
        return self.ev.add(self.key, 1, events)

    def moved(self, key, event=None):
        return self.ev.add(key, 16, [event or key])

    def free(self, ring):
        n = self.jobs.get(ring, -1) + 1
        return self.at(("drained", ring, n - 4) if n >= 4 else "consts_in")

    def bank(self, ring):
        n = self.jobs[ring] = self.jobs.get(ring, -1) + 1
        return self.banks[ring][n % 4]

    def filled(self, ring, *events):
        return self.done(("filled", ring, self.jobs[ring]), *events)

    def full(self, ring):
        return self.at(("filled", ring, self.jobs.get(ring, -1) + 1))

    def job(self, ring):
        return self.bank(ring)

    def drained(self, ring, *events):
        return self.done(("drained", ring, self.jobs[ring]), *events)


def build(nc, t_in, t_out, known):
    ctx = ExitStack()
    with ctx:
        return program(nc, ctx, t_in, t_out, known)


def program(nc, ctx, I, O_, known):
    ev = Events(nc, ctx, known)
    arena = ctx.enter_context(nc.sbuf_tensor("arena", [P, 53200], F32))
    banks = {r: [ctx.enter_context(nc.psum_tensor(f"{r}{n}", [P, 512], F32))[:, :] for n in range(4)] for r in ("vec", "act")}
    x_spill = nc.dram_tensor("x_spill", (P, NT * D), F32, kind="Internal").ap()
    strip_rows = nc.dram_tensor("strip_rows", (H, P, STRIPW), F32, kind="Internal").ap()

    class Zone:

        def __init__(self, at):
            self.at = at

        def take(self, n, *shape, dt=F32):
            a = arena[:, self.at:self.at + n]
            self.at += n
            assert self.at <= 53200, self.at
            if dt is not F32:
                a = a.bitcast(dt)
            if len(shape) == 1:
                a = a.rearrange("p (a b) -> p a b", a=shape[0])
            if len(shape) == 2:
                a = a.rearrange("p (a b c) -> p a b c", a=shape[0], b=shape[1])
            return a

    def skew(base, offset, *dims):
        return bass.AP(base.tensor, base.offset + offset, [list(base.ap[0])] + [list(d) for d in dims])

    z = Zone(0)
    consts = z.take(CW)
    C = {n: consts[:, a:a + w] for n, (a, w) in CONST.items()}
    ident, ones = C["ident"], C["ones"]
    ln_g, ln_b = z.take(D), z.take(D)
    eps_col = z.take(1)
    stats, mv, rstd = z.take(NT * 12, NT), z.take(NT * 2, NT), z.take(NT)
    LF, GT, tmp9 = z.take(NT * 4, NT), z.take(NT * 12, NT), z.take(NT * 16, NT)
    QTs = z.take(H * NS, H)
    fkv8, nkvg8 = z.take(512), z.take(400)
    oTh = z.take(4 * NTOK, 4)
    body = z.at
    top = 53200 - (8 * 512 + 32 * P + 2 * P + P + 2 + 240 + 240 + 64 + 64 + 2 * P)
    z = Zone(top)
    OT = z.take(8 * 512, 8)
    w1c, w2 = z.take(32 * P, 32), z.take(2 * P, 2)
    pe_sb, pc = z.take(P), z.take(2)
    gx, gu, KC, VC = z.take(240), z.take(240), z.take(64), z.take(64)
    w2d = z.take(2 * P)

    X1 = Zone(body).take(NT * D, NT)
    tail = 53200 - 2 * 4096 - NC * NTOK
    z = Zone(tail)
    xT = z.take(NC * NTOK, NC)
    W = [z.take(4096, NC) for _ in range(2)]

    z = Zone(body)
    V, b_v, lvmask, reset, bcol = z.take(NT * 512, NT), z.take(512), z.take(1024, 8, dt=I32), z.take(NTOK), z.take(20)
    hk, hb, hs, qe, ke = (z.take(NTOK) for _ in range(5))
    HZ, HQs, HY = ([z.take(NTOK) for _ in range(2)] for _ in range(3))
    lev = [z.take(NTOK) for _ in range(2)]
    AT, ATs, Sall, KeT = z.take(SEQ, 8), z.take(NS), z.take(9 * P, 9), z.take(9 * P, 9)
    S0, VM, ebl = z.take(DB * P, DB), z.take(DB * P, DB), z.take(16)
    assert z.at <= tail, (z.at, tail)

    z = Zone(body)
    QT = z.take(H * SEQ, H)
    fkv, nkvg = z.take(8 * 512, 8), z.take(8 * 400, 8)
    bcolq, b_fkv, b_nkvg = z.take(H), z.take(512), z.take(400)
    assert z.at <= tail
    tab33, tabB = z.take(H), z.take(H * P, H)
    small = z.take(4 * 16, 4)
    KT, kcvc = z.take(4 * SEQ, 4), z.take(NTOK)
    strip_s, strip_w, negc, foxdiag = z.take(1024), z.take(640), z.take(1024), z.take(SEQ, 8)
    zs = Zone(z.at)
    S = [z.take(1024) for _ in range(4)]
    PT = [z.take(1024, 8) for _ in range(2)]
    assert z.at <= top, (z.at, top)
    attention_end = z.at
    onehot, strip_tmp = zs.take(STRIPW), zs.take(STRIPW)

    z = Zone(body)
    oTa = z.take(4 * NTOK, 4)
    Fc = z.take(DB * NP * 512, DB, NP)
    early = Zone(attention_end)
    Nc, Wc, LFc = early.take(DB * NP * 256, DB, NP), early.take(DB * NP * P, DB, NP), early.take(DB * NP * H, DB, NP)
    tabX, pt_sb = early.take(H), early.take(16, dt=I32)
    assert early.at <= top
    LFr, LFn = z.take(NP * P, NP), z.take(P)
    FKT, KVT, T1 = z.take(2 * DB * PAST, 2, DB), z.take(DB * PAST, DB), z.take(DB * PAST, DB)
    KTn = z.take(4 * NS, 4)
    QS, QSall, QN, QNall = z.take(2 * DB * P, 2, DB), z.take(2 * P, 2), z.take(DB * P, DB), z.take(P)
    TX, s_bias, f_bias = z.take(P), z.take(SKC), z.take(SK)
    zl = Zone(CW)
    Ss = [zl.take(SK) for _ in range(4)]
    PTs = [z.take(3 * P, 3) for _ in range(4)]
    KCs, VCs = z.take(120), z.take(DB * 64, DB)
    sg, sm, ss, gsel = z.take(12), z.take(8), z.take(8), z.take(4)
    assert z.at <= attention_end, (z.at, attention_end)

    z = Zone(body + 4 * NTOK)
    X, x1T = z.take(NT * D, NT), z.take(NC * NTOK, NC)
    Wo = Zone(z.at).take(NC * D, NC)
    Wgu = z.take(3 * NC * 512, 3 * NC)
    Wd = Zone(body - 4 * NTOK).take(3 * 2 * D, 6)
    gathered = Zone(z.at - 12288).take(8 * D, 8)
    zr = Zone(z.at)
    rs, rb, rm, r1, r2, slot = (zr.take(NT * NE, NT) for _ in range(6))
    rbias, rg, rgm, rt1, rt2, rw = zr.take(NE), zr.take(NT * 4, NT), zr.take(NT * 4, NT), zr.take(NT), zr.take(NT), zr.take(NC * NE, NC)
    csum, cnt, ntl, cum, rcmp = zr.take(10 * NE, 10), zr.take(NE), zr.take(NE), zr.take(NE), zr.take(TILES * NE, TILES)
    ek, change, flip, par = zr.take(TILES), zr.take(TILES), zr.take(TILES), zr.take(TILES)
    c12, s12 = zr.take(2 * NT, 2), zr.take(2 * NT, 2)
    s_int, ek_int, change_int, par_int = zr.take(2 * NT, 2, dt=I32), zr.take(TILES, dt=I32), zr.take(TILES, dt=I32), zr.take(TILES, dt=I32)
    zx = Zone(zr.at)
    hid, hT = [zx.take(FE) for _ in range(2)], [zx.take(2 * P, 2) for _ in range(2)]
    eb = [zx.take(FE) for _ in range(2)]
    xg = [zx.take(D, NC) for _ in range(2)]
    zy = Zone(body + 4 * NTOK + NT * D)
    xgT = [zy.take(D, NC) for _ in range(2)]
    ysb = [zy.take(D, 2) for _ in range(2)]

    PROJECTION = [[(m, x) for x in part] for m in range(3) for part in (CHUNKS[:1], CHUNKS[1:])]

    w_blocks = [[(0, HI, 512)]]
    for h in range(H):
        w_blocks.append([(0, HQ + h * P, P), (P, HF + h * P, P), (2 * P, HG + h * P, P)])
    w_blocks.append([x for h in range(H) for x in ((h * P, FQ + h * HD, HD), (h * P + HD, NQ + h * HD, HD))])
    w_blocks.append([(0, FK, 512)])
    w_blocks.append([(0, NKV, 396), (396, FF, 4)])
    w_view = I["w_in"][0].rearrange("(c p) n -> p c n", p=P)

    UNITS = [(h, kind, i) for h in range(H) for i in range(8) for kind in ("fox", "slc", "win", "cmp")]

    def unit_keys(kind, i):
        if kind == "cmp":
            return 0, min(8 * i + 7, NCMP), 1
        first = max(0, i - 4) if kind == "win" else 0
        return first * P, (i + 1 - first) * P, i + 1 - first

    def transpose_rings(u, nb):
        return [("act", "vec")[(u + j) % 2] for j in range((nb + 3) // 4)]

    xt_bank, ht_bank = (banks["act"][0], banks["vec"][0]), banks["act"][1]
    gu_bank, dn_bank = (banks["vec"][1], banks["vec"][2]), (banks["act"][2], banks["vec"][3])
    msem = {n: ctx.enter_context(nc.semaphore(f"moe_{n}")) for n in
            ("x0_loaded", "x1_loaded", "w0_loaded", "w1_loaded", "w2_loaded", "w3_loaded", "xt_filled", "xt_by_act", "xt_by_vec", "gu_filled", "exp_done",
             "silu_steps", "hidden_done", "ht_filled", "ht_done", "dn_filled", "y_by_act", "y_by_vec", "y0_stored", "y1_stored")}
    x_rows = nc.dram_tensor("x_rows", (SLOTS, D), F32, kind="Internal").ap()
    y_rows = nc.dram_tensor("y_rows", (SLOTS, D), F32, kind="Internal").ap()

    block = ctx.enter_context(nc.Block())

    def bcast(src, n):
        return bass.AP(src.tensor, src.offset, [[0, P], [1, n]])

    def after(k, n):
        return not isinstance(k, int) or k >= n

    def load_rows(e, k, b):
        e.dma_start(xg[b], x_rows[bass.ds(k * P, P)].rearrange("p (c n) -> p c n", c=NC)).then_inc(msem[f"x{b}_loaded"], 16)

    def expert_of(e, k):
        at = bass.ds(k, 1)
        expert = e.value_load(ek_int[0:1, at], min_val=0, max_val=NE - 1)
        half = e.value_load(par_int[0:1, at], min_val=0, max_val=2)
        fresh = e.value_load(change_int[0:1, at], min_val=0, max_val=1)
        return expert, half, fresh

    def load_expert(e, b, expert, half, fresh):
        one = bass.ds(expert, 1)
        for dst, src in ((Wgu[:, bass.ds(half * NC, NC), 0:FE], I["exp_w1"]), (Wgu[:, bass.ds(half * NC, NC), FE:], I["exp_w3"]),
                         (Wd[:, bass.ds(half * 2, 2), :], I["exp_w2"])):
            e.dma_start(dst, src[0, one].rearrange("e (c p) f -> p (e c) f", p=P), cond=fresh).then_inc(msem[f"w{b}_loaded"], 16)

    @block.sync
    def _(e):
        E = Engine(ev, e, "sync")
        xp, xs = I["x_prompt"][0], I["x_sample"].rearrange("b t d -> (b t) d")
        for t in range(NT):
            e.dma_start(X1[:rows(t), t, :], xp[t * P:(t + 1) * P] if t < 8 else xs).then_inc(*E.moved(f"x{t}_in"))
            if t == 2:
                e.dma_start(ln_g, bcast(I["ln_in_g"], D)).then_inc(*E.moved("ln_in"))
                e.dma_start(ln_b, bcast(I["ln_in_b"], D)).then_inc(*E.moved("ln_in"))
                e.dma_start(consts, I["consts"]).then_inc(*E.moved("consts_in"))

        def load_w(k):
            if k >= 2:
                e.wait_ge(*E.at(("w_in used", k - 2)))
            for a, c, n in w_blocks[k]:
                e.dma_start(W[k % 2][:, :, a:a + n], w_view[:, :, c:c + n]).then_inc(*E.moved(f"w{k % 2}_in", ("w_in", k)))

        load_w(0)
        load_w(1)
        e.wait_ge(*E.at("x transposed pe"))
        e.wait_ge(*E.at("x_spill"))
        e.dma_start(b_v, bcast(I["b_in"][0, HI:HI + 512], 512)).then_inc(*E.moved("hgrn_in"))
        e.dma_start(lvmask, I["level_masks"].rearrange("p (a b) -> p a b", a=8)).then_inc(*E.moved("hgrn_in"))
        b = I["b_in"][0]
        e.dma_start(bcol[:, 0:8], b[HQ:HQ + 1024].rearrange("(h p) -> p h", p=P), allow_slow_non_contiguous=True).then_inc(*E.moved("hgrn_in"))
        e.dma_start(bcol[:, 8:12], b[HG:HG + 512].rearrange("(h p) -> p h", p=P), allow_slow_non_contiguous=True).then_inc(*E.moved("hgrn_in"))
        e.dma_start(bcol[:, 12:13], I["hg_norm_g"][0].rearrange("(p a) -> p a", a=1), allow_slow_non_contiguous=True).then_inc(*E.moved("hgrn_in"))
        for h in range(H):
            load_w(2 + h)
            if h:
                e.wait_ge(*E.at(("hgrn done", h - 1)))
            e.dma_start(S0, I["state_hgrn"][0, :, h].rearrange("b d v -> d b v")).then_inc(*E.moved("s0_in", ("s0", h)))
        load_w(6)
        e.wait_ge(*E.at(("hgrn done", H - 1)))
        e.dma_start(bcolq[0:64, :], b[FQ:FQ + 256].rearrange("(h p) -> p h", p=HD), allow_slow_non_contiguous=True).then_inc(*E.moved("attn_in"))
        e.dma_start(bcolq[64:128, :], b[NQ:NQ + 256].rearrange("(h p) -> p h", p=HD), allow_slow_non_contiguous=True).then_inc(*E.moved("attn_in"))
        e.dma_start(b_fkv, bcast(b[FK:FK + 512], 512)).then_inc(*E.moved("attn_in"))
        e.dma_start(b_nkvg[:, 0:396], bcast(b[NKV:NKV + 396], 396)).then_inc(*E.moved("attn_in"))
        e.dma_start(b_nkvg[:, 396:400], bcast(b[FF:FF + 4], 4)).then_inc(*E.moved("attn_in"))
        e.wait_ge(*E.at(("states stored", H - 1)))
        e.dma_start(tab33[0:32, :], I["rel_bias_table"]).then_inc(*E.moved("tab_in"))
        e.dma_start(tab33[32:33, :], I["masked_row"]).then_inc(*E.moved("tab_in"))
        e.dma_start(onehot[0:33, :], I["bucket_rows"]).then_inc(*E.moved("tab_in"))
        load_w(7)
        for h in range(H):
            e.wait_ge(*E.at(("strip rows", h)))
            e.dma_start(strip_rows[h], strip_tmp).then_inc(*E.moved("strip_out", ("strip stored", h)))
            e.wait_ge(*E.at(("strip stored", h)))

        def load_strips(h):
            at = strip_rows.offset + h * P * STRIPW
            e.dma_start(strip_s, bass.AP(strip_rows.tensor, at + 127, [[STRIPW - 1, P], [1, 1024]])).then_inc(*E.moved("strip_in", ("strips", h)))
            e.dma_start(strip_w, bass.AP(strip_rows.tensor, at + SLCW + 127, [[STRIPW - 1, P], [1, 640]])).then_inc(*E.moved("strip_in", ("strips", h)))

        load_strips(0)
        e.wait_ge(*E.at(("w_in used", 7)))
        e.dma_start(w1c[0:64], I["nsa_cmp_w1"][0, 0].rearrange("l d x -> d l x")).then_inc(*E.moved("cmp_in"))
        e.dma_start(w1c[64:128], I["nsa_cmp_w1"][0, 1].rearrange("l d x -> d l x")).then_inc(*E.moved("cmp_in"))
        e.dma_start(w2[:, :, 0:64], I["nsa_cmp_w2"][0].rearrange("k x d -> x k d")).then_inc(*E.moved("cmp_in"))
        e.dma_start(pe_sb[0:32, :].rearrange("l (k d) -> l k d", k=2), I["nsa_cmp_pe"][0].rearrange("k l d -> l k d")).then_inc(*E.moved("cmp_in"))
        e.dma_start(pt_sb[0:1, :], I["page_table"].rearrange("b j -> (b j)").rearrange("(a n) -> a n", a=1)).then_inc(*E.moved("table_in"))
        for q in range(DS):
            e.dma_start(tabX[32 * q:32 * q + 32, :], I["rel_bias_table"]).then_inc(*E.moved("tabx_in"))
        e.wait_ge(*E.at("table_in"))
        kvp = I["cache_fox_kv"][0].rearrange("n p k h d -> n p (k h d)")
        nkp = I["cache_nsa_kv"][0].rearrange("n p k d -> n p (k d)")
        lfp = I["cache_fox_logf"][0]

        def page_of(n):
            return e.value_load(pt_sb[0:1, n:n + 1], min_val=0, max_val=kvp.shape[0] - 1)

        for n in range(DB * NP):
            page = page_of(n)
            bb, jj = n // NP, n % NP
            e.dma_start(Nc[:, bb, jj, :], nkp[bass.ds(page, 1)].rearrange("a p x -> p (a x)")).then_inc(*E.moved("cache_in"))
            e.dma_start(LFc[:, bb, jj, :], lfp[bass.ds(page, 1)].rearrange("a p x -> p (a x)")).then_inc(*E.moved("cache_in"))
        for bb in range(DB):
            e.dma_start(Wc[:, bb], I["state_nsa_win"][0, bb].rearrange("(j p) k d -> p j (k d)", p=P)).then_inc(*E.moved("cache_in"))
        for h in range(1, H):
            e.wait_ge(*E.at(("strips used", h - 1)))
            load_strips(h)
        e.wait_ge(*E.at("prompt attention done"))
        e.wait_ge(*E.at("kv_out"))
        for n in range(DB * NP):
            bb, jj = n // NP, n % NP
            e.dma_start(Fc[:, bb, jj, :], kvp[bass.ds(page_of(n), 1)].rearrange("a p x -> p (a x)")).then_inc(*E.moved(f"fox{bb // 2}_in"))
        e.wait_ge(*E.at("sample attention done"))
        e.dma_start(Wo, I["w_out"][0].rearrange("(c p) n -> p c n", p=P)).then_inc(*E.moved("wo_in"))
        for t in range(NT):
            e.dma_start(X[:rows(t), t, :], x_spill[:rows(t), t * D:(t + 1) * D]).then_inc(*E.moved(f"xres{t}_in"))
        e.dma_start(ln_g, bcast(I["ln1_g"][0], D)).then_inc(*E.moved("ln1_in"))
        e.dma_start(ln_b, bcast(I["ln1_b"][0], D)).then_inc(*E.moved("ln1_in"))
        e.wait_ge(*E.at("projected out"))
        e.dma_start(rw, I["router_w"].rearrange("(c p) n -> p c n", p=P)).then_inc(*E.moved("router_in"))
        e.dma_start(rbias, bcast(I["router_bias"], NE)).then_inc(*E.moved("router_in"))
        e.wait_ge(*E.at("x1 normalised"))
        e.dma_start(ln_g, bcast(I["ln2_g"][0], D)).then_inc(*E.moved("ln2_in"))
        e.dma_start(ln_b, bcast(I["ln2_b"][0], D)).then_inc(*E.moved("ln2_in"))
        e.wait_ge(*E.at("router done"))
        for k in range(3):
            load_expert(e, k, *expert_of(e, k))
        e.wait_ge(*E.at("rows scattered"))
        for k in range(2):
            load_rows(e, k, k)

        def load_ahead(k, b):
            if not isinstance(k, int) or k < TILES - 1:
                e.wait_ge(msem["xt_filled"], 2 * k)
                load_rows(e, k + 1, 1 - b % 2)
            regs = expert_of(e, k)
            e.wait_ge(msem["dn_filled"], 2 * k - 4)
            load_expert(e, b, *regs)

        for k in range(2, 4):
            e.wait_ge(msem["xt_filled"], 2 * k - 2)
            load_rows(e, k, k % 2)
        load_ahead(3, 3)
        with e.Fori(1, TILES // 4 - 1) as i:
            for b in range(4):
                load_ahead(4 * i + b, b)
        for b in range(4):
            load_ahead(TILES - 4 + b, b)
        yp, ys = O_["y_prompt"][0], O_["y_sample"].rearrange("b t d -> (b t) d")
        for t in range(NT):
            e.wait_ge(*E.at(("y normalised", t)))
            e.dma_start(yp[t * P:(t + 1) * P] if t < 8 else ys, X[:rows(t), t, :]).then_inc(*E.moved("y_out"))
        e.wait_ge(*E.at("y_out"))

    @block.tensor
    def _(e):
        E = Engine(ev, e, "tensor")
        E.banks = banks
        mm = e.matmul
        E.stage("p1")
        e.wait_ge(*E.at("consts_in"))
        for t in range(NT):
            e.wait_ge(*E.at(("x normal", t)))
            r = rows(t)
            for half in range(2):
                ring = "act" if half else "vec"
                e.wait_ge(*E.free(ring))
                bk = E.bank(ring)
                for c in range(4):
                    last = e.transpose(bk[:, c * P:c * P + r], X1[:r, t, (4 * half + c) * P:(4 * half + c + 1) * P], ident[:r, :r])
                last.then_inc(*E.filled(ring, "x transposed pe"))

        def channel_major(k, m, col, ring):
            for a, n in CHUNKS:
                e.wait_ge(*E.free(ring))
                bk = E.bank(ring)
                for c in range(NC):
                    last = mm(bk[:, 0:n], W[k % 2][:, c, col:col + P], xT[:, c, a:a + n], start=c == 0, stop=c == NC - 1)
                last.then_inc(*E.filled(ring, ("w_in used", k)))

        def token_major(k, width, ring):
            for t in range(NT):
                r = rows(t)
                e.wait_ge(*E.free(ring))
                bk = E.bank(ring)
                for c in range(NC):
                    last = mm(bk[:r, 0:width], xT[:, c, t * P:t * P + r], W[k % 2][:, c, 0:width], start=c == 0, stop=c == NC - 1)
                last.then_inc(*E.filled(ring, ("w_in used", k)))

        e.wait_ge(*E.at("xT by vec"))
        e.wait_ge(*E.at("xT by act"))
        e.wait_ge(*E.at(("w_in", 0)))
        token_major(0, 512, "vec")

        def hgrn_project(h, part):
            e.wait_ge(*E.at(("w_in", 1 + h)))
            for m, (a, n) in part:
                e.wait_ge(*E.free("act"))
                bk = E.bank("act")
                for c in range(NC):
                    last = mm(bk[:, 0:n], W[(1 + h) % 2][:, c, m * P:(m + 1) * P], xT[:, c, a:a + n], start=c == 0, stop=c == NC - 1)
                last.then_inc(*E.filled("act", ("w_in used", 1 + h)))

        for part in PROJECTION:
            hgrn_project(0, part)
        for h in range(H):
            E.stage("hgrn")
            hq = HQs[h % 2]
            for l in range(8):
                for x in [("level q", h, l), ("level k", h, l)] if l < 7 else [("k", h), ("projected", h, 0)]:
                    e.wait_ge(*E.at(x))
                for g in range(2):
                    e.wait_ge(*E.free("vec"))
                    bk = E.bank("vec")
                    for c in range(4):
                        ch = slice((4 * g + c) * P, (4 * g + c + 1) * P)
                        a, b = (hk, hq) if l == 7 else (lev[l % 2], lev[l % 2])
                        last = mm(bk[:, c * P:(c + 1) * P], a[:, ch], b[:, ch], start=True, stop=True)
                    last.then_inc(*E.filled("vec", ("level used", h, l)))
                if l >= 5:
                    e.wait_ge(*E.free("vec"))
                    bk = E.bank("vec")
                    mm(bk[:NS, 0:NS], a[:, SEQ:], b[:, SEQ:], start=True, stop=True).then_inc(*E.filled("vec", ("level used", h, l)))
                if h < H - 1 and l < len(PROJECTION):
                    hgrn_project(h + 1, PROJECTION[l])
            e.wait_ge(*E.at(("ke", h)))
            for g in range(2):
                e.wait_ge(*E.free("act"))
                bk = E.bank("act")
                for c in range(4):
                    last = e.transpose(bk[:, c * P:(c + 1) * P], ke[:, (4 * g + c) * P:(4 * g + c + 1) * P], ident)
                last.then_inc(*E.filled("act"))
            e.wait_ge(*E.free("act"))
            bk = E.bank("act")
            e.transpose(bk[:NS, 0:P], ke[:, SEQ:], ident).then_inc(*E.filled("act"))
            e.wait_ge(*E.at(("KeT", h)))
            e.wait_ge(*E.at("V ready"))
            hv = slice(h * P, (h + 1) * P)
            for g in range(2):
                e.wait_ge(*E.free("vec"))
                bk = E.bank("vec")
                for c in range(4):
                    last = mm(bk[:, c * P:(c + 1) * P], KeT[:, 4 * g + c, :], V[:, 4 * g + c, hv], start=True, stop=True)
                last.then_inc(*E.filled("vec"))
            e.wait_ge(*E.at(("VM", h)))
            for g in range(2):
                e.wait_ge(*E.free("vec"))
                bk = E.bank("vec")
                mm(bk, KeT[:NS, 8, :], VM[:NS, 4 * g:4 * g + 4, :], start=True, stop=True).then_inc(*E.filled("vec"))
            e.wait_ge(*E.at(("AT", h)))
            e.wait_ge(*E.at(("states", h)))
            e.wait_ge(*E.at(("qe", h)))
            e.wait_ge(*E.at(("s0", h)))
            for g in range(2):
                e.wait_ge(*E.free("act"))
                bk = E.bank("act")
                for c in range(4):
                    n = 4 * g + c
                    mm(bk[:, c * P:(c + 1) * P], V[:, n, hv], AT[:, n, :], start=True, stop=False)
                    last = mm(bk[:, c * P:(c + 1) * P], Sall[:, n, :], qe[:, n * P:(n + 1) * P], start=False, stop=True)
                last.then_inc(*E.filled("act"))
            e.wait_ge(*E.free("act"))
            bk = E.bank("act")
            mm(bk[:, 0:NS], V[:NS, 8, hv], ATs[:NS, :], start=True, stop=False)
            for b in range(DB):
                last = mm(bk[:, 4 * b:4 * b + 4], S0[:, b, :], qe[:, SEQ + 4 * b:SEQ + 4 * b + 4], start=False, stop=b == DB - 1)
            last.then_inc(*E.filled("act", ("hgrn outputs", h)))
            e.wait_ge(*E.at(("squares", h)))
            for a, n in CHUNKS:
                e.wait_ge(*E.free("act"))
                bk = E.bank("act")
                mm(bk[:, 0:n], ones, lev[0][:, a:a + n], start=True, stop=True).then_inc(*E.filled("act", ("sums", h)))
        E.stage("p2b")
        e.wait_ge(*E.at(("hgrn done", H - 1)))
        e.wait_ge(*E.at(("w_in", 5)))
        for h in range(H):
            channel_major(5, h, h * P, "act")
        e.wait_ge(*E.at("tab_in"))
        e.wait_ge(*E.at("tabB"))

        def bias_rows(h):
            for a in range(0, STRIPW, 512):
                n = min(512, STRIPW - a)
                e.wait_ge(*E.free("act"))
                bk = E.bank("act")
                mm(bk[:, 0:n], tabB[:33, h, :], onehot[:33, a:a + n], start=True, stop=True).then_inc(*E.filled("act"))

        bias_rows(0)
        bias_rows(1)
        e.wait_ge(*E.at(("w_in", 6)))
        token_major(6, 512, "vec")
        bias_rows(2)
        bias_rows(3)
        e.wait_ge(*E.at(("w_in", 7)))
        token_major(7, 400, "vec")

        E.stage("p3")
        e.wait_ge(*E.at("fkv ready"))
        e.wait_ge(*E.at("nkvg ready"))
        for t in range(8):
            e.wait_ge(*E.free("act"))
            bk = E.bank("act")
            for h in range(H):
                last = e.transpose(bk[0:64, h * P:(h + 1) * P], fkv[:, t, h * HD:(h + 1) * HD], ident)
            last.then_inc(*E.filled("act"))
            e.wait_ge(*E.free("vec"))
            bk = E.bank("vec")
            for j, a in enumerate((0, 64, 192)):
                last = e.transpose(bk[:, j * P:(j + 1) * P], nkvg[:, t, a:a + P], ident)
            last.then_inc(*E.filled("vec"))
        e.wait_ge(*E.free("vec"))
        bk = E.bank("vec")
        e.wait_ge(*E.at("cmp_in"))
        e.transpose(bk[:, 0:32], pe_sb[0:32, :], ident[0:32, 0:32]).then_inc(*E.filled("vec"))
        e.wait_ge(*E.at("kcvc ready"))
        for kv in range(2):
            s = slice(64 * kv, 64 * kv + 64)
            e.wait_ge(*E.free("vec"))
            bk = E.bank("vec")
            for l in range(32):
                last = mm(bk[:, 0:65], w1c[s, l, :], skew(kcvc[s, :], l, [16, 65]), start=l == 0, stop=l == 31)
            last.then_inc(*E.filled("vec"))
        e.wait_ge(*E.at("cmp hidden"))
        e.wait_ge(*E.free("vec"))
        bk = E.bank("vec")
        mm(bk[:, 0:NCMP], w2d[:, 0:P], gx[:, 0:NCMP], start=True, stop=True).then_inc(*E.filled("vec"))
        e.wait_ge(*E.free("vec"))
        bk = E.bank("vec")
        mm(bk[:NCMP, 0:64], gx[:, NCMP:2 * NCMP], w2[:, 1, 0:64], start=True, stop=True).then_inc(*E.filled("vec"))

        def decay_rows(h):
            for g in range(2):
                e.wait_ge(*E.free("vec"))
                bk = E.bank("vec")
                for c in range(4):
                    lf = LF[:, 4 * g + c, h:h + 1].to_broadcast([P, P])
                    last = mm(bk[:, c * P:(c + 1) * P], lf, C["negtri"], start=True, stop=True)
                last.then_inc(*E.filled("vec"))

        def scores(u):
            h, kind, i = UNITS[u]
            first, L, nb = unit_keys(kind, i)
            s = slice(0, 64) if kind == "fox" else slice(64, 128)
            q = QT[s, h, i * P:(i + 1) * P]
            for a in range(0, L, 512):
                n = min(512, L - a)
                k = {"fox": KT[0:64, h], "slc": KT[64:128, 0], "win": KT[64:128, 1], "cmp": KC[64:128]}[kind]
                e.wait_ge(*E.free("vec"))
                bk = E.bank("vec")
                mm(bk[:, 0:n], q, k[:, first + a:first + a + n], start=True, stop=True).then_inc(*E.filled("vec"))

        def transposes(u):
            h, kind, i = UNITS[u]
            _, L, nb = unit_keys(kind, i)
            e.wait_ge(*E.at(("probs", u)))
            for j, ring in enumerate(transpose_rings(u, nb)):
                e.wait_ge(*E.free(ring))
                bk = E.bank(ring)
                for c in range(min(4, nb - 4 * j)):
                    n = min(P, L)
                    last = e.transpose(bk[:n, c * P:(c + 1) * P], S[u % 4][:, (4 * j + c) * P:(4 * j + c) * P + n], ident)
                last.then_inc(*E.filled(ring))

        def values(u):
            h, kind, i = UNITS[u]
            first, L, nb = unit_keys(kind, i)
            for x in [("pt", u, j) for j in range((nb + 3) // 4)]:
                e.wait_ge(*E.at(x))
            e.wait_ge(*E.free("vec"))
            bk = E.bank("vec")
            for c in range(nb):
                b = first // P + c
                v = {"fox": fkv[:, b, 256 + h * HD:256 + (h + 1) * HD], "slc": nkvg[:, b, 192:256],
                     "win": nkvg[:, b, 320:384], "cmp": VC[:min(L, P)]}[kind]
                last = mm(bk[:, 0:64], PT[u % 2][:min(P, L), c, :], v, start=c == 0, stop=c == nb - 1)
            last.then_inc(*E.filled("vec", ("unit", u)))

        E.stage("attn")
        e.wait_ge(*E.at("KC ready"))
        e.wait_ge(*E.at("QT ready"))
        e.wait_ge(*E.at("KT by act"))
        e.wait_ge(*E.at("KT by vec"))
        n = len(UNITS)
        for u in range(n + 3):
            if u < n:
                if u % 32 == 0:
                    decay_rows(UNITS[u][0])
                scores(u)
            if 2 <= u < n + 2:
                transposes(u - 2)
            if u >= 3:
                values(u - 3)

        E.stage("p4")
        e.wait_ge(*E.at("prompt attention done"))
        e.wait_ge(*E.at("kv_out"))
        e.wait_ge(*E.at("cache_in"))
        for b in range(DB):
            e.wait_ge(*E.free("vec"))
            bk = E.bank("vec")
            for c in range(2):
                for j in range(NP):
                    last = e.transpose(bk[:, (2 * c + j) * P:(2 * c + j + 1) * P], Nc[:, b, j, 64 * c:64 * c + P], ident)
            last.then_inc(*E.filled("vec"))
            e.wait_ge(*E.free("vec"))
            bk = E.bank("vec")
            for j in range(NP):
                last = e.transpose(bk[:, j * P:(j + 1) * P], Wc[:, b, j, :], ident)
            last.then_inc(*E.filled("vec"))
        for t in range(8):
            e.wait_ge(*E.free("act"))
            bk = E.bank("act")
            for c in range(4):
                last = e.transpose(bk[:, c * P:(c + 1) * P], OT[:, t, c * P:(c + 1) * P], ident)
            last.then_inc(*E.filled("act"))
        for b in range(DB):
            e.wait_ge(*E.at(f"fox{b // 2}_in"))
            e.wait_ge(*E.free("act"))
            bk = E.bank("act")
            for c in range(2):
                for j in range(NP):
                    last = e.transpose(bk[:, (2 * c + j) * P:(2 * c + j + 1) * P], Fc[:, b, j, c * P:(c + 1) * P], ident)
            last.then_inc(*E.filled("act"))
        e.wait_ge(*E.free("vec"))
        bk = E.bank("vec")
        for j, src in enumerate((fkv8[:NS, 0:P], fkv8[:NS, P:2 * P], nkvg8[:NS, 64:192], nkvg8[:NS, 256:384])):
            last = e.transpose(bk[:, j * NS:(j + 1) * NS], src, ident[:NS, :NS])
        last.then_inc(*E.filled("vec"))
        e.wait_ge(*E.at("sample operands"))
        e.wait_ge(*E.at("tabx_in"))
        e.wait_ge(*E.free("vec"))
        bk = E.bank("vec")
        mm(bk[:, 0:P], LFr[:, 0, :], C["negtri"], start=True, stop=True)
        mm(bk[:, P:2 * P], LFr[:, 0, :], C["negones"], start=True, stop=False)
        mm(bk[:, P:2 * P], LFr[:, 1, :], C["negtri"], start=False, stop=True)
        mm(bk[:, 2 * P:SK], LFr[:, 0, :], C["negones"][:, 0:NS], start=True, stop=False)
        mm(bk[:, 2 * P:SK], LFr[:, 1, :], C["negones"][:, 0:NS], start=False, stop=False)
        mm(bk[:, 2 * P:SK], LFn, C["s_negtri"], start=False, stop=True).then_inc(*E.filled("vec"))
        e.wait_ge(*E.free("vec"))
        bk = E.bank("vec")
        mm(bk[:, 0:SKC], TX, C["s_onehot"], start=True, stop=True).then_inc(*E.filled("vec"))
        e.wait_ge(*E.free("vec"))
        bk = E.bank("vec")
        mm(bk[:, 0:12], C["s_sel"][:NS, :], GT[:NS, 8, :], start=True, stop=True).then_inc(*E.filled("vec"))
        e.wait_ge(*E.at("sample keys"))
        for kv in range(2):
            s = slice(64 * kv, 64 * kv + 64)
            e.wait_ge(*E.free("vec"))
            bk = E.bank("vec")
            for l in range(32):
                last = mm(bk[:, 0:DB * NCMPS], w1c[s, l, :], skew(KVT[s, 0, :], l, [PAST, DB], [16, NCMPS]), start=l == 0, stop=l == 31)
            last.then_inc(*E.filled("vec"))
        e.wait_ge(*E.at("sample cmp hidden"))
        e.wait_ge(*E.free("vec"))
        bk = E.bank("vec")
        mm(bk[:, 0:120], w2d[:, 0:P], gx[:, 0:120], start=True, stop=True).then_inc(*E.filled("vec"))
        e.wait_ge(*E.free("vec"))
        bk = E.bank("vec")
        for b in range(DB):
            last = mm(bk[:NCMPS, b * 64:(b + 1) * 64], gx[:, 120 + 15 * b:120 + 15 * b + 15], w2[:, 1, 0:64], start=True, stop=True)
        last.then_inc(*E.filled("vec"))
        e.wait_ge(*E.at("sample keys by act"))
        e.wait_ge(*E.at("sample cmp ready"))
        e.wait_ge(*E.free("vec"))
        bk = E.bank("vec")
        for b in range(DB):
            for c in range(2):
                mm(bk[:, 0:PAST], QS[:, c, b, :], FKT[:, c, b, :], start=b + c == 0, stop=b * 2 + c == 15)
        for c in range(2):
            last = mm(bk[:, PAST:SK], QSall[:, c, :], KTn[:, c, :], start=c == 0, stop=c == 1)
        last.then_inc(*E.filled("vec"))
        for s, slot in ((slice(64, 128), 2), (slice(0, 64), 3)):
            e.wait_ge(*E.free("vec"))
            bk = E.bank("vec")
            for b in range(DB):
                mm(bk[:, 0:PAST], QN[s, b, :], T1[s, b, :], start=b == 0, stop=b == DB - 1)
            mm(bk[:, PAST:SK], QNall[s, :], KTn[s, slot, :], start=True, stop=True).then_inc(*E.filled("vec"))
        e.wait_ge(*E.free("vec"))
        bk = E.bank("vec")
        for b in range(DB):
            last = mm(bk[:, 0:NCMPS], QN[64:128, b, :], KCs[64:128, 15 * b:15 * b + 15], start=b == 0, stop=b == DB - 1)
        last.then_inc(*E.filled("vec"))
        for k in range(4):
            e.wait_ge(*E.at(("sample probs", k)))
            e.wait_ge(*E.free("vec"))
            bk = E.bank("vec")
            if k < 3:
                e.transpose(bk[:, 0:P], Ss[k][:, 0:P], ident)
                e.transpose(bk[:, P:2 * P], Ss[k][:, P:2 * P], ident)
                last = e.transpose(bk[:NS, 2 * P:3 * P], Ss[k][:, 2 * P:SK], ident)
            else:
                last = e.transpose(bk[:NCMPS, 0:P], Ss[k][:, 0:NCMPS], ident)
            last.then_inc(*E.filled("vec"))
        e.wait_ge(*E.at("sample PT"))
        e.wait_ge(*E.free("vec"))
        bk = E.bank("vec")
        for c in range(2):
            o = slice(c * P, (c + 1) * P)
            mm(bk[:, o], fkv8[:NS, 256 + c * P:256 + (c + 1) * P], PTs[0][:NS, 2, :], start=True, stop=False)
            for b in range(DB):
                for j in range(NP):
                    last = mm(bk[:, c * P + 16 * b:c * P + 16 * b + 16], Fc[:, b, j, 256 + c * P:256 + (c + 1) * P],
                              PTs[0][:, j, 16 * b:16 * b + 16], start=False, stop=b * NP + j == 15)
        last.then_inc(*E.filled("vec"))
        e.wait_ge(*E.free("vec"))
        bk = E.bank("vec")
        mm(bk[:64, 0:P], nkvg8[:NS, 192:256], PTs[1][:NS, 2, :], start=True, stop=False)
        mm(bk[:64, 0:P], nkvg8[:NS, 320:384], PTs[2][:NS, 2, :], start=False, stop=False)
        for b in range(DB):
            o = slice(16 * b, 16 * b + 16)
            for j in range(NP):
                mm(bk[:64, o], Nc[:, b, j, 192:256], PTs[1][:, j, o], start=False, stop=False)
                mm(bk[:64, o], Wc[:, b, j, 64:128], PTs[2][:, j, o], start=False, stop=False)
            last = mm(bk[:64, o], VCs[:NCMPS, b, :], PTs[3][:NCMPS, 0, o], start=False, stop=b == DB - 1)
        last.then_inc(*E.filled("vec"))

        E.stage("p5")
        e.wait_ge(*E.at("oTa by act"))
        e.wait_ge(*E.at("sample attention done"))
        e.wait_ge(*E.at(("hgrn done", H - 1)))
        e.wait_ge(*E.at("wo_in"))

        def turn_x1(t):
            e.wait_ge(*E.at(("x1", t)))
            r = rows(t)
            for half in range(2):
                ring = "act" if half else "vec"
                e.wait_ge(*E.free(ring))
                bk = E.bank(ring)
                for c in range(4):
                    last = e.transpose(bk[:, c * P:c * P + r], X[:r, t, (4 * half + c) * P:(4 * half + c + 1) * P], ident[:r, :r])
                last.then_inc(*E.filled(ring, ("x1 read", t)))

        for t in range(NT):
            r = rows(t)
            for half in range(2):
                e.wait_ge(*E.free("vec"))
                bk = E.bank("vec")
                for c in range(NC):
                    src = oTa[:, c, :] if c < 4 else oTh[:, c - 4, :]
                    last = mm(bk[:r], src[:, t * P:t * P + r], Wo[:, c, half * 512:(half + 1) * 512], start=c == 0, stop=c == NC - 1)
                last.then_inc(*E.filled("vec", "projected out"))
            if t in (5, 8):
                for x in GROUPS[t // 3 - 1]:
                    turn_x1(x)
        for t in GROUPS[-1]:
            turn_x1(t)
        e.wait_ge(*E.at("x1T by act"))
        e.wait_ge(*E.at("x1T by vec"))
        e.wait_ge(*E.at("router_in"))
        e.wait_ge(*E.free("vec"))
        bk = E.bank("vec")
        for t in range(NT):
            r = rows(t)
            for c in range(NC):
                last = mm(bk[:r, t * NE:(t + 1) * NE], x1T[:, c, t * P:t * P + r], rw[:, c, :], start=c == 0, stop=c == NC - 1)
        last.then_inc(*E.filled("vec"))
        e.wait_ge(*E.at("choices"))
        e.wait_ge(*E.free("vec"))
        bk = E.bank("vec")
        for t in range(NT):
            o = slice(t * NE, (t + 1) * NE)
            mm(bk[:, o], C["before"], rm[:, t, :], start=True, stop=False)
            mm(bk[:, o], ones, csum[:, t, :], start=False, stop=True)
        mm(bk[:, NT * NE:(NT + 1) * NE], ones, csum[:, NT, :], start=True, stop=True).then_inc(*E.filled("vec"))
        e.wait_ge(*E.at("router done"))

        def turn_rows(k, b):
            e.wait_ge(msem[f"x{b}_loaded"], 8 * k - 8 * b + 16)
            if after(k, 1):
                e.wait_ge(msem["xt_by_act"], k)
                e.wait_ge(msem["xt_by_vec"], k)
            for half in range(2):
                for c in range(4):
                    last = e.transpose(xt_bank[half][:, c * P:(c + 1) * P], xg[b][:, 4 * half + c, :], ident)
                last.then_inc(msem["xt_filled"], 1)

        def turn_hidden(k, b):
            e.wait_ge(msem["hidden_done"], k + 2)
            e.wait_ge(msem["ht_done"], k + 1)
            e.transpose(ht_bank[:, 0:P], hid[b][:, 0:P], ident)
            e.transpose(ht_bank[:, P:2 * P], hid[b][:, P:2 * P], ident).then_inc(msem["ht_filled"], 1)

        def gate_up(k, b, w4):
            half = e.value_load(par_int[0:1, bass.ds(k, 1)], min_val=0, max_val=2)
            e.wait_ge(msem["xt_by_act"], k + 1)
            e.wait_ge(msem["xt_by_vec"], k + 1)
            e.wait_ge(msem[f"w{w4}_loaded"], 12 * k - 12 * w4 + 48)
            if after(k, 1):
                e.wait_ge(msem["hidden_done"], k)
            for c in range(NC):
                w = Wgu[:, bass.ds(half * NC + c, 1), :].rearrange("p a n -> p (a n)")
                last = mm(gu_bank[b], xgT[b][:, c, :], w, start=c == 0, stop=c == NC - 1)
            last.then_inc(msem["gu_filled"], 1)

        def down(k, b):
            half = e.value_load(par_int[0:1, bass.ds(k, 1)], min_val=0, max_val=2)
            e.wait_ge(msem["ht_done"], k + 2)
            for o, done in enumerate(("y_by_act", "y_by_vec")):
                e.wait_ge(msem[done], k + 1)
                for f in range(2):
                    w = Wd[:, bass.ds(half * 2 + f, 1), o * 512:(o + 1) * 512].rearrange("p a n -> p (a n)")
                    last = mm(dn_bank[o], hT[b][:, f, :], w, start=f == 0, stop=f == 1)
                last.then_inc(msem["dn_filled"], 1)

        turn_rows(0, 0)
        turn_rows(1, 1)
        gate_up(0, 0, 0)

        def four_tiles(i, n):
            for b in range(n):
                k = 4 * i + 1 + b
                turn_rows(k + 1, b % 2)
                turn_hidden(k - 1, b % 2)
                gate_up(k, 1 - b % 2, (1 + b) % 4)
                down(k - 1, b % 2)

        four_tiles(0, 4)
        with e.Fori(1, TILES // 4 - 1) as i:
            four_tiles(i, 4)
        four_tiles(TILES // 4 - 1, 2)
        turn_hidden(TILES - 2, 0)
        gate_up(TILES - 1, 1, 3)
        down(TILES - 2, 0)
        turn_hidden(TILES - 1, 1)
        down(TILES - 1, 1)

    @block.scalar
    def _(e):
        E = Engine(ev, e, "scalar")
        E.banks = banks
        act = e.activation

        def rsqrt_of_variance(tag, between=lambda g: None):
            E.stage(tag)
            for g, tiles in enumerate(GROUPS):
                r = rstd[:, tiles[0]:tiles[-1] + 1]
                e.wait_ge(*E.at(("variances", tag, g)))
                act(r, r, ACT.Ln).then_inc(*E.done())
                e.wait_ge(*E.own())
                act(r, r, ACT.Exp, scale=-0.5).then_inc(*E.done(("rstd", tag, g)))
                between(g)

        def transposed(dst, tag, tiles=range(NT)):
            for t in tiles:
                r = rows(t)
                e.wait_ge(*E.full("act"))
                bk = E.job("act")
                e.copy(dst[:, 4:8, t * P:t * P + r], bk.rearrange("p (c n) -> p c n", c=4)[:, :, 0:r]).then_inc(*E.drained("act", tag))

        rsqrt_of_variance("ln0", lambda g: transposed(xT, "xT by act", GROUPS[g - 1] if g else ()))
        transposed(xT, "xT by act", GROUPS[-1])
        e.wait_ge(*E.at("hgrn_in"))
        E.stage("hgrn")

        def projected(h, part):
            for m, (a, n) in part:
                dst = (HQs, HZ, HY)[m][h % 2]
                e.wait_ge(*E.full("act"))
                bk = E.job("act")
                act(dst[:, a:a + n], bk[:, 0:n], ACT.Identity, bias=bcol[:, 4 * m + h:4 * m + h + 1]).then_inc(*E.drained("act", ("projected", h, m)))

        def softplus(h):
            e.wait_ge(*E.own())
            act(ke, HZ[h % 2], ACT.Abs).then_inc(*E.done())
            e.wait_ge(*E.own())
            act(ke, ke, ACT.Exp, scale=-1.0).then_inc(*E.done())
            e.wait_ge(*E.own())
            act(ke, ke, ACT.Ln, bias=1.0).then_inc(*E.done(("softplus", h)))

        for part in PROJECTION:
            projected(0, part)
        softplus(0)
        for h in range(H):
            hz, hy = HZ[h % 2], HY[h % 2]
            oraw = hz
            if h:
                e.wait_ge(*E.at(("hgrn done", h - 1)))
            act(hs, hy, ACT.Exp, scale=-1.0).then_inc(*E.done(("gate exp", h)))
            e.wait_ge(*E.at(("g-z", h)))
            act(hk, hk, ACT.Exp).then_inc(*E.done(("k", h)))
            e.wait_ge(*E.at(("b", h)))
            act(qe, hb, ACT.Exp).then_inc(*E.done(("exp b", h)))
            e.wait_ge(*E.at(("bl-b", h)))
            act(ke, ke, ACT.Exp).then_inc(*E.done(("decay to end", h)))
            for l in range(7):
                n = NTOK if l >= 5 else SEQ
                e.wait_ge(*E.at(("diff", h, l)))
                act(lev[l % 2][:, 0:n], lev[l % 2][:, 0:n], ACT.Exp).then_inc(*E.done(("decay", h, l)))
                if h < H - 1 and l >= 2:
                    projected(h + 1, PROJECTION[l - 2])
            if h < H - 1:
                projected(h + 1, PROJECTION[5])
            for g in range(2):
                e.wait_ge(*E.full("act"))
                bk = E.job("act")
                e.copy(KeT[:, 4 * g:4 * g + 4, :], bk.rearrange("p (c n) -> p c n", c=4)).then_inc(*E.drained("act"))
            e.wait_ge(*E.full("act"))
            bk = E.job("act")
            e.copy(KeT[:NS, 8, :], bk[:NS, 0:P]).then_inc(*E.drained("act", ("KeT", h)))
            if h < H - 1:
                softplus(h + 1)
            for a, n in CHUNKS:
                e.wait_ge(*E.full("act"))
                bk = E.job("act")
                e.copy(oraw[:, a:a + n], bk[:, 0:n]).then_inc(*E.drained("act"))
            e.wait_ge(*E.own())
            act(lev[0], oraw, ACT.Square).then_inc(*E.done(("squares", h)))
            e.wait_ge(*E.at(("eps", 0)))
            for a, n in CHUNKS:
                e.wait_ge(*E.full("act"))
                bk = E.job("act")
                act(lev[1][:, a:a + n], bk[:, 0:n], ACT.Ln, scale=1.0 / P, bias=eps_col[:, 0:1]).then_inc(*E.drained("act"))
            e.wait_ge(*E.own())
            act(lev[1], lev[1], ACT.Exp, scale=-0.5).then_inc(*E.done(("rrms", h)))
        E.stage("p2b")
        e.wait_ge(*E.at("bcolq ready"))
        for h in range(H):
            for a, n in CHUNKS:
                e.wait_ge(*E.full("act"))
                bk = E.job("act")
                dst = QT[:, h, a:a + n] if a < SEQ else QTs[:, h, :]
                act(dst, bk[:, 0:n], ACT.Identity, bias=bcolq[:, h:h + 1], scale=HD ** -0.5).then_inc(*E.drained("act", "QT ready"))
        for h in range(H):
            if h:
                e.wait_ge(*E.at(("strip stored", h - 1)))
            for a in range(0, STRIPW, 512):
                n = min(512, STRIPW - a)
                e.wait_ge(*E.full("act"))
                bk = E.job("act")
                e.copy(strip_tmp[:, a:a + n], bk[:, 0:n]).then_inc(*E.drained("act", ("strip rows", h)))
        e.wait_ge(*E.at("gate logits"))
        act(LF, tmp9[:, :, 0:4], ACT.Abs).then_inc(*E.done())
        act(GT, tmp9[:, :, 4:16], ACT.Exp, scale=-1.0).then_inc(*E.done("gate exps"))
        e.wait_ge(*E.own())
        act(LF, LF, ACT.Exp, scale=-1.0).then_inc(*E.done())
        e.wait_ge(*E.own())
        act(LF, LF, ACT.Ln, bias=1.0).then_inc(*E.done("fox softplus"))
        E.stage("p3")
        for t in range(8):
            e.wait_ge(*E.full("act"))
            bk = E.job("act")
            e.copy(KT[0:64, :, t * P:(t + 1) * P], bk[0:64].rearrange("p (c n) -> p c n", c=4)).then_inc(*E.drained("act", "KT by act"))

        def gelu_exp(n, tag):
            e.wait_ge(*E.at((tag, "inner")))
            act(gu[:, 0:n], gu[:, 0:n], ACT.Exp, scale=-1.5957691216057308).then_inc(*E.done((tag, "exp")))

        gelu_exp(126, "cmp hidden")
        E.stage("attn")
        n = len(UNITS)
        for it in range(n + 3):
            u = it - 2
            if 0 <= u < n:
                h, kind, i = UNITS[u]
                _, L, nb = unit_keys(kind, i)
                for j, ring in enumerate(transpose_rings(u, nb)):
                    if ring == "act":
                        k, w = min(4, nb - 4 * j), min(P, L)
                        e.wait_ge(*E.full("act"))
                        bk = E.job("act")
                        if u >= 2:
                            e.wait_ge(*E.at(("unit", u - 2)))
                        e.copy(PT[u % 2][:w, 4 * j:4 * j + k, :], bk[:w, 0:k * P].rearrange("p (c n) -> p c n", c=k)).then_inc(*E.drained("act", ("pt", u, j)))
            u = it
            if u < n:
                h, kind, i = UNITS[u]
                _, L, _ = unit_keys(kind, i)
                e.wait_ge(*E.at(("scores", u)))
                s = S[u % 4][:, 0:L]
                act(s, s, ACT.Exp, bias=small[:, u % 4, 0:1], accum_out=small[:, u % 4, 1:2]).then_inc(*E.done(("probs", u)))
        E.stage("p4")
        for t in range(8):
            e.wait_ge(*E.full("act"))
            bk = E.job("act")
            e.copy(oTa[:, :, t * P:(t + 1) * P], bk.rearrange("p (c n) -> p c n", c=4)).then_inc(*E.drained("act", "oTa by act"))
        for b in range(DB):
            e.wait_ge(*E.full("act"))
            bk = E.job("act")
            e.copy(FKT[:, :, b, :], bk.rearrange("p (c n) -> p c n", c=2)).then_inc(*E.drained("act", "sample keys by act"))
        gelu_exp(240, "sample cmp hidden")
        for k in range(4):
            e.wait_ge(*E.at(("sample scores", k)))
            s = Ss[k][:, 0:(SK if k < 3 else NCMPS)]
            act(s, s, ACT.Exp, bias=sm[:, k:k + 1], accum_out=ss[:, k:k + 1]).then_inc(*E.done(("sample exp", k)))
        rsqrt_of_variance("ln1", lambda g: transposed(x1T, "x1T by act", GROUPS[g - 1] if g else ()))
        transposed(x1T, "x1T by act", GROUPS[-1])
        e.wait_ge(*E.at("router logits"))
        act(rs, rs, ACT.Exp, scale=-1.0).then_inc(*E.done("router exp"))

        def rows_turned(k, b):
            e.wait_ge(msem["xt_filled"], 2 * k + 1)
            if after(k, 2):
                e.wait_ge(msem["gu_filled"], k - 1)
            e.copy(xgT[b][:, 0:4, :], xt_bank[0].rearrange("p (c n) -> p c n", c=4)).then_inc(msem["xt_by_act"], 1)

        def gate_exp(k, b):
            e.wait_ge(msem["gu_filled"], k + 1)
            if after(k, 1):
                e.wait_ge(msem["hidden_done"], k)
            act(eb[b], gu_bank[b][:, 0:FE], ACT.Exp, scale=-1.0).then_inc(msem["exp_done"], 1)

        def hidden_turned(k, b):
            e.wait_ge(msem["ht_filled"], k + 1)
            e.copy(hT[b], ht_bank[:, 0:2 * P].rearrange("p (c n) -> p c n", c=2)).then_inc(msem["ht_done"], 1)

        def output(k, b):
            e.wait_ge(msem["dn_filled"], 2 * k + 1)
            if after(k, 2):
                e.wait_ge(msem[f"y{b}_stored"], 8 * k - 8 * b)
            e.copy(ysb[b][:, 0, :], dn_bank[0]).then_inc(msem["y_by_act"], 1)

        e.wait_ge(*E.at("router done"))
        rows_turned(0, 0)
        rows_turned(1, 1)
        gate_exp(0, 0)
        def two_tiles(i):
            for b in range(2):
                k = 2 * i + 1 + b
                rows_turned(k + 1, b)
                hidden_turned(k - 1, b)
                gate_exp(k, 1 - b)
                output(k - 1, b)

        two_tiles(0)
        with e.Fori(1, TILES // 2 - 1) as i:
            two_tiles(i)
        hidden_turned(TILES - 2, 0)
        gate_exp(TILES - 1, 1)
        output(TILES - 2, 0)
        hidden_turned(TILES - 1, 1)
        output(TILES - 1, 1)
        rsqrt_of_variance("ln2")

    @block.vector
    def _(e):
        E = Engine(ev, e, "vector")
        E.banks = banks
        tt, ts, stt, cp = e.tensor_tensor, e.tensor_scalar, e.scalar_tensor_tensor, e.tensor_copy

        def layer_norm(Xt, tag, loaded, name, between=lambda g: None):
            e.memset(mv, 1.0).then_inc(*E.done())

            def last_steps(g):
                e.wait_ge(*E.own())
                e.wait_ge(*E.at(("rstd", tag, g)))
                for t in GROUPS[g]:
                    r = rows(t)
                    stt(Xt[:r, t, :], Xt[:r, t, :], rstd[:r, t:t + 1], ln_b[:r], ALU.mult, ALU.add).then_inc(*E.done((name, t)))

            for g, tiles in enumerate(GROUPS):
                for t in tiles:
                    r = rows(t)
                    loaded(t)
                    for half in range(2):
                        e.bn_stats(stats[:r, t, 6 * half:6 * half + 6], Xt[:r, t, 512 * half:512 * half + 512]).then_inc(*E.done())
                    if g and t == tiles[0]:
                        last_steps(g - 1)
                e.wait_ge(*E.own())
                for t in tiles:
                    r = rows(t)
                    e.bn_aggr(mv[:r, t, :], stats[:r, t, :]).then_inc(*E.done())
                e.wait_ge(*E.own())
                ts(rstd[:, tiles[0]:tiles[-1] + 1], mv[:, tiles[0]:tiles[-1] + 1, 1], EPS, None, ALU.add).then_inc(*E.done(("variances", tag, g)))
                if g == 0:
                    e.wait_ge(*E.at(f"{tag}_in" if tag != "ln0" else "ln_in"))
                for t in tiles:
                    r = rows(t)
                    stt(Xt[:r, t, :], Xt[:r, t, :], mv[:r, t, 0:1], ln_g[:r], ALU.subtract, ALU.mult).then_inc(*E.done())
                between(g)
            last_steps(len(GROUPS) - 1)

        def transposed(dst, tag, tiles=range(NT)):
            for t in tiles:
                r = rows(t)
                e.wait_ge(*E.full("vec"))
                bk = E.job("vec")
                cp(dst[:, 0:4, t * P:t * P + r], bk.rearrange("p (c n) -> p c n", c=4)[:, :, 0:r]).then_inc(*E.drained("vec", tag))

        E.stage("ln0")
        e.memset(eps_col, EPS).then_inc(*E.done(("eps", 0)))
        layer_norm(X1, "ln0", lambda t: e.wait_ge(*E.at(f"x{t}_in")), "x normal",
                   lambda g: transposed(xT, "xT by vec", GROUPS[g - 1] if g else ()))
        transposed(xT, "xT by vec", GROUPS[-1])
        E.stage("p2")
        e.wait_ge(*E.at("x_spill"))
        e.wait_ge(*E.at("hgrn_in"))
        e.wait_ge(*E.at("x transposed pe"))
        e.memset(reset, 1.0).then_inc(*E.done())
        e.wait_ge(*E.own())
        e.memset(skew(reset, 0, [P, 8]), 0.0).then_inc(*E.done())
        e.memset(skew(reset, SEQ, [DS, DB]), 0.0).then_inc(*E.done())
        for t in range(NT):
            r = rows(t)
            e.wait_ge(*E.full("vec"))
            bk = E.job("vec")
            tt(V[:r, t, :], bk[:r], b_v[:r], ALU.add).then_inc(*E.drained("vec", "V ready"))

        e.wait_ge(*E.own())
        E.stage("hgrn")
        for h in range(H):
            hz, hq, hy = HZ[h % 2], HQs[h % 2], HY[h % 2]
            oraw = hz
            e.wait_ge(*E.own())
            e.wait_ge(*E.at(("softplus", h)))
            e.wait_ge(*E.at(("projected", h, 1)))
            stt(lev[0], hz, 0.0, ke, ALU.min, ALU.subtract).then_inc(*E.done())
            e.wait_ge(*E.own())
            tt(hk, lev[0], hz, ALU.subtract).then_inc(*E.done(("g-z", h)))
            e.tensor_tensor_scan(hb, reset, lev[0], 0.0, ALU.mult, ALU.add).then_inc(*E.done(("b", h)))
            e.memset(AT, 0.0).then_inc(*E.done())
            e.memset(ATs, 0.0).then_inc(*E.done())
            e.memset(Sall[:, 0, :], 0.0).then_inc(*E.done())
            e.wait_ge(*E.own())
            for n, c, a in ((P, 8, 0), (DS, DB, SEQ)):
                ends = skew(hb, a + n - 1, [n, c], [0, n])
                o = (a, a + n * c)
                v = [x[:, o[0]:o[1]].rearrange("p (c n) -> p c n", n=n) for x in (ke, hb)]
                tt(v[0], ends, v[1], ALU.subtract).then_inc(*E.done(("bl-b", h)))
            e.wait_ge(*E.at(("exp b", h)))
            cp(ebl[:, 0:8], skew(qe, P - 1, [P, 8])).then_inc(*E.done())
            cp(ebl[:, 8:16], skew(qe, SEQ + DS - 1, [DS, DB])).then_inc(*E.done(("ebl", h)))

            def views(x, l):
                n = NTOK if l >= 5 else SEQ
                return x[:, 0:n].rearrange("p (n two m) -> p n two m", two=2, m=LEVELS[l])

            def refs(l):
                m, n = LEVELS[l], (NTOK if l >= 5 else SEQ)
                return skew(hb, m - 1, [2 * m, n // (2 * m)], [0, m])

            for l in range(10):
                if l < 7:
                    if l >= 2:
                        e.wait_ge(*E.at(("level used", h, l - 2)))
                    lv, b = views(lev[l % 2], l), views(hb, l)
                    tt(lv[:, :, 0, :], refs(l), b[:, :, 0, :], ALU.subtract).then_inc(*E.done())
                    tt(lv[:, :, 1, :], b[:, :, 1, :], refs(l), ALU.subtract).then_inc(*E.done(("diff", h, l)))
                if 1 <= l < 8:
                    e.wait_ge(*E.at(("decay", h, l - 1)))
                    lv, q = views(lev[(l - 1) % 2], l - 1), views(hq, l - 1)
                    tt(lv[:, :, 1, :], lv[:, :, 1, :], q[:, :, 1, :], ALU.mult).then_inc(*E.done(("level q", h, l - 1)))
                if l >= 2:
                    k = l - 2
                    e.wait_ge(*E.own())
                    for g in range(2):
                        e.wait_ge(*E.full("vec"))
                        bk = E.job("vec")
                        mask = lvmask[:, k:k + 1, :].to_broadcast([P, 4, P])
                        e.copy_predicated(AT[:, 4 * g:4 * g + 4, :], mask, bk.rearrange("p (c n) -> p c n", c=4)).then_inc(*E.drained("vec", ("AT", h)))
                    if k >= 5:
                        e.wait_ge(*E.full("vec"))
                        bk = E.job("vec")
                        e.copy_predicated(ATs[:NS, :], lvmask[:NS, k, 0:NS], bk[:NS, 0:NS]).then_inc(*E.drained("vec", ("AT", h)))
            if h:
                e.wait_ge(*E.at(("states stored", h - 1)))
            vb = V[:NS, 8, h * P:(h + 1) * P].unsqueeze(1).to_broadcast([NS, DB, P])
            tt(VM[:NS], vb, C["s_batch"][:NS].unsqueeze(2).to_broadcast([NS, DB, P]), ALU.mult).then_inc(*E.done(("VM", h)))
            for g in range(2):
                e.wait_ge(*E.full("vec"))
                bk = E.job("vec")
                for c in range(4):
                    n = 4 * g + c
                    e.wait_ge(*E.own())
                    i = stt(Sall[:, n + 1, :], Sall[:, n, :], ebl[:, n:n + 1], bk[:, c * P:(c + 1) * P], ALU.mult, ALU.add)
                    i.then_inc(*(E.done() if c < 3 else E.drained("vec", ("states", h))))
            e.wait_ge(*E.at(("s0", h)))
            for g in range(2):
                e.wait_ge(*E.full("vec"))
                bk = E.job("vec")
                if g == 0:
                    e.wait_ge(*E.at(("filled", "vec", E.jobs["vec"] + 1)))
                for c in range(4):
                    b = 4 * g + c
                    i = stt(VM[:, b, :], S0[:, b, :], ebl[:, 8 + b:9 + b], bk[:, c * P:(c + 1) * P], ALU.mult, ALU.add)
                    i.then_inc(*(E.done() if c < 3 else E.drained("vec", ("new states", h))))
            e.wait_ge(*E.at(("gate exp", h)))
            ts(hs, hs, 1.0, None, ALU.add).then_inc(*E.done())
            e.wait_ge(*E.own())
            e.reciprocal(hs, hs).then_inc(*E.done())
            e.wait_ge(*E.own())
            tt(hy, hy, hs, ALU.mult).then_inc(*E.done())
            e.wait_ge(*E.at(("rrms", h)))
            e.wait_ge(*E.at(("hgrn outputs", h)))
            stt(oraw, oraw, bcol[:, 12:13], lev[1], ALU.mult, ALU.mult).then_inc(*E.done())
            e.wait_ge(*E.own())
            tt(oTh[:, h, :], oraw, hy, ALU.mult).then_inc(*E.done(("hgrn done", h)))

        E.stage("p2b")
        e.wait_ge(*E.at("attn_in"))
        e.wait_ge(*E.at(("states stored", H - 1)))
        e.wait_ge(*E.at(("hgrn done", H - 1)))
        ts(bcolq, bcolq, HD ** -0.5, None, ALU.mult).then_inc(*E.done("bcolq ready"))
        e.wait_ge(*E.at("tab_in"))
        cp(tabB[:33], tab33[:33].unsqueeze(2).to_broadcast([33, H, P])).then_inc(*E.done("tabB"))
        for t in range(NT):
            r = rows(t)
            e.wait_ge(*E.full("vec"))
            bk = E.job("vec")
            dst = fkv[:, t, :] if t < 8 else fkv8[:NS]
            tt(dst, bk[:r], b_fkv[:r], ALU.add).then_inc(*E.drained("vec", ("fkv", t), "fkv ready"))
        e.memset(tmp9, 0.0).then_inc(*E.done())
        for t in range(NT):
            r = rows(t)
            e.wait_ge(*E.full("vec"))
            bk = E.job("vec")
            dst = nkvg[:, t, :] if t < 8 else nkvg8[:NS]
            tt(dst, bk[:r, 0:400], b_nkvg[:r], ALU.add).then_inc(*E.drained("vec", ("nkvg", t), "nkvg ready"))
        e.wait_ge(*E.own())
        for src, dst in ((nkvg, tmp9[:, 0:8, :]), (nkvg8[:NS].rearrange("p (a n) -> p a n", a=1), tmp9[:NS, 8:9, :])):
            cp(dst[:, :, 0:4], src[:, :, 396:400]).then_inc(*E.done())
            cp(dst[:, :, 4:16], src[:, :, 384:396]).then_inc(*E.done("gate logits"))
        e.wait_ge(*E.own())
        e.wait_ge(*E.at("fox softplus"))
        e.wait_ge(*E.at("gate exps"))
        stt(LF, tmp9[:, :, 0:4], 0.0, LF, ALU.min, ALU.subtract).then_inc(*E.done("LF ready"))
        ts(GT, GT, 1.0, None, ALU.add).then_inc(*E.done())
        e.wait_ge(*E.own())
        e.reciprocal(GT, GT).then_inc(*E.done())

        E.stage("p3")
        for t in range(8):
            e.wait_ge(*E.full("vec"))
            bk = E.job("vec")
            cp(kcvc[:, t * P:(t + 1) * P], bk[:, 0:P]).then_inc(*E.done())
            cp(KT[64:128, 0:2, t * P:(t + 1) * P], bk[64:128, P:3 * P].rearrange("p (c n) -> p c n", c=2)).then_inc(*E.drained("vec", "KT by vec"))
        e.wait_ge(*E.full("vec"))
        bk = E.job("vec")
        cp(kcvc[:, SEQ:], bk[:, 0:32]).then_inc(*E.drained("vec", "kcvc ready"))

        def gelu(n, tag):
            x, u = gx[:, 0:n], gu[:, 0:n]
            e.wait_ge(*E.own())
            tt(u, x, x, ALU.mult).then_inc(*E.done())
            e.wait_ge(*E.own())
            ts(u, u, 0.044715, 1.0, ALU.mult, ALU.add).then_inc(*E.done())
            e.wait_ge(*E.own())
            tt(u, u, x, ALU.mult).then_inc(*E.done((tag, "inner")))
            e.wait_ge(*E.at((tag, "exp")))
            ts(u, u, 1.0, None, ALU.add).then_inc(*E.done())
            e.wait_ge(*E.own())
            e.reciprocal(u, u).then_inc(*E.done())
            e.wait_ge(*E.own())
            tt(x, x, u, ALU.mult).then_inc(*E.done(tag))

        for kv in range(2):
            e.wait_ge(*E.full("vec"))
            bk = E.job("vec")
            cp(pc[:, kv:kv + 1], bk[:, 64:65]).then_inc(*E.done())
            e.wait_ge(*E.own())
            ts(gx[:, NCMP * kv:NCMP * (kv + 1)], bk[:, 0:NCMP], pc[:, kv:kv + 1], None, ALU.add).then_inc(*E.drained("vec"))
        for k in range(2):
            cp(w2d[:, 64 * k:64 * k + 64], w2[:, 0, 0:64]).then_inc(*E.done())
        gelu(2 * NCMP, "cmp hidden")
        e.wait_ge(*E.full("vec"))
        bk = E.job("vec")
        cp(KC[64:128, 0:NCMP], bk[64:128, 0:NCMP]).then_inc(*E.drained("vec"))
        e.wait_ge(*E.full("vec"))
        bk = E.job("vec")
        cp(VC[:NCMP, :], bk[:NCMP, 0:64]).then_inc(*E.drained("vec", "KC ready"))

        E.stage("attn")

        def decay_rows(h):
            e.wait_ge(*E.own())
            for g in range(2):
                e.wait_ge(*E.full("vec"))
                bk = E.job("vec")
                for c in range(4):
                    n = 4 * g + c
                    e.wait_ge(*E.own())
                    carry = negc[:, n * P - 1:n * P] if n else 0.0
                    i = ts(negc[:, n * P:(n + 1) * P], bk[:, c * P:(c + 1) * P], carry, None, ALU.add)
                    i.then_inc(*(E.done() if c < 3 else E.drained("vec", ("negc", h))))

        def scores(u):
            h, kind, i = UNITS[u]
            first, L, nb = unit_keys(kind, i)
            sm_, s = small[:, u % 4], S[u % 4]
            if u >= 4:
                e.wait_ge(*E.at(("unit", u - 4)))
            e.wait_ge(*E.at(("foxdiag", h) if kind == "fox" else ("strips", h)))
            m = -1
            for a in range(0, L, 512):
                n = min(512, L - a)
                if kind == "fox":
                    off = min(n, i * P - a)
                    pieces = [(0, off, negc[:, a:a + off])] if off > 0 else []
                    if a + n == L:
                        pieces.append((n - P, P, foxdiag[:, i, :]))
                elif kind == "cmp":
                    pieces = [(0, n, skew(strip_s, 896 - P * i + 31, [16, n]))]
                else:
                    st, off = (strip_s, 896 - P * i) if kind == "slc" else (strip_w, WIN - P * i)
                    pieces = [(0, n, st[:, off + first + a:off + first + a + n])]
                e.wait_ge(*E.full("vec"))
                bk = E.job("vec")
                for j, (o, w, bias) in enumerate(pieces):
                    if m >= 0:
                        e.wait_ge(*E.own())
                    prior = sm_[:, 4 + m:5 + m] if m >= 0 else FLOOR
                    m += 1
                    ins = e.tensor_tensor_reduce(out=s[:, a + o:a + o + w], in0=bk[:, o:o + w], in1=bias, scale=1.0, scalar=prior,
                                                 op0=ALU.add, op1=ALU.max, accum_out=sm_[:, 4 + m:5 + m])
                    ins.then_inc(*(E.drained("vec") if j == len(pieces) - 1 else E.done()))
            e.wait_ge(*E.own())
            used = [("strips used", h)] if u % 32 == 31 else []
            ts(sm_[:, 0:1], sm_[:, 4 + m:5 + m], -1.0, None, ALU.mult).then_inc(*E.done(("scores", u), *used))

        def finish(u):
            h, kind, i = UNITS[u]
            sm_ = small[:, u % 4]
            e.wait_ge(*E.full("vec"))
            bk = E.job("vec")
            ts(sm_[:, 2:3], sm_[:, 1:2], TINY, None, ALU.max).then_inc(*E.done())
            e.wait_ge(*E.own())
            e.reciprocal(sm_[:, 2:3], sm_[:, 2:3]).then_inc(*E.done())
            e.wait_ge(*E.own())
            if kind == "fox":
                ins = ts(OT[:, i, h * HD:(h + 1) * HD], bk[:, 0:64], sm_[:, 2:3], None, ALU.mult)
            else:
                g = {"cmp": 0, "slc": 1, "win": 2}[kind]
                o = OT[:, i, 256 + h * HD:256 + (h + 1) * HD]
                gate = GT[:, i, 3 * h + g:3 * h + g + 1]
                if kind == "slc":
                    ins = ts(o, bk[:, 0:64], sm_[:, 2:3], gate, ALU.mult, ALU.mult)
                else:
                    tt(sm_[:, 3:4], sm_[:, 2:3], gate, ALU.mult).then_inc(*E.done())
                    e.wait_ge(*E.own())
                    ins = stt(o, bk[:, 0:64], sm_[:, 3:4], o, ALU.mult, ALU.add)
            ins.then_inc(*E.drained("vec", "prompt attention done"))

        n = len(UNITS)
        for it in range(n + 3):
            if it < n:
                if it % 32 == 0:
                    decay_rows(UNITS[it][0])
                scores(it)
            u = it - 2
            if 0 <= u < n:
                h, kind, i = UNITS[u]
                _, L, nb = unit_keys(kind, i)
                for j, ring in enumerate(transpose_rings(u, nb)):
                    if ring == "vec":
                        k, w = min(4, nb - 4 * j), min(P, L)
                        e.wait_ge(*E.full("vec"))
                        bk = E.job("vec")
                        if u >= 2:
                            e.wait_ge(*E.at(("unit", u - 2)))
                        cp(PT[u % 2][:w, 4 * j:4 * j + k, :], bk[:w, 0:k * P].rearrange("p (c n) -> p c n", c=k)).then_inc(*E.drained("vec", ("pt", u, j)))
            if it >= 3:
                finish(it - 3)

        E.stage("p4")
        for b in range(DB):
            e.wait_ge(*E.full("vec"))
            bk = E.job("vec")
            cp(KVT[:, b, :], bk[:, 0:PAST]).then_inc(*E.done())
            cp(T1[64:128, b, :], bk[64:128, PAST:512]).then_inc(*E.drained("vec"))
            e.wait_ge(*E.full("vec"))
            bk = E.job("vec")
            cp(T1[0:64, b, :], bk[0:64, 0:PAST]).then_inc(*E.drained("vec"))
        e.wait_ge(*E.full("vec"))
        bk = E.job("vec")
        cp(KTn, bk[:, 0:P].rearrange("p (c n) -> p c n", c=4)).then_inc(*E.drained("vec", "sample keys"))
        e.wait_ge(*E.at("sample zeros"))
        e.wait_ge(*E.at("tabx_in"))
        for h in range(H):
            s = slice(64 * (h % 2), 64 * (h % 2) + 64)
            q = QTs[:, h, :].rearrange("p (b q) -> p b q", q=DS)
            cp(skew(QSall[s, h // 2, :], 4 * h, [16, DB], [1, DS]), q[0:64]).then_inc(*E.done())
            for s in (slice(0, 64), slice(64, 128)):
                cp(skew(QNall[s, :], 4 * h, [16, DB], [1, DS]), q[64:128]).then_inc(*E.done())
        e.wait_ge(*E.own())
        for c in range(2):
            cp(skew(QS[:, c, 0, :], 0, [P + 16, DB], [1, 16]), QSall[:, c, :].rearrange("p (b r) -> p b r", b=DB)).then_inc(*E.done())
        cp(skew(QN[:, 0, :], 0, [P + 16, DB], [1, 16]), QNall.rearrange("p (b r) -> p b r", b=DB)).then_inc(*E.done())
        bhq = "p (b h q) -> p b h q"
        for j in range(NP):
            cp(LFr[:, j, :].rearrange(bhq, b=DB, h=H), skew(LFc[:, 0, j, :], 0, [NP * H, DB], [1, H], [0, DS])).then_inc(*E.done())
        cp(LFn[:NS].rearrange(bhq, b=DB, h=H), skew(LF[:NS, 8, :], 0, [0, DB], [1, H], [0, DS])).then_inc(*E.done())
        tt(TX.rearrange(bhq, b=DB, h=H), skew(tabX, 0, [0, DB], [1, H], [0, DS]),
                C["s_expand"].rearrange(bhq, b=DB, h=H), ALU.mult).then_inc(*E.done("sample operands"))
        e.wait_ge(*E.full("vec"))
        bk = E.job("vec")
        tt(f_bias, bk[:, 0:SK], C["s_mask"][:, 0:SK], ALU.add).then_inc(*E.drained("vec"))
        e.wait_ge(*E.full("vec"))
        bk = E.job("vec")
        tt(s_bias, bk[:, 0:SKC], C["s_mask"], ALU.add).then_inc(*E.drained("vec"))
        e.wait_ge(*E.full("vec"))
        bk = E.job("vec")
        tt(sg.rearrange("p (g h) -> p g h", g=3), bk[:, 0:12].rearrange("p (h g) -> p g h", g=3),
                            C["s_head"].unsqueeze(1).to_broadcast([P, 3, H]), ALU.mult).then_inc(*E.drained("vec"))
        e.wait_ge(*E.own())
        e.tensor_reduce(gsel[:, 0:3], sg.rearrange("p (g h) -> p g h", g=3), AXX, ALU.add).then_inc(*E.done())
        for kv in range(2):
            e.wait_ge(*E.full("vec"))
            bk = E.job("vec")
            ts(gx[:, 120 * kv:120 * (kv + 1)], bk[:, 0:120], pc[:, kv:kv + 1], None, ALU.add).then_inc(*E.drained("vec"))
        gelu(240, "sample cmp hidden")
        e.wait_ge(*E.full("vec"))
        bk = E.job("vec")
        cp(KCs[64:128, :], bk[64:128, 0:120]).then_inc(*E.drained("vec"))
        e.wait_ge(*E.full("vec"))
        bk = E.job("vec")
        cp(VCs[:NCMPS], bk[:NCMPS].rearrange("p (b d) -> p b d", b=DB)).then_inc(*E.drained("vec", "sample cmp ready"))
        for k in range(4):
            w = SK if k < 3 else NCMPS
            bias = f_bias if k == 0 else s_bias[:, 0:SK] if k < 3 else s_bias[:, SK:SKC]
            e.wait_ge(*E.full("vec"))
            bk = E.job("vec")
            e.tensor_tensor_reduce(out=Ss[k][:, 0:w], in0=bk[:, 0:w], in1=bias, scale=1.0, scalar=FLOOR,
                                                    op0=ALU.add, op1=ALU.max, accum_out=sm[:, 4 + k:5 + k]).then_inc(*E.drained("vec"))
            e.wait_ge(*E.own())
            ts(sm[:, k:k + 1], sm[:, 4 + k:5 + k], -1.0, None, ALU.mult).then_inc(*E.done(("sample scores", k)))
        for k in range(4):
            w = SK if k < 3 else NCMPS
            e.wait_ge(*E.at(("sample exp", k)))
            ts(ss[:, 4 + k:5 + k], ss[:, k:k + 1], TINY, None, ALU.max).then_inc(*E.done())
            e.wait_ge(*E.own())
            e.reciprocal(ss[:, 4 + k:5 + k], ss[:, 4 + k:5 + k]).then_inc(*E.done())
            e.wait_ge(*E.own())
            gate = None if k == 0 else gsel[:, (1, 2, 0)[k - 1]:(1, 2, 0)[k - 1] + 1]
            if k:
                ins = ts(Ss[k][:, 0:w], Ss[k][:, 0:w], ss[:, 4 + k:5 + k], gate, ALU.mult, ALU.mult)
            else:
                ins = ts(Ss[k][:, 0:w], Ss[k][:, 0:w], ss[:, 4 + k:5 + k], None, ALU.mult)
            ins.then_inc(*E.done(("sample probs", k)))
        for k in range(4):
            e.wait_ge(*E.full("vec"))
            bk = E.job("vec")
            if k < 3:
                cp(PTs[k][:, 0:2, :], bk[:, 0:2 * P].rearrange("p (c n) -> p c n", c=2)).then_inc(*E.done())
                cp(PTs[k][:NS, 2, :], bk[:NS, 2 * P:3 * P]).then_inc(*E.drained("vec"))
            else:
                cp(PTs[k][:NCMPS, 0, :], bk[:NCMPS, 0:P]).then_inc(*E.drained("vec", "sample PT"))
        for part in range(2):
            e.wait_ge(*E.full("vec"))
            bk = E.job("vec")
            for h in range(H):
                s = slice(64 * (h % 2), 64 * (h % 2) + 64)
                src = skew(bk[s, :], P * (h // 2) + 4 * h, [16, DB], [1, DS]) if part == 0 else skew(bk[0:64, :], 4 * h, [16, DB], [1, DS])
                dst = oTa[s, 2 * part + h // 2, SEQ:].rearrange("p (b q) -> p b q", q=DS)
                ins = cp(dst, src)
                ins.then_inc(*(E.done() if h < 3 else E.drained("vec", "sample attention done")))

        E.stage("p5")

        def add_residual(t):
            r = rows(t)
            e.wait_ge(*E.at(f"xres{t}_in"))
            for half in range(2):
                x = X[:r, t, half * 512:(half + 1) * 512]
                e.wait_ge(*E.full("vec"))
                bk = E.job("vec")
                stt(x, x, ALPHA, bk[:r], ALU.mult, ALU.add).then_inc(*E.drained("vec"))
            e.wait_ge(*E.own())

        layer_norm(X, "ln1", add_residual, "x1", lambda g: transposed(x1T, "x1T by vec", GROUPS[g - 1] if g else ()))
        transposed(x1T, "x1T by vec", GROUPS[-1])
        E.ev.at["x1 normalised"] = (E.key, E.ev.count[E.key])
        e.memset(rs, 0.0).then_inc(*E.done())
        e.wait_ge(*E.full("vec"))
        bk = E.job("vec")
        e.wait_ge(*E.own())
        cp(rs[:, 0:8, :], bk[:, 0:8 * NE].rearrange("p (t n) -> p t n", n=NE)).then_inc(*E.done())
        cp(rs[:NS, 8, :], bk[:NS, 8 * NE:9 * NE]).then_inc(*E.drained("vec", "router logits"))
        e.wait_ge(*E.at("router exp"))
        b3 = [P, NT, NE]

        def step(ins, *ev_):
            ins.then_inc(*E.done(*ev_))
            e.wait_ge(*E.own())

        step(ts(rs, rs, 1.0, None, ALU.add))
        step(e.reciprocal(rs, rs))
        step(tt(rb, rs, rbias.unsqueeze(1).to_broadcast(b3), ALU.add))
        g4 = rb.rearrange("p t (g j) -> p t g j", g=4)
        first = True
        for a in range(4):
            for b in range(a + 1, 4):
                dst = rg if first else rgm
                step(tt(dst, g4[:, :, :, a], g4[:, :, :, b], ALU.add))
                if not first:
                    step(tt(rg, rg, rgm, ALU.max))
                first = False

        def first_best(scores_, n, best, out):
            step(e.tensor_reduce(best, scores_, AXX, ALU.max))
            step(tt(out, scores_, best.unsqueeze(2).to_broadcast([P, NT, n]), ALU.is_equal))
            step(tt(out, out, C["iota16"][:, 0:n].unsqueeze(1).to_broadcast([P, NT, n]), ALU.mult))
            step(e.tensor_reduce(best, out, AXX, ALU.min))
            step(tt(out, out, best.unsqueeze(2).to_broadcast([P, NT, n]), ALU.is_equal))

        first_best(rg, 4, rt1, rgm)
        step(cp(rm.rearrange("p t (g j) -> p (t g) j", g=4), rgm.rearrange("p t g -> p (t g)").unsqueeze(2).to_broadcast([P, NT * 4, 4])))
        step(tt(rb, rb, rm, ALU.mult))
        step(ts(rm, rm, -1.0, -MASKED, ALU.add, ALU.mult))
        step(tt(rb, rb, rm, ALU.add))
        first_best(rb, NE, rt1, r1)
        step(stt(rb, r1, 2 * MASKED, rb, ALU.mult, ALU.add))
        first_best(rb, NE, rt1, r2)
        valid = C["token"].unsqueeze(2).to_broadcast(b3)
        for r in (r1, r2):
            step(tt(r, r, valid, ALU.mult))
        step(tt(rm, r1, r2, ALU.add))
        step(e.memset(csum[:, 0, :], 0.0))
        for t in range(NT):
            step(tt(csum[:, t + 1, :], csum[:, t, :], rm[:, t, :], ALU.add), "choices")
        for n, r in enumerate((r1, r2)):
            step(tt(rb, r, rs, ALU.mult))
            step(e.tensor_reduce(c12[:, n, :], rb, AXX, ALU.add))
        step(tt(rt1, c12[:, 0, :], c12[:, 1, :], ALU.add))
        step(ts(rt1, rt1, TINY, None, ALU.max))
        step(e.reciprocal(rt1, rt1))
        step(tt(c12, c12, rt1.unsqueeze(1).to_broadcast([P, 2, NT]), ALU.mult))
        e.wait_ge(*E.full("vec"))
        bk = E.job("vec")
        step(cp(cnt, bk[:, NT * NE:(NT + 1) * NE]))
        big = [P, NE, NT]
        cmp9 = rb.rearrange("p t n -> p (t n)").rearrange("p (n t) -> p n t", n=NE)
        step(tt(cmp9, cnt.unsqueeze(2).to_broadcast(big), C["steps"].unsqueeze(1).to_broadcast(big), ALU.is_gt))
        step(e.tensor_reduce(ntl, cmp9, AXX, ALU.add))
        step(e.tensor_tensor_scan(cum, ones[:, 0:NE], ntl, 0.0, ALU.mult, ALU.add))
        step(tt(cnt, cum, ntl, ALU.subtract))
        step(ts(cnt, cnt, float(P), None, ALU.mult))
        tt(slot, bk[:, 0:NT * NE].rearrange("p (t n) -> p t n", n=NE), cnt.unsqueeze(1).to_broadcast(b3), ALU.add).then_inc(*E.drained("vec"))
        e.wait_ge(*E.own())
        for n, r in enumerate((r1, r2)):
            step(tt(rb, r, slot, ALU.mult))
            step(e.tensor_reduce(s12[:, n, :], rb, AXX, ALU.add))
        step(cp(s_int, s12), "row numbers")
        tn = [P, TILES, NE]
        step(tt(rcmp, cum.unsqueeze(1).to_broadcast(tn), C["tiles"].unsqueeze(2).to_broadcast(tn), ALU.is_le))
        step(e.tensor_reduce(ek, rcmp, AXX, ALU.add))
        step(ts(ek, ek, NE - 1.0, None, ALU.min))
        step(e.memset(change, 1.0))
        step(tt(change[:, 1:], ek[:, 1:], ek[:, 0:TILES - 1], ALU.not_equal))
        step(e.tensor_tensor_scan(flip, ones[:, 0:TILES], change, -1.0, ALU.mult, ALU.add))
        step(ts(par[:, 0:NE], C["tiles"][:, 0:NE], 3.0, 3.0, ALU.mult, ALU.add))
        step(tt(rcmp, par[:, 0:NE].unsqueeze(1).to_broadcast(tn), flip.unsqueeze(2).to_broadcast(tn), ALU.is_le))
        step(e.tensor_reduce(par, rcmp, AXX, ALU.add))
        step(stt(par, par, -3.0, flip, ALU.mult, ALU.add))
        step(cp(ek_int, ek))
        step(cp(change_int, change))
        for n in ("hidden_done", "ht_done", "y_by_act", "y_by_vec"):
            e.sem_inc(msem[n], 1)
        step(cp(par_int, par), "router done")

        def rows_turned(k, b):
            e.wait_ge(msem["xt_filled"], 2 * k + 2)
            if after(k, 2):
                e.wait_ge(msem["gu_filled"], k - 1)
            cp(xgT[b][:, 4:8, :], xt_bank[1].rearrange("p (c n) -> p c n", c=4)).then_inc(msem["xt_by_vec"], 1)

        def silu(k, b):
            g, u = gu_bank[b][:, 0:FE], gu_bank[b][:, FE:]
            e.wait_ge(msem["exp_done"], k + 1)
            ts(eb[b], eb[b], 1.0, None, ALU.add).then_inc(msem["silu_steps"], 1)
            e.wait_ge(msem["silu_steps"], 3 * k + 1)
            e.reciprocal(eb[b], eb[b]).then_inc(msem["silu_steps"], 1)
            e.wait_ge(msem["silu_steps"], 3 * k + 2)
            tt(eb[b], eb[b], g, ALU.mult).then_inc(msem["silu_steps"], 1)
            e.wait_ge(msem["silu_steps"], 3 * k + 3)
            tt(hid[b], eb[b], u, ALU.mult).then_inc(msem["hidden_done"], 1)

        def output(k, b):
            e.wait_ge(msem["dn_filled"], 2 * k + 2)
            if after(k, 2):
                e.wait_ge(msem[f"y{b}_stored"], 8 * k - 8 * b)
            cp(ysb[b][:, 1, :], dn_bank[1]).then_inc(msem["y_by_vec"], 1)

        rows_turned(0, 0)
        rows_turned(1, 1)
        silu(0, 0)
        def two_tiles(i):
            for b in range(2):
                k = 2 * i + 1 + b
                rows_turned(k + 1, b)
                silu(k, 1 - b)
                output(k - 1, b)

        two_tiles(0)
        with e.Fori(1, TILES // 2 - 1) as i:
            two_tiles(i)
        silu(TILES - 1, 1)
        output(TILES - 2, 0)
        output(TILES - 1, 1)
        E.stage("combine")
        e.wait_ge(*E.at("residual scaled"))

        def combine(t):
            r = rows(t)
            e.wait_ge(*E.at(("gathered", t)))
            for n in range(2):
                stt(X[:r, t, :], gathered[:r, 2 * (t % 4) + n, :], c12[:r, n, t:t + 1], X[:r, t, :], ALU.mult, ALU.add).then_inc(*E.done(("combined", t)))
                e.wait_ge(*E.own())
        layer_norm(X, "ln2", combine, "y normalised")

    @block.gpsimd
    def _(e):
        E = Engine(ev, e, "gpsimd")
        tt = e.tensor_tensor
        for t in range(NT):
            e.wait_ge(*E.at(("x normal", t)))
            e.dma_start(x_spill[:rows(t), t * D:(t + 1) * D], X1[:rows(t), t, :]).then_inc(*E.moved("x_spill"))
        E.stage("hgrn")
        for h in range(H):
            e.wait_ge(*E.at(("ebl", h)))
            e.wait_ge(*E.at(("projected", h, 0)))
            tt(qe, qe, HQs[h % 2], ALU.mult).then_inc(*E.done(("qe", h)))
            e.wait_ge(*E.at(("decay to end", h)))
            e.wait_ge(*E.at(("k", h)))
            tt(ke, ke, hk, ALU.mult).then_inc(*E.done(("ke", h)))
            for l in range(7):
                n = NTOK if l >= 5 else SEQ
                e.wait_ge(*E.at(("decay", h, l)))
                lv, k = (x[:, 0:n].rearrange("p (n two m) -> p n two m", two=2, m=LEVELS[l])[:, :, 0, :] for x in (lev[l % 2], hk))
                tt(lv, lv, k, ALU.mult).then_inc(*E.done(("level k", h, l)))
            e.wait_ge(*E.at(("states", h)))
            e.dma_start(O_["new_hgrn_p"][0, 0, h], Sall[:, 8, :]).then_inc(*E.moved("hgrn_out", ("states stored", h)))
            e.wait_ge(*E.at(("new states", h)))
            e.dma_start(O_["new_hgrn_s"][0, :, h].rearrange("b d v -> d b v"), VM).then_inc(*E.moved("hgrn_out", ("states stored", h)))
        E.stage("p2b")
        for b in range(DB):
            e.dma_start(O_["new_nsa_win_s"][0, b, 0:PAST - DS].rearrange("t k d -> t (k d)"), I["state_nsa_win"][0, b, DS:].rearrange("t k d -> t (k d)")).then_inc(*E.moved("kv_out"))
        e.wait_ge(*E.at("fkv ready"))
        e.wait_ge(*E.at("nkvg ready"))
        e.wait_ge(*E.at("LF ready"))
        e.dma_start(O_["new_fox_kv_p"][0, 0].rearrange("(t p) k h d -> p t (k h d)", p=P), fkv).then_inc(*E.moved("kv_out"))
        e.dma_start(O_["new_nsa_kv_p"][0, 0].rearrange("(t p) k d -> p t (k d)", p=P), nkvg[:, :, 0:256]).then_inc(*E.moved("kv_out"))
        e.dma_start(O_["new_nsa_win_p"][0, 0].rearrange("(t p) k d -> p t (k d)", p=P), nkvg[:, 4:8, 256:384]).then_inc(*E.moved("kv_out"))
        e.dma_start(O_["new_fox_logf_p"][0, 0].rearrange("(t p) h -> p t h", p=P), LF[:, 0:8, :]).then_inc(*E.moved("kv_out"))
        e.dma_start(O_["new_fox_kv_s"][0].rearrange("b t k h d -> (b t) (k h d)"), fkv8[:NS]).then_inc(*E.moved("kv_out"))
        e.dma_start(O_["new_nsa_kv_s"][0].rearrange("b t k d -> (b t) (k d)"), nkvg8[:NS, 0:256]).then_inc(*E.moved("kv_out"))
        e.dma_start(O_["new_fox_logf_s"][0].rearrange("b t h -> (b t) h"), LF[:NS, 8, :]).then_inc(*E.moved("kv_out"))
        for b in range(DB):
            e.dma_start(O_["new_nsa_win_s"][0, b, PAST - DS:].rearrange("t k d -> t (k d)"), nkvg8[DS * b:DS * b + DS, 256:384]).then_inc(*E.moved("kv_out"))
        E.stage("attn")
        e.memset(ln_g, 0.0).then_inc(*E.done("zeros"))
        e.wait_ge(*E.own())
        e.dma_start(x_rows.rearrange("(k p) n -> p k n", p=P), ln_g.unsqueeze(1).to_broadcast([P, TILES, D])).then_inc(*E.moved("zeros stored"))
        for h in range(H):
            e.wait_ge(*E.at(("negc", h)))
            tt(foxdiag, negc.rearrange("p (t k) -> p t k", t=8), C["diagmask"].unsqueeze(1).to_broadcast([P, 8, P]), ALU.add).then_inc(*E.done(("foxdiag", h)))
        E.stage("p4")
        e.wait_ge(*E.at("prompt attention done"))
        e.wait_ge(*E.at("kv_out"))
        e.wait_ge(*E.at(("states stored", H - 1)))
        e.wait_ge(*E.at("zeros stored"))
        for x in (QS, QSall, QN, LFn):
            e.memset(x, 0.0).then_inc(*E.done("sample zeros"))

        E.stage("scatter")
        e.wait_ge(*E.at("row numbers"))
        e.wait_ge(*E.at("zeros stored"))
        for t in range(NT):
            for n in range(2):
                e.indirect_dma_start(x_rows, bass.IndirectOffsetOnAxis(ap=s_int[:rows(t), n, t:t + 1], axis=0),
                                     X[:rows(t), t, :], None).then_inc(*E.moved("rows scattered"))
        e.wait_ge(*E.at("rows scattered"))
        for t in range(NT):
            r = rows(t)
            e.tensor_scalar(X[:r, t, :], X[:r, t, :], ALPHA, None, ALU.mult).then_inc(*E.done("residual scaled"))

        def store(k, b):
            e.wait_ge(msem["y_by_act"], k + 2)
            e.wait_ge(msem["y_by_vec"], k + 2)
            e.dma_start(y_rows[bass.ds(k * P, P)].rearrange("p (c n) -> p c n", c=2), ysb[b]).then_inc(msem[f"y{b}_stored"], 16)

        with e.Fori(0, TILES // 2) as i:
            for b in range(2):
                store(2 * i + b, b)
        for b in range(2):
            e.wait_ge(msem[f"y{b}_stored"], 16 * (TILES // 2))
        for t in range(NT):
            if t >= 4:
                e.wait_ge(*E.at(("combined", t - 4)))
            for n in range(2):
                e.indirect_dma_start(gathered[:rows(t), 2 * (t % 4) + n, :], None, y_rows,
                                     bass.IndirectOffsetOnAxis(ap=s_int[:rows(t), n, t:t + 1], axis=0)).then_inc(*E.moved(f"gather{t % 4}", ("gathered", t)))

    return dict(ev.at)


OUTPUTS = [("y_prompt", (1, SEQ, D)), ("y_sample", (DB, DS, D)), ("new_fox_kv_p", (1, 1, SEQ, 2, H, HD)),
           ("new_fox_logf_p", (1, 1, SEQ, H)), ("new_nsa_kv_p", (1, 1, SEQ, 4, HD)), ("new_nsa_win_p", (1, 1, WIN, 2, HD)),
           ("new_hgrn_p", (1, 1, H, P, P)), ("new_fox_kv_s", (1, DB, DS, 2, H, HD)), ("new_fox_logf_s", (1, DB, DS, H)),
           ("new_nsa_kv_s", (1, DB, DS, 4, HD)), ("new_nsa_win_s", (1, DB, PAST, 2, HD)), ("new_hgrn_s", (1, DB, H, P, P))]


def kernel(**inputs):
    import concourse.bacc as bacc
    from concourse.bass_utils import run_bass_kernel_spmd

    arrays = {n: np.ascontiguousarray(a) for n, a in inputs.items() if n != "hg_lb_logits"}
    for n, a in zip(("consts", "level_masks", "bucket_rows", "masked_row"), shape_constants()):
        arrays[n] = a
    known = None
    for _ in range(2):
        nc = bacc.Bacc("TRN2", target_bir_lowering=False, num_devices=1)
        t_in = {n: nc.dram_tensor(f"in_{n}", a.shape, mybir.dt.from_np(a.dtype), kind="ExternalInput").ap() for n, a in arrays.items()}
        t_out = {n: nc.dram_tensor(f"out_{n}", s, F32, kind="ExternalOutput").ap() for n, s in OUTPUTS}
        known = build(nc, t_in, t_out, known)
    r = run_bass_kernel_spmd(nc, [{f"in_{n}": a for n, a in arrays.items()}], core_ids=[0])
    return tuple(r.results[0][f"out_{n}"] for n, _ in OUTPUTS)
```
